# Optimizing a Trainium2 kernel written in Bass

```python
import math
import jax, jax.numpy as jnp
from jax import lax
import numpy as np

D_MODEL = 1024
BATCH = 1
SEQ = 256
DEPTH = 1

HEAD_DIM = 64
H_SB = 6
H_MOBA = 5
H_DSA = 5
W_SB = H_SB * HEAD_DIM
W_MOBA = H_MOBA * HEAD_DIM
W_DSA = H_DSA * HEAD_DIM
MOBA_BLOCK = 256
MOBA_TOPK = 3
MOBA_Q_CHUNK = 64
DSA_TOPK_MAX = 256
IDX_HEADS = 8
IDX_DIM = 64
Q_BLOCK = 128
D_FF = -(-8 * D_MODEL // (3 * 256)) * 256
N_BRANCH = 3
D_IN = 3 * W_SB + 3 * W_MOBA + 3 * W_DSA + IDX_HEADS * IDX_DIM + IDX_DIM + IDX_HEADS + N_BRANCH * D_MODEL
RMS_EPS = 1e-6
NEG_BIG = -1e30
ALIBI_HEADS = H_MOBA + H_DSA

kernel_name = "hybrid_sb_moba_dsa_adaln_sandwich"

def _mixer_split_points():
    sizes = [W_SB] * 3 + [W_MOBA] * 3 + [W_DSA] * 3 + [IDX_HEADS * IDX_DIM, IDX_DIM, IDX_HEADS, N_BRANCH * D_MODEL]
    return [int(v) for v in np.cumsum(sizes)[:-1]]

def _alibi_slopes():
    return jnp.asarray(2.0 ** (-8.0 * np.arange(1, ALIBI_HEADS + 1) / ALIBI_HEADS), dtype=jnp.float32)

def rms_norm(x, g):
    xf = x.astype(jnp.float32)
    y = xf * lax.rsqrt(jnp.mean(xf * xf, axis=-1, keepdims=True) + RMS_EPS)
    return (y * g.astype(jnp.float32)).astype(x.dtype)

def stick_breaking_attention(q, k, v):
    B, S, H, dh = q.shape
    scale = dh ** -0.5
    kpos = jnp.arange(S)

    def block(i):
        start = i * Q_BLOCK
        qb = lax.dynamic_slice_in_dim(q, start, Q_BLOCK, axis=1)
        z = jnp.einsum('bqhd,bshd->bhqs', qb, k, preferred_element_type=jnp.float32) * scale
        qpos = start + jnp.arange(Q_BLOCK)
        past = kpos[None, :] < qpos[:, None]
        log_beta = jax.nn.log_sigmoid(z)
        log_one_minus = jnp.where(past, jax.nn.log_sigmoid(-z), 0.0)
        between = lax.cumsum(log_one_minus, axis=3, reverse=True) - log_one_minus
        a = jnp.where(past, jnp.exp(log_beta + between), 0.0)
        return jnp.einsum('bhqs,bshd->bqhd', a.astype(v.dtype), v)

    out = lax.map(block, jnp.arange(S // Q_BLOCK))
    return jnp.moveaxis(out, 0, 1).reshape(B, S, H * dh)

def moba_attention(q, k, v, slopes):
    B, S, H, dh = q.shape
    scale = dh ** -0.5
    nb = -(-S // MOBA_BLOCK)
    pad = nb * MOBA_BLOCK - S
    kp = jnp.pad(k, ((0, 0), (0, pad), (0, 0), (0, 0)))
    vp = jnp.pad(v, ((0, 0), (0, pad), (0, 0), (0, 0)))
    kb = kp.reshape(B, nb, MOBA_BLOCK, H, dh)
    vb = vp.reshape(B, nb, MOBA_BLOCK, H, dh)
    k_mean = jnp.mean(kb.astype(jnp.float32), axis=2)
    kb_h = jnp.moveaxis(kb, 3, 1)
    vb_h = jnp.moveaxis(vb, 3, 1)
    n_sel = min(MOBA_TOPK, nb - 1)
    b_ix = jnp.arange(B)[:, None, None, None]
    h_ix = jnp.arange(H)[None, :, None, None]
    blk_off = jnp.arange(MOBA_BLOCK)

    def chunk(i):
        start = i * MOBA_Q_CHUNK
        own = start // MOBA_BLOCK
        qc = lax.dynamic_slice_in_dim(q, start, MOBA_Q_CHUNK, axis=1)
        qpos = start + jnp.arange(MOBA_Q_CHUNK)
        k_own = lax.dynamic_slice_in_dim(kp, own * MOBA_BLOCK, MOBA_BLOCK, axis=1)
        v_own = lax.dynamic_slice_in_dim(vp, own * MOBA_BLOCK, MOBA_BLOCK, axis=1)
        own_pos = own * MOBA_BLOCK + blk_off
        dist_own = (qpos[:, None] - own_pos[None, :]).astype(jnp.float32)
        s_own = jnp.einsum('bqhd,bkhd->bhqk', qc, k_own, preferred_element_type=jnp.float32) * scale \
            - slopes[None, :, None, None] * dist_own[None, None]
        s_own = jnp.where((own_pos[None, :] <= qpos[:, None])[None, None], s_own, -jnp.inf)
        if n_sel > 0:
            gate = jnp.einsum('bqhd,bnhd->bhqn', qc.astype(jnp.float32), k_mean)
            gate = jnp.where(jnp.arange(nb) < own, gate, NEG_BIG)
            _, sel = lax.top_k(gate, n_sel)
            valid = sel < own
            k_sel = kb_h[b_ix, h_ix, sel]
            v_sel = vb_h[b_ix, h_ix, sel]
            sel_pos = sel[..., None] * MOBA_BLOCK + blk_off
            dist_sel = (qpos[None, None, :, None, None] - sel_pos).astype(jnp.float32)
            s_sel = jnp.einsum('bqhd,bhqnkd->bhqnk', qc, k_sel, preferred_element_type=jnp.float32) * scale \
                - slopes[None, :, None, None, None] * dist_sel
            s_sel = jnp.where(valid[..., None], s_sel, -jnp.inf).reshape(B, H, MOBA_Q_CHUNK, n_sel * MOBA_BLOCK)
            p = jax.nn.softmax(jnp.concatenate([s_sel, s_own], axis=-1), axis=-1).astype(v.dtype)
            p_sel = p[..., :n_sel * MOBA_BLOCK].reshape(B, H, MOBA_Q_CHUNK, n_sel, MOBA_BLOCK)
            p_own = p[..., n_sel * MOBA_BLOCK:]
            return jnp.einsum('bhqnk,bhqnkd->bqhd', p_sel, v_sel) + jnp.einsum('bhqk,bkhd->bqhd', p_own, v_own)
        p_own = jax.nn.softmax(s_own, axis=-1).astype(v.dtype)
        return jnp.einsum('bhqk,bkhd->bqhd', p_own, v_own)

    out = lax.map(chunk, jnp.arange(S // MOBA_Q_CHUNK))
    return jnp.moveaxis(out, 0, 1).reshape(B, S, H * dh)

def dsa_attention(q, k, v, q_idx, k_idx, w_idx, slopes):
    B, S, H, dh = q.shape
    scale = dh ** -0.5
    top = min(DSA_TOPK_MAX, S // 4)
    kpos = jnp.arange(S)
    b_ix = jnp.arange(B)[:, None, None]

    def block(i):
        start = i * Q_BLOCK
        qi = lax.dynamic_slice_in_dim(q_idx, start, Q_BLOCK, axis=1)
        wi = lax.dynamic_slice_in_dim(w_idx, start, Q_BLOCK, axis=1)
        qc = lax.dynamic_slice_in_dim(q, start, Q_BLOCK, axis=1)
        qpos = start + jnp.arange(Q_BLOCK)
        logits = jnp.einsum('bqhd,bsd->bqhs', qi, k_idx, preferred_element_type=jnp.float32)
        score = jnp.einsum('bqhs,bqh->bqs', jax.nn.relu(logits), wi.astype(jnp.float32))
        admissible = kpos[None, :] <= qpos[:, None]
        score = jnp.where(admissible[None], score, NEG_BIG)
        _, idx = lax.top_k(score, top)
        valid = idx <= qpos[None, :, None]
        k_sel = k[b_ix, idx]
        v_sel = v[b_ix, idx]
        dist = (qpos[None, :, None] - idx).astype(jnp.float32)
        s = jnp.einsum('bqhd,bqkhd->bhqk', qc, k_sel, preferred_element_type=jnp.float32) * scale \
            - slopes[None, :, None, None] * dist[:, None]
        s = jnp.where(valid[:, None], s, -jnp.inf)
        p = jax.nn.softmax(s, axis=-1).astype(v.dtype)
        return jnp.einsum('bhqk,bqkhd->bqhd', p, v_sel)

    out = lax.map(block, jnp.arange(S // Q_BLOCK))
    return jnp.moveaxis(out, 0, 1).reshape(B, S, H * dh)

def hybrid_mixer(h, w_in, b_gate, w_proj_sb, w_proj_moba, w_proj_dsa, w_o, slopes):
    B, S, _ = h.shape
    proj = h @ w_in
    (q_sb, k_sb, v_sb, q_mb, k_mb, v_mb, q_ds, k_ds, v_ds,
     q_ix, k_ix, w_ix, gate_logits) = jnp.split(proj, _mixer_split_points(), axis=-1)
    heads = lambda t: t.reshape(B, S, -1, HEAD_DIM)
    o_sb = stick_breaking_attention(heads(q_sb), heads(k_sb), heads(v_sb))
    o_mb = moba_attention(heads(q_mb), heads(k_mb), heads(v_mb), slopes[0::2])
    o_ds = dsa_attention(heads(q_ds), heads(k_ds), heads(v_ds),
                         q_ix.reshape(B, S, IDX_HEADS, IDX_DIM), k_ix, w_ix, slopes[1::2])
    g_sb, g_mb, g_ds = jnp.split(jax.nn.sigmoid(gate_logits + b_gate), N_BRANCH, axis=-1)
    merged = g_sb * (o_sb @ w_proj_sb) + g_mb * (o_mb @ w_proj_moba) + g_ds * (o_ds @ w_proj_dsa)
    return merged @ w_o

def swiglu(h, w_up, w_down):
    gate, up = jnp.split(h @ w_up, 2, axis=-1)
    return (jax.nn.silu(gate) * up) @ w_down

def setup_inputs(seed: int = 0) -> dict:
    key = jax.random.key(seed)
    ks = jax.random.split(key, 16)
    nrm = lambda k, shape, s: jax.random.normal(k, shape, jnp.float32) * s
    L, D = DEPTH, D_MODEL
    return {
        "x": nrm(ks[0], (BATCH, SEQ, D), 1.0),
        "c": nrm(ks[1], (BATCH, D), 1.0),
        "w_ada": nrm(ks[2], (L, D, 6 * D), 0.5 * D ** -0.5),
        "b_ada": nrm(ks[3], (L, 6 * D), 0.01),
        "g_pre_mix": 1.0 + nrm(ks[4], (L, D), 0.02),
        "g_post_mix": 1.0 + nrm(ks[5], (L, D), 0.02),
        "w_in": nrm(ks[6], (L, D, D_IN), D ** -0.5),
        "b_gate": nrm(ks[7], (L, N_BRANCH * D), 0.01),
        "w_proj_sb": nrm(ks[8], (L, W_SB, D), W_SB ** -0.5),
        "w_proj_moba": nrm(ks[9], (L, W_MOBA, D), W_MOBA ** -0.5),
        "w_proj_dsa": nrm(ks[10], (L, W_DSA, D), W_DSA ** -0.5),
        "w_o": nrm(ks[11], (L, D, D), D ** -0.5),
        "g_pre_ffn": 1.0 + nrm(ks[12], (L, D), 0.02),
        "g_post_ffn": 1.0 + nrm(ks[13], (L, D), 0.02),
        "w_up": nrm(ks[14], (L, D, 2 * D_FF), D ** -0.5),
        "w_down": nrm(ks[15], (L, D_FF, D), D_FF ** -0.5),
    }

def reference(x, c, w_ada, b_ada, g_pre_mix, g_post_mix, w_in, b_gate, w_proj_sb, w_proj_moba,
              w_proj_dsa, w_o, g_pre_ffn, g_post_ffn, w_up, w_down):
    slopes = _alibi_slopes()
    c_act = jax.nn.silu(c)
    for l in range(DEPTH):
        mod = c_act @ w_ada[l] + b_ada[l]
        sh1, sc1, g1, sh2, sc2, g2 = [m[:, None, :] for m in jnp.split(mod, 6, axis=-1)]
        h = rms_norm(x, g_pre_mix[l]) * (1.0 + sc1) + sh1
        y = hybrid_mixer(h, w_in[l], b_gate[l], w_proj_sb[l], w_proj_moba[l], w_proj_dsa[l], w_o[l], slopes)
        x = x + g1 * rms_norm(y, g_post_mix[l])
        h = rms_norm(x, g_pre_ffn[l]) * (1.0 + sc2) + sh2
        y = swiglu(h, w_up[l], w_down[l])
        x = x + g2 * rms_norm(y, g_post_ffn[l])
    return x


_drawn_inputs = setup_inputs


def setup_inputs(seed=0):
    import zlib

    import numpy as np

    out = dict(_drawn_inputs(seed))
    spreads = {}
    factors = {'b_ada': 2.875,
     'g_pre_mix': 2.873,
     'g_post_mix': 8.0,
     'b_gate': 21.505,
     'g_pre_ffn': 22.579,
     'g_post_ffn': 33.176}
    for name, (base, spread) in spreads.items():
        noise = np.random.default_rng([zlib.crc32(name.encode()), seed]).standard_normal(out[name].shape)
        drawn = base * np.exp(spread * noise) if base else spread * noise
        out[name] = __import__('jax').numpy.asarray(drawn.astype(out[name].dtype))
    for name, factor in factors.items():
        out[name] = (out[name] * factor).astype(out[name].dtype)
    return out
```

```python
from contextlib import ExitStack

import concourse.bass as bass
from concourse import mybir

F32 = mybir.dt.float32
F32R = mybir.dt.float32r
ALU = mybir.AluOpType
ACT = mybir.ActivationFunctionType
AX_X = mybir.AxisListType.X

P = 128
D = 1024
KC = D // P
S = 256
TT = S // P
HD = 64
H_SB, H_MB, H_DS, H_IX = 6, 5, 5, 8
W_SB, W_MB, W_DS, W_IX = H_SB * HD, H_MB * HD, H_DS * HD, H_IX * HD
FF = 2816
TOPK = min(256, S // 4)
EPS = 1e-6
SCALE = HD ** -0.5
MASKED = -1e30
TAKEN = -3e38
SLOPES = [2.0 ** (-8.0 * (i + 1) / (H_MB + H_DS)) for i in range(H_MB + H_DS)]
CAUSAL = 3 * P
BANK = 512

sizes = [W_SB] * 3 + [W_MB] * 3 + [W_DS] * 3 + [W_IX, HD, H_IX, 3 * D]
offs = [sum(sizes[:i]) for i in range(len(sizes))]
(O_QSB, O_KSB, O_VSB, O_QMB, O_KMB, O_VMB, O_QDS, O_KDS, O_VDS, O_QIX, O_KIX, O_WIX, O_GATE) = offs

T_QIX, T_KIX, T_QMB, T_KMB, T_QSB, T_KSB, T_QDS, T_KDS, T_END = 0, 4, 5, 8, 11, 14, 17, 20, 23
V_MB, V_SB, V_DS = 0, W_MB, W_MB + W_SB

GATE_BLOCKS = 3 * D // BANK
MIX_BLOCKS = [(O_QIX, W_IX), (O_KIX, HD + H_IX), (O_QMB, W_MB), (O_KMB, W_MB), (O_VMB, W_MB),
              (O_QSB, W_SB), (O_KSB, W_SB), (O_VSB, W_SB), (O_QDS, W_DS), (O_KDS, W_DS), (O_VDS, W_DS)]
MIX_BLOCKS += [(O_GATE + BANK * i, BANK) for i in range(GATE_BLOCKS)]
N_MIX = len(MIX_BLOCKS)
PROJ_COLS = 256
N_PROJ = D // PROJ_COLS
B_PROJ = N_MIX
B_WO = B_PROJ + N_PROJ
B_FFN = B_WO + 2
FSTEP = 2 * P
N_FFN = FF // FSTEP


def mix_units():
    units = []
    def features(b, tile, cols, base=0):
        for n, c in enumerate(range(0, cols, P)):
            units.append((b, "features", base + c, min(P, cols - c), tile + n))
    def tokens(b, what, base, cols, dest):
        for t in range(TT):
            units.append((b, what, base, cols, (t, dest)))
    features(0, T_QIX, W_IX)
    features(1, T_KIX, HD)
    tokens(1, "index weights", HD, H_IX, 0)
    features(2, T_QMB, W_MB)
    features(3, T_KMB, W_MB)
    tokens(4, "values", 0, W_MB, V_MB)
    features(5, T_QSB, W_SB)
    features(6, T_KSB, W_SB)
    tokens(7, "values", 0, W_SB, V_SB)
    features(8, T_QDS, W_DS)
    features(9, T_KDS, W_DS)
    tokens(10, "values", 0, W_DS, V_DS)
    for g in range(3 * D // P):
        units.append((11 + g // 4, "gate", g % 4 * P, P, g))
    return units


UNITS = mix_units()
N_UNITS = len(UNITS)
FIRST_GATE = N_UNITS - 3 * D // P
UNITS_DONE = [max(n for n, u in enumerate(UNITS) if u[0] == b) + 1 for b in range(N_MIX)]
PROJ_DONE = [N_UNITS + 2 * (i + 1) for i in range(N_PROJ)]
WO_DONE = [PROJ_DONE[-1] + 3, PROJ_DONE[-1] + 4]
BLOCK_DONE = UNITS_DONE + PROJ_DONE + WO_DONE

O_CHUNK = {"mb": [3, 3, 4, 4, 7], "sb": [0, 0, 1, 1, 2, 2], "ds": [5, 5, 6, 6, 8]}
N_OCH = 9
FULL_OCH = 7
BRANCH_CHUNKS = {"sb": [0, 1, 2], "mb": [3, 4, 7], "ds": [5, 6, 8]}
HEADS = [("mb", h, T_QMB, T_KMB, V_MB) for h in range(H_MB)]
HEADS += [("sb", h, T_QSB, T_KSB, V_SB) for h in range(H_SB)]
HEADS += [("ds", h, T_QDS, T_KDS, V_DS) for h in range(H_DS)]
N_HEADS = len(HEADS)
HEAD_START = 16
HEAD_EVERY = 2
SCORES_AT = {HEAD_START + HEAD_EVERY * n: n for n in range(N_HEADS)}
NORM_AT = {u + 2: n for u, n in SCORES_AT.items()}
SECOND_AT = {u + 3: n for u, n in SCORES_AT.items()}
OUTPUT_AT = {u + 5: n for u, n in SCORES_AT.items()}
LOGITS_AT = {7 + h: h for h in range(H_IX)}
TOPK_ROUNDS = TOPK // 8
ROUND_AT = {16 + r: r for r in range(TOPK_ROUNDS)}
N_SOFT = H_MB + H_DS
SOFT_NO = {n: i for i, n in enumerate(n for n in range(N_HEADS) if HEADS[n][0] != "sb")}
SB_NO = {n: i for i, n in enumerate(n for n in range(N_HEADS) if HEADS[n][0] == "sb")}


def softs_before(n):
    return sum(1 for m in SOFT_NO if m < n)


def sbs_before(n):
    return sum(1 for m in SB_NO if m < n)


def pieces_at():
    plan = {}
    for b in range(N_MIX):
        us = [n for n, u in enumerate(UNITS) if u[0] == b]
        for q in range(4):
            plan.setdefault(us[q * len(us) // 4], []).append((b + 1, q))
    return plan


PIECES_AT = pieces_at()


def raw_uses():
    uses = [("ada", 0, u) for u in range(2)]
    uses += [("block", b, 0) for b in range(B_PROJ + 1)]
    uses += [("ada", 1, u) for u in range(4)]
    uses += [("block", b, 0) for b in range(B_PROJ + 1, B_WO + 1)]
    uses += [("ada", 2, u) for u in range(4)]
    uses += [("block", b, 0) for b in range(B_WO + 1, B_FFN)]
    return uses


RAW = raw_uses()
N_RAW = len(RAW)
LOADS = {b: 1 for b in range(B_FFN)}
LOADS.update({b: 5 for b in range(B_PROJ, B_WO)})


def raw_arrivals():
    count, out = [0, 0], []
    for r, (kind, b, _) in enumerate(RAW):
        count[r % 2] += 16 * (1 if kind == "ada" else LOADS[b])
        out.append(count[r % 2])
    return out, count


RAW_ARRIVED, RAW_COUNT = raw_arrivals()
RAW_OF_BLOCK = {b: r for r, (kind, b, _) in enumerate(RAW) if kind == "block"}
RAW_OF_ADA = {(g, u): r for r, (kind, g, u) in enumerate(RAW) if kind == "ada"}


def decoder_layer(nc, x, c, w_ada, b_ada, g_pre_mix, g_post_mix, w_in, b_gate, w_proj_sb,
                  w_proj_moba, w_proj_dsa, w_o, g_pre_ffn, g_post_ffn, w_up, w_down, out):
    ctx = ExitStack()
    with ctx:
        def sb(name, shape, dt=F32, scope=ctx):
            return scope.enter_context(nc.sbuf_tensor(name, shape, dt))

        def sem(name):
            return ctx.enter_context(nc.semaphore(name))

        raw = [sb(f"raw{i}", [P, KC * BANK]) for i in range(2)]
        whi = [sb(f"whi{i}", [P, KC * BANK], F32R) for i in range(2)]
        wlo = [sb(f"wlo{i}", [P, KC * BANK], F32R) for i in range(2)]
        xt = sb("xt", [P, TT, D])
        hhi = sb("hhi", [P, KC, S], F32R)
        hlo = sb("hlo", [P, KC, S], F32R)
        xn = sb("xn", [P, TT, D])
        h32 = xn[:, :, :].rearrange("p t (k n) -> p (t k) n", n=S)
        ident = sb("ident", [P, P])
        crep = sb("crep", [P, KC, 32])
        ccol = sb("ccol", [P, KC])
        csil = sb("csil", [P, KC])
        col = [sb(f"col{g}", [P, 16]) for g in range(3)]
        stat = sb("stat", [P, 16])
        rinv = sb("rinv", [P, 4])
        brow = sb("brow", [P, BANK])
        grow = sb("grow", [P, BANK])
        mrow = sb("mrow", [P, BANK])
        select = sb("select", [P, 4, P])

        mix = ExitStack()
        v = sb("v", [P, TT, D], scope=mix)
        qk = sb("qk", [P, 3 * KC, S], scope=mix)
        gates = qk
        ohi = sb("ohi", [P, N_OCH, S], F32R, scope=mix)
        olo = sb("olo", [P, N_OCH, S], F32R, scope=mix)
        wix = sb("wix", [P, TT, H_IX], scope=mix)
        dist = sb("dist", [P, CAUSAL], scope=mix)
        dsel = sb("dsel", [P, CAUSAL], scope=mix)
        tri = sb("tri", [P, P], scope=mix)
        neg1 = sb("neg1", [P, P], scope=mix)
        bgr = sb("bgr", [3 * KC, P], scope=mix)
        bgc = sb("bgc", [P, 3 * KC], scope=mix)
        score = sb("score", [P, CAUSAL], scope=mix)
        work = sb("work", [P, CAUSAL], scope=mix)
        top8 = sb("top8", [P, TT, 8], scope=mix)
        bufa = [sb(f"bufa{i}", [P, CAUSAL], scope=mix) for i in range(2)]
        bufp = [sb(f"bufp{i}", [P, CAUSAL], scope=mix) for i in range(2)]
        buft = [sb(f"buft{i}", [P, CAUSAL], scope=mix) for i in range(2)]
        smax = sb("smax", [P, 2, TT], scope=mix)
        ssum = sb("ssum", [P, 2, TT], scope=mix)
        gp = [b[:, 0:S] for b in (bufa[0], bufa[1], bufp[0])]
        mix.close()

        start = ExitStack()
        ada_end = [sb(f"ada_end{i}", [P, KC * BANK], scope=start) for i in range(2)]
        start.close()

        ffn = ExitStack()
        gb = [None] + [sb(f"gb{g}", [P, D], scope=ffn) for g in (1, 2)]
        draw = [sb(f"draw{i}", [P, 2, D], scope=ffn) for i in range(2)]
        dhi = [sb(f"dhi{i}", [P, 2, D], F32R, scope=ffn) for i in range(2)]
        dlo = [sb(f"dlo{i}", [P, 2, D], F32R, scope=ffn) for i in range(2)]
        fsil = [sb(f"fsil{i}", [P, 2, S], scope=ffn) for i in range(2)]
        fhi = [sb(f"fhi{i}", [P, 2, S], F32R, scope=ffn) for i in range(2)]
        flo = [sb(f"flo{i}", [P, 2, S], F32R, scope=ffn) for i in range(2)]
        ffn.close()

        bank = [ctx.enter_context(nc.psum_tensor(f"bank{i}", [P, BANK], F32)) for i in range(8)]
        B_UNIT, B_Z, B_T, B_O = 0, 2, 4, 6

        ada_in = [sem(f"ada_in{i}") for i in range(2)]
        raw_in = [sem(f"raw_in{i}") for i in range(2)]
        down_in = [sem(f"down_in{i}") for i in range(2)]
        pool_step = sem("pool_step")
        x_in, c_in, rows_in, stored = sem("x_in"), sem("c_in"), sem("rows_in"), sem("stored")
        rows_set, consts = sem("rows_set"), sem("consts")
        w_hi, w_lo = sem("w_hi"), sem("w_lo")
        units = sem("units")
        unit_read = sem("unit_read")
        gemv = sem("gemv")
        c_ready = sem("c_ready")
        act_step, dve_step = sem("act_step"), sem("dve_step")
        ss_ready, var_ready, sqrt_ready, xn_ready = sem("ss_ready"), sem("var_ready"), sem("sqrt_ready"), sem("xn_ready")
        x_turned, h_even, h_odd, h_hi, h_lo = sem("x_turned"), sem("h_even"), sem("h_odd"), sem("h_hi"), sem("h_lo")
        m_ready, m_turned, col_ready, m_spread, gb_ready = (sem("m_ready"), sem("m_turned"), sem("col_ready"),
                                                           sem("m_spread"), sem("gb_ready"))
        bg_in, bg_turned, bg_ready = sem("bg_in"), sem("bg_turned"), sem("bg_ready")
        logits, relu_ready, score_added, score_masked, sel_ready = (sem("logits"), sem("relu_ready"),
                                                                   sem("score_added"), sem("score_masked"), sem("sel_ready"))
        z_ready, y_ready, max_ready, exp_ready, p_ready = sem("z_ready"), sem("y_ready"), sem("max_ready"), sem("exp_ready"), sem("p_ready")
        p_turned, pt_ready = sem("p_turned"), sem("pt_ready")
        ln_ready, sp_ready, sp_masked, sums, a_ready, a_masked = (sem("ln_ready"), sem("sp_ready"), sem("sp_masked"),
                                                                 sem("sums"), sem("a_ready"), sem("a_masked"))
        o_ready, o_hi, o_lo = sem("o_ready"), sem("o_hi"), sem("o_lo")
        sig_ready, gated, merged, m_hi, m_lo = sem("sig_ready"), sem("gated"), sem("merged"), sem("m_hi"), sem("m_lo")
        y_scaled, x_new = sem("y_scaled"), sem("x_new")
        up_done, down_done, silu_done, f_ready, f_hi, f_lo = (sem("up_done"), sem("down_done"), sem("silu_done"),
                                                             sem("f_ready"), sem("f_hi"), sem("f_lo"))
        d_hi, d_lo, up_hi, up_lo = sem("d_hi"), sem("d_lo"), sem("up_hi"), sem("up_lo")

        block = ctx.enter_context(nc.Block())

        x_dram = x.rearrange("b (t p) d -> p (b t) d", p=P)
        out_dram = out.rearrange("b (t p) d -> p (b t) d", p=P)
        ada_dram = w_ada.rearrange("l (p k) n -> p (l k) n", k=KC)
        in_dram = w_in.rearrange("l (k p) n -> p (l k) n", p=P)
        up_dram = w_up.rearrange("l (k p) n -> p (l k) n", p=P)
        down_dram = w_down.rearrange("l (k p) n -> p (l k) n", p=P)
        wo_dram = w_o.rearrange("l (k p) n -> p (l k) n", p=P)

        def block_view(buf, b):
            if b < N_MIX:
                n = MIX_BLOCKS[b][1]
                return buf[:, 0:KC * n].rearrange("p (k n) -> p k n", n=n)
            if b < B_WO:
                return buf[:, 0:N_OCH * PROJ_COLS].rearrange("p (k n) -> p k n", n=PROJ_COLS)
            if b < B_FFN:
                return buf[:, :].rearrange("p (k n) -> p k n", n=D)
            return buf[:, :].rearrange("p (k n) -> p k n", n=BANK)

        def block_parts(b):
            if b < N_MIX or b >= B_FFN:
                return [(P, 2 * q, 2 * q + 2) for q in range(4)]
            if b < B_WO:
                return [(P, 0, 3), (P, 3, 5), (P, 5, FULL_OCH), (HD, FULL_OCH, N_OCH)]
            return [(P, q, q + 1) for q in range(4)]

        def hold(b):
            return BLOCK_DONE[b - 2] if b >= 2 else 0

        @block.sync
        def _(sp):
            sp.dma_start(ccol[:, :], c.rearrange("b (p k) -> p (b k)", k=KC)).then_inc(c_in, 16)
            for t in range(TT):
                sp.dma_start(xt[:, t, :], x_dram[:, t, :]).then_inc(x_in, 16)

            def load(r):
                kind, b, u = RAW[r]
                dst, arrived = raw[r % 2], raw_in[r % 2]
                if r >= 2:
                    before, b0, u0 = RAW[r - 2]
                    if before == "ada":
                        sp.wait_ge(gemv, 4 * b0 + u0 + 1)
                    else:
                        sp.wait_ge(w_hi, 4 * (b0 + 1))
                        sp.wait_ge(w_lo, 4 * (b0 + 1))
                if kind == "ada":
                    sp.dma_start(dst[:, :].rearrange("p (k n) -> p k n", k=2),
                                 ada_dram[:, 2 * u:2 * u + 2, 4 * BANK * b:4 * BANK * (b + 1)]).then_inc(arrived, 16)
                elif b < N_MIX:
                    c0, n = MIX_BLOCKS[b]
                    sp.dma_start(block_view(dst, b), in_dram[:, :, c0:c0 + n]).then_inc(arrived, 16)
                elif b < B_WO:
                    c0 = PROJ_COLS * (b - B_PROJ)
                    view = block_view(dst, b)
                    cols = slice(c0, c0 + PROJ_COLS)
                    for w, k0, n, last in ((w_proj_sb, 0, 3, None), (w_proj_moba, 3, 2, 7), (w_proj_dsa, 5, 2, 8)):
                        sp.dma_start(view[:, k0:k0 + n, :],
                                     w[0, 0:n * P, cols].rearrange("(k p) n -> p k n", p=P)).then_inc(arrived, 16)
                        if last is not None:
                            sp.dma_start(view[0:HD, last, :], w[0, n * P:n * P + HD, cols]).then_inc(arrived, 16)
                else:
                    k0 = 4 * (b - B_WO)
                    sp.dma_start(block_view(dst, b), wo_dram[:, k0:k0 + 4, :]).then_inc(arrived, 16)

            def load_rows(g):
                if g == 0:
                    sp.wait_ge(rows_set, 2)
                else:
                    sp.wait_ge(m_ready, g)
                sp.dma_start(brow[0:P:32, :], b_ada[0, 4 * BANK * g:4 * BANK * (g + 1)].rearrange("(j n) -> j n", n=BANK)).then_inc(rows_in, 16)
                for w, j in GAIN_ROWS[g]:
                    sp.dma_start(grow[32 * j:32 * j + 33:32, :], w.rearrange("l (j n) -> (l j) n", j=2)).then_inc(rows_in, 16)

            GAIN_ROWS = [[(g_pre_mix, 2)], [(g_post_mix, 0)], [(g_pre_ffn, 0), (g_post_ffn, 2)]]
            sp.dma_start(bgr[:, :], b_gate.rearrange("l (k p) -> (l k) p", p=P)).then_inc(bg_in, 16)
            load(0)
            load(1)
            for i in range(2):
                sp.dma_start(ada_end[i][:, :].rearrange("p (k n) -> p k n", k=2),
                             ada_dram[:, 4 + 2 * i:6 + 2 * i, 0:4 * BANK]).then_inc(ada_in[i], 16)
            load_rows(0)
            for r in range(2, N_RAW):
                load(r)
                if RAW[r][0] == "ada" and RAW[r][1] > 0 and RAW[r][2] == 1:
                    load_rows(RAW[r][1])

            def load_step(i, slot, first):
                view = block_view(raw[slot], B_FFN).rearrange("p k (a n) -> p k a n", a=2)
                if first and i == 0:
                    sp.wait_ge(gemv, 12)
                elif first:
                    sp.wait_ge(w_hi, 4 * B_FFN)
                    sp.wait_ge(w_lo, 4 * B_FFN)
                else:
                    sp.wait_ge(up_hi, 4 * (i - 1))
                    sp.wait_ge(up_lo, 4 * (i - 1))
                for a in range(2):
                    sp.dma_start(view[:, :, a, :], up_dram[:, :, bass.ds(i * FSTEP + FF * a, FSTEP)]).then_inc(raw_in[slot], 16)
                if first:
                    sp.wait_ge(units, BLOCK_DONE[B_WO - 1])
                    sp.wait_ge(merged, KC)
                else:
                    sp.wait_ge(d_hi, i - 1)
                    sp.wait_ge(d_lo, i - 1)
                sp.dma_start(draw[slot][:, :, :], down_dram[:, bass.ds(2 * i, 2), :]).then_inc(down_in[slot], 16)

            load_step(0, 1, True)
            load_step(1, 0, True)
            load_step(2, 1, False)
            with sp.Fori(3, N_FFN - 1, 2) as i:
                load_step(i, 0, False)
                load_step(i + 1, 1, False)

            for t in range(TT):
                sp.wait_ge(x_new, 2 * TT + 2 * (t + 1))
                sp.dma_start(out_dram[:, t, :], xt[:, t, :]).then_inc(stored, 16)
            sp.wait_ge(stored, 16 * TT)

        @block.gpsimd
        def _(pool):
            pool.memset(brow[:, :], 0.0).then_inc(rows_set, 1)
            pool.memset(grow[:, :], 1.0).then_inc(rows_set, 1)
            pool.memset(ident[:, :], 0.0).then_inc(consts, 1)
            pool.memset(tri[:, :], -1.0).then_inc(consts, 1)
            pool.memset(neg1[:, :], -1.0).then_inc(consts, 1)
            pool.iota(bufa[0][:, 0:P].bitcast(mybir.dt.int32), pattern=[[1, P]], base=0, channel_multiplier=-1).then_inc(consts, 1)
            pool.iota(bufa[0][:, P:CAUSAL].bitcast(mybir.dt.int32), pattern=[[1, 2 * P]], base=-P, channel_multiplier=-1).then_inc(consts, 1)
            pool.wait_ge(consts, 5)
            pool.affine_select(out=ident[:, :], in_=ident[:, :], compare_op=ALU.not_equal, fill=1.0,
                               base=0, pattern=[[-1, P]], channel_multiplier=1).then_inc(consts, 1)
            pool.affine_select(out=tri[:, :], in_=tri[:, :], compare_op=ALU.is_ge, fill=0.0,
                               base=0, pattern=[[-1, P]], channel_multiplier=1).then_inc(consts, 1)
            pool.tensor_copy(dist[:, :], bufa[0][:, :].bitcast(mybir.dt.int32)).then_inc(consts, 1)
            pool.wait_ge(consts, 8)
            for c0 in (0, 2 * P):
                pool.affine_select(out=dist[:, c0:c0 + P], in_=dist[:, c0:c0 + P], compare_op=ALU.is_ge, fill=MASKED,
                                   base=0, pattern=[[-1, P]], channel_multiplier=1).then_inc(consts, 1)

            for u in range(N_UNITS):
                if u == LOGITS_LAST:
                    pool.wait_ge(score_added, TT * H_IX)
                    for c0 in (0, 2 * P):
                        pool.affine_select(out=score[:, c0:c0 + P], in_=score[:, c0:c0 + P], compare_op=ALU.is_ge, fill=MASKED,
                                           base=0, pattern=[[-1, P]], channel_multiplier=1).then_inc(score_masked, 1)
                if u in SECOND_AT and SECOND_AT[u] in SB_NO:
                    i = SB_NO[SECOND_AT[u]]
                    n = SECOND_AT[u]
                    pool.wait_ge(a_ready, i + 1)
                    for c0 in (0, 2 * P):
                        pool.affine_select(out=buft[n % 2][:, c0:c0 + P], in_=buft[n % 2][:, c0:c0 + P], compare_op=ALU.is_gt, fill=0.0,
                                           base=0, pattern=[[1, P]], channel_multiplier=-1).then_inc(a_masked, 1)
                if u in SCORES_AT and SCORES_AT[u] in SB_NO:
                    n = SCORES_AT[u]
                    i = SB_NO[n]
                    pool.wait_ge(sp_ready, i + 1)
                    for c0 in (0, 2 * P):
                        pool.affine_select(out=bufp[n % 2][:, c0:c0 + P], in_=bufp[n % 2][:, c0:c0 + P], compare_op=ALU.is_gt, fill=0.0,
                                           base=0, pattern=[[1, P]], channel_multiplier=-1).then_inc(sp_masked, 1)

            for f in range(KC):
                pool.wait_ge(gated, 3 * (f + 1))
                pool.tensor_tensor(gp[0], gp[0], gp[1], ALU.add).then_inc(pool_step, 1)
                pool.wait_ge(pool_step, f + 1)
                pool.tensor_tensor(h32[:, f, :], gp[0], gp[2], ALU.add).then_inc(merged, 1)

        @block.scalar
        def _(act):
            steps = [0]

            def then(ins):
                steps[0] += 1
                ins.then_inc(act_step, 1)
                act.wait_ge(act_step, steps[0])

            def cut_hi(b, q):
                if q == 0:
                    r = RAW_OF_BLOCK[b]
                    act.wait_ge(raw_in[r % 2], RAW_ARRIVED[r])
                    if b >= 2:
                        act.wait_ge(units, hold(b))
                r = RAW_OF_BLOCK[b]
                p, k0, k1 = block_parts(b)[q]
                act.activation(block_view(whi[b % 2], b)[0:p, k0:k1, :], block_view(raw[r % 2], b)[0:p, k0:k1, :],
                               ACT.Copy).then_inc(w_hi, 1)

            def square_sums(t, sources, at):
                for n, src in enumerate(sources):
                    ins = act.activation(h32_scrap(t, n, src.shape[1]), src, ACT.Square, accum_out=stat[:, at + n:at + n + 1])
                ins.then_inc(ss_ready, 1)

            def h32_scrap(t, n, cols):
                return xn[:, t, n * cols:(n + 1) * cols]

            def root(k):
                act.wait_ge(var_ready, k + 1)
                act.activation(rinv[:, 2:4], rinv[:, 0:2], ACT.Sqrt).then_inc(sqrt_ready, 1)

            def modulate(k):
                base, (shift, gain) = (0, (col[0][:, 0:8], col[0][:, 8:16])) if k == 0 else (4, (col[1][:, 8:16], col[2][:, 0:8]))
                act.wait_ge(x_turned, 4 * (k + 1))
                act.wait_ge(col_ready, 1 if k == 0 else 3)
                for c in (0, 1, 4, 5):
                    act.activation(h32[:, c, :], bank[base + c // 2][:, S * (c % 2):S * (c % 2 + 1)], ACT.Identity,
                                   bias=shift[:, c:c + 1], scale=gain[:, c:c + 1]).then_inc(h_even, 1)
                for m in range(KC // 2):
                    act.wait_ge(h_even if m % 2 == 0 else h_odd, 4 * k + (m // 2 + 1) * 2)
                    act.activation(hhi[:, 2 * m:2 * m + 2, :], h32[:, 2 * m:2 * m + 2, :], ACT.Copy).then_inc(h_hi, 1)

            def take_unit(u):
                b, what, c0, n, dest = UNITS[u]
                src = bank[B_UNIT + u % 2]
                act.wait_ge(units, u + 1)
                if what == "features":
                    scale = SCALE if T_QSB <= dest < T_KSB else 1.0
                    ins = act.activation(qk[0:n, dest, :], src[0:n, 0:S], ACT.Copy, scale=scale)
                    if dest == T_KIX:
                        ins = act.activation(qk[HD:2 * HD, dest, :], src[0:HD, 0:S], ACT.Copy)
                elif what == "index weights":
                    ins = act.activation(wix[:, dest[0], :], src[:, 0:n], ACT.Copy)
                elif what == "values":
                    ins = act.activation(v[:, dest[0], dest[1]:dest[1] + n], src[:, 0:n], ACT.Copy)
                else:
                    if u == FIRST_GATE:
                        act.wait_ge(bg_ready, 1)
                    ins = act.activation(gates[:, dest, :], src[:, 0:S], ACT.Identity, bias=bgc[:, dest:dest + 1])
                ins.then_inc(unit_read, 1)

            act.wait_ge(c_in, 16)
            act.activation(csil[:, :], ccol[:, :], ACT.Silu).then_inc(c_ready, 1)
            act.wait_ge(x_in, 16 * TT)
            for t in range(TT):
                square_sums(t, [xt[:, t, :]], t)
            root(0)
            for q in range(2):
                cut_hi(0, q)
            modulate(0)
            for q in range(2, 4):
                cut_hi(0, q)

            for u in range(N_UNITS):
                for b, q in PIECES_AT.get(u, []):
                    cut_hi(b, q)
                take_unit(u)
                if u in LOGITS_AT:
                    h = LOGITS_AT[u]
                    act.wait_ge(logits, h + 1)
                    if h >= 2:
                        act.wait_ge(score_added, TT * (h - 1))
                    act.activation(bufp[h % 2][:, :], bank[B_Z + h % 4][:, 0:CAUSAL], ACT.Relu).then_inc(relu_ready, 1)
                if u in OUTPUT_AT:
                    n = OUTPUT_AT[u]
                    p0, ch = HD * (HEADS[n][1] % 2), O_CHUNK[HEADS[n][0]][HEADS[n][1]]
                    act.wait_ge(o_ready, n + 1)
                    act.activation(ohi[p0:p0 + HD, ch, :], bank[B_O + n % 2][p0:p0 + HD, 0:S], ACT.Copy).then_inc(o_hi, 1)
                if u in SECOND_AT:
                    n = SECOND_AT[u]
                    if n >= 2:
                        act.wait_ge(o_ready, n - 1)
                    if n in SB_NO:
                        act.wait_ge(sums, SB_NO[n] + 1)
                        act.activation(buft[n % 2][:, :], bank[B_Z + n % 2][:, 0:CAUSAL], ACT.Exp).then_inc(a_ready, 1)
                    else:
                        act.wait_ge(p_turned, SOFT_NO[n] + 1)
                        act.activation(buft[n % 2][:, :], bank[B_T + n % 2][:, 0:CAUSAL], ACT.Copy).then_inc(pt_ready, 1)
                if u in SCORES_AT:
                    n = SCORES_AT[u]
                    branch, h = HEADS[n][0:2]
                    if n in SB_NO:
                        act.wait_ge(z_ready, n + 1)
                        if SB_NO[n] == 0:
                            act.wait_ge(p_turned, softs_before(n))
                        z = bank[B_Z + n % 2][:, 0:CAUSAL]
                        e = bufa[n % 2][:, :]
                        if n >= 2:
                            act.wait_ge(sp_ready if n - 2 in SB_NO else p_ready, (SB_NO[n - 2] + 1) if n - 2 in SB_NO else SOFT_NO[n - 2] + 1)
                        then(act.activation(e, z, ACT.Abs))
                        then(act.activation(e, e, ACT.Exp, scale=-1.0))
                        act.activation(e, e, ACT.Ln, bias=1.0).then_inc(ln_ready, 1)
                    else:
                        i = SOFT_NO[n]
                        slope = SLOPES[2 * h + (branch == "ds")]
                        act.wait_ge(max_ready, i + 1)
                        if n >= 2:
                            if n - 2 in SB_NO:
                                act.wait_ge(sums, SB_NO[n - 2] + 1)
                            else:
                                act.wait_ge(p_turned, SOFT_NO[n - 2] + 1)
                        for t, (c0, c1) in enumerate(((0, P), (P, CAUSAL))):
                            ins = act.activation(bufp[n % 2][:, c0:c1], bufa[n % 2][:, c0:c1], ACT.Exp, scale=slope,
                                                 bias=smax[:, n % 2, t:t + 1], accum_out=ssum[:, n % 2, t:t + 1])
                        ins.then_inc(exp_ready, 1)

            act.wait_ge(unit_read, N_UNITS)
            for i in range(4):
                view = gates[:, :, :].rearrange("p (b f) n -> p b f n", b=3)[:, :, 2 * i:2 * i + 2, :]
                act.activation(view.rearrange("p b f n -> p b (f n)"), view.rearrange("p b f n -> p b (f n)"),
                               ACT.Sigmoid).then_inc(sig_ready, 1)

            def spread_rows(g):
                for n in range(2):
                    act.wait_ge(m_spread, 2 * (g - 1) + n + 1)
                    act.activation(gb[g][:, BANK * n:BANK * (n + 1)], bank[6 + n][:, :], ACT.Copy).then_inc(gb_ready, 1)

            for f in range(KC):
                b = B_PROJ + f // 2
                for q in (0, 1) if f % 2 == 0 else (2, 3):
                    cut_hi(b + 1, q)
                act.wait_ge(merged, f + 1)
                act.wait_ge(units, N_UNITS)
                act.activation(hhi[:, f, :], h32[:, f, :], ACT.Copy).then_inc(m_hi, 1)
                if f == 1:
                    spread_rows(1)
            for q in range(4):
                cut_hi(B_WO + 1, q)

            spread_rows(2)
            for t in range(TT):
                act.wait_ge(units, BLOCK_DONE[B_WO - 1] + 2 * (t + 1))
                square_sums(t, [bank[2 * t + n][:, :] for n in range(2)], 4 + 2 * t)

            def cut_up_hi(i, slot, q, first=False):
                if q == 0:
                    act.wait_ge(raw_in[slot], RAW_COUNT[slot] + 16 * (i + 1 + slot))
                    if first:
                        act.wait_ge(units, BLOCK_DONE[B_WO + i])
                    else:
                        act.wait_ge(up_done, 2 * (i - 1))
                act.activation(block_view(whi[slot], B_FFN)[:, 2 * q:2 * q + 2, :],
                               block_view(raw[slot], B_FFN)[:, 2 * q:2 * q + 2, :], ACT.Copy).then_inc(up_hi, 1)

            def cut_down_hi(i, slot, first=False):
                act.wait_ge(down_in[slot], 8 * (i + 1 + slot))
                if not first:
                    act.wait_ge(down_done, i - 1)
                act.activation(dhi[slot][:, :, :], draw[slot][:, :, :], ACT.Copy).then_inc(d_hi, 1)

            root(1)
            for q in range(4):
                cut_up_hi(0, 1, q, True)
            for t in range(TT):
                act.wait_ge(x_new, 2 * (t + 1))
                square_sums(t, [xt[:, t, :]], 8 + t)
            root(2)
            modulate(1)
            cut_down_hi(0, 1, True)

            def silu_tile(i, slot, j):
                act.wait_ge(up_done, 2 * i + j + 1)
                act.activation(fsil[slot][:, j, :], bank[2 * (1 - slot) + j][:, 0:S], ACT.Silu).then_inc(silu_done, 1)

            def f_part(i, slot, j):
                act.wait_ge(f_ready, 2 * i + j + 1)
                act.activation(fhi[slot][:, j, :], fsil[slot][:, j, :], ACT.Copy).then_inc(f_hi, 1)

            def step(i, slot, first, last):
                if not last:
                    for q in range(2):
                        cut_up_hi(i + 1, 1 - slot, q, first)
                silu_tile(i, slot, 0)
                if not last:
                    for q in range(2, 4):
                        cut_up_hi(i + 1, 1 - slot, q, first)
                f_part(i, slot, 0)
                silu_tile(i, slot, 1)
                if not last:
                    cut_down_hi(i + 1, 1 - slot, first)
                f_part(i, slot, 1)

            step(0, 1, True, False)
            with act.Fori(1, N_FFN - 2, 2) as i:
                step(i, 0, False, False)
                step(i + 1, 1, False, False)
            step(N_FFN - 2, 0, False, False)
            step(N_FFN - 1, 1, False, True)
            for t in range(TT):
                act.wait_ge(down_done, N_FFN + t)
                square_sums(t, [bank[4 + 2 * t + n][:, :] for n in range(2)], 10 + 2 * t)
            root(3)

        @block.vector
        def _(dve):
            steps = [0]

            def then(ins):
                steps[0] += 1
                ins.then_inc(dve_step, 1)
                dve.wait_ge(dve_step, steps[0])

            def cut_lo(b, q):
                dve.wait_ge(w_hi, 4 * b + q + 1)
                r = RAW_OF_BLOCK[b]
                p, k0, k1 = block_parts(b)[q]
                dve.tensor_tensor(block_view(wlo[b % 2], b)[0:p, k0:k1, :], block_view(raw[r % 2], b)[0:p, k0:k1, :],
                                  block_view(whi[b % 2], b)[0:p, k0:k1, :].bitcast(F32), ALU.subtract).then_inc(w_lo, 1)

            def inverse_root(k, ss):
                then(dve.tensor_scalar(rinv[:, 0:2], ss, 1.0 / D, EPS, ALU.mult, ALU.add))
                dve.sem_inc(var_ready, 1)
                dve.wait_ge(sqrt_ready, k + 1)
                r, t = stat[:, 14:16], rinv[:, 2:4]
                then(dve.reciprocal(r, rinv[:, 2:4]))
                then(dve.tensor_tensor(t, r, r, ALU.mult))
                then(dve.tensor_tensor(t, t, rinv[:, 0:2], ALU.mult))
                then(dve.tensor_scalar(t, t, -0.5, 1.5, ALU.mult, ALU.add))
                then(dve.tensor_tensor(r, r, t, ALU.mult))

            def normalise(k):
                for t in range(TT):
                    dve.tensor_scalar(xn[:, t, :], xt[:, t, :], stat[:, 14 + t:15 + t], None, ALU.mult).then_inc(xn_ready, 1)

            def modulate(k):
                base, (shift, gain) = (0, (col[0][:, 0:8], col[0][:, 8:16])) if k == 0 else (4, (col[1][:, 8:16], col[2][:, 0:8]))
                dve.wait_ge(x_turned, 4 * (k + 1))
                for c in (2, 3, 6, 7):
                    dve.tensor_scalar(h32[:, c, :], bank[base + c // 2][:, S * (c % 2):S * (c % 2 + 1)], gain[:, c:c + 1],
                                      shift[:, c:c + 1], ALU.mult, ALU.add).then_inc(h_odd, 1)
                for m in range(KC // 2):
                    dve.wait_ge(h_hi, 4 * k + m + 1)
                    dve.tensor_tensor(hlo[:, 2 * m:2 * m + 2, :], h32[:, 2 * m:2 * m + 2, :],
                                      hhi[:, 2 * m:2 * m + 2, :].bitcast(F32), ALU.subtract).then_inc(h_lo, 1)

            def rows(g):
                dve.wait_ge(gemv, 4 * (g + 1))
                dve.wait_ge(rows_in, (32, 64, 112)[g])
                if g:
                    dve.wait_ge(m_turned, g)
                    dve.wait_ge(m_spread, 2 * (g - 1))
                then(dve.tensor_tensor(mrow[:, :], bank[6][:, :], brow[:, :], ALU.add))
                lo, hi = mrow[0:HD, :], mrow[HD:P, :]
                if g == 0:
                    ins = dve.scalar_tensor_tensor(hi, hi, 1.0, grow[HD:P, :], ALU.add, ALU.mult)
                elif g == 1:
                    ins = dve.tensor_tensor(lo, lo, grow[0:HD, :], ALU.mult)
                else:
                    dve.scalar_tensor_tensor(lo, lo, 1.0, grow[0:HD, :], ALU.add, ALU.mult)
                    ins = dve.tensor_tensor(hi, hi, grow[HD:P, :], ALU.mult)
                then(ins)
                dve.sem_inc(m_ready, 1)

            def columns(g):
                dve.wait_ge(m_turned, g + 1)
                then(dve.tensor_copy(col[g][:, :].rearrange("p (j c) -> p j c", j=4),
                                     bank[7][:, :].rearrange("p (c j r) -> p j c r", c=4, j=4)[:, :, :, 0]))
                dve.sem_inc(col_ready, 1)

            then(dve.memset(select[:, :, :], 0.0))
            for j in range(4):
                ins = dve.memset(select[32 * j:32 * j + 1, j, :], 1.0)
            then(ins)
            dve.wait_ge(c_ready, 1)
            dve.tensor_copy(crep[:, :, :], csil[:, :, None].to_broadcast([P, KC, 32])).then_inc(c_ready, 1)
            dve.wait_ge(ss_ready, 2)
            inverse_root(0, stat[:, 0:2])
            normalise(0)
            rows(0)
            columns(0)
            for q in range(2):
                cut_lo(0, q)
            modulate(0)
            for q in range(2, 4):
                cut_lo(0, q)
            dve.wait_ge(bg_turned, 1)
            dve.tensor_copy(bgc[:, :], bank[5][:, 0:3 * KC]).then_inc(bg_ready, 1)

            def reach(n):
                return dsel if HEADS[n][0] == "ds" else dist

            for u in range(N_UNITS):
                for b, q in PIECES_AT.get(u, []):
                    cut_lo(b, q)
                if u in LOGITS_AT:
                    h = LOGITS_AT[u]
                    dve.wait_ge(relu_ready, h + 1)
                    if h == 0:
                        dve.wait_ge(unit_read, 7)
                    else:
                        dve.wait_ge(score_added, TT * h)
                    for t, (c0, c1) in enumerate(((0, P), (P, CAUSAL))):
                        w = wix[:, t, h:h + 1]
                        if h == 0:
                            ins = dve.tensor_scalar(score[:, c0:c1], bufp[0][:, c0:c1], w, 0.0, ALU.mult, ALU.add)
                        else:
                            ins = dve.scalar_tensor_tensor(score[:, c0:c1], bufp[h % 2][:, c0:c1], w, score[:, c0:c1],
                                                           ALU.mult, ALU.add)
                        ins.then_inc(score_added, 1)
                if u in ROUND_AT:
                    r = ROUND_AT[u]
                    src = score if r == 0 else work
                    if r == 0:
                        dve.wait_ge(score_masked, 2)
                    halves = ((0, 0, P), (1, P, CAUSAL))
                    for t, c0, c1 in halves:
                        ins = dve.max(top8[:, t, :], src[:, c0:c1])
                    then(ins)
                    for t, c0, c1 in halves:
                        ins = dve.match_replace(work[:, c0:c1], top8[:, t, :], src[:, c0:c1], TAKEN)
                    then(ins)
                    if r == TOPK_ROUNDS - 1:
                        then(dve.tensor_tensor(work[:, :], work[:, :], score[:, :], ALU.not_equal))
                        then(dve.tensor_scalar(work[:, :], work[:, :], -MASKED, MASKED, ALU.mult, ALU.add))
                        dve.wait_ge(consts, 10)
                        then(dve.tensor_tensor(dsel[:, :], work[:, :], dist[:, :], ALU.add))
                if u in OUTPUT_AT:
                    n = OUTPUT_AT[u]
                    p0, ch = HD * (HEADS[n][1] % 2), O_CHUNK[HEADS[n][0]][HEADS[n][1]]
                    dve.wait_ge(o_hi, n + 1)
                    dve.tensor_tensor(olo[p0:p0 + HD, ch, :], bank[B_O + n % 2][p0:p0 + HD, 0:S],
                                      ohi[p0:p0 + HD, ch, :].bitcast(F32), ALU.subtract).then_inc(o_lo, 1)
                if u in NORM_AT and NORM_AT[u] in SOFT_NO:
                    n = NORM_AT[u]
                    i = SOFT_NO[n]
                    dve.wait_ge(exp_ready, i + 1)
                    then(dve.reciprocal(ssum[:, n % 2, :], ssum[:, n % 2, :]))
                    for t, (c0, c1) in enumerate(((0, P), (P, CAUSAL))):
                        ins = dve.tensor_scalar(bufp[n % 2][:, c0:c1], bufp[n % 2][:, c0:c1], ssum[:, n % 2, t:t + 1], None, ALU.mult)
                    ins.then_inc(p_ready, 1)
                if u in SCORES_AT:
                    n = SCORES_AT[u]
                    branch, h = HEADS[n][0:2]
                    z = bank[B_Z + n % 2][:, 0:CAUSAL]
                    if n in SB_NO:
                        i = SB_NO[n]
                        dve.wait_ge(ln_ready, i + 1)
                        if n >= 2:
                            if n - 2 in SB_NO:
                                dve.wait_ge(sums, SB_NO[n - 2] + 1)
                            else:
                                dve.wait_ge(p_turned, SOFT_NO[n - 2] + 1)
                        dve.scalar_tensor_tensor(bufp[n % 2][:, :], z, 0.0, bufa[n % 2][:, :], ALU.max, ALU.add).then_inc(sp_ready, 1)
                    else:
                        i = SOFT_NO[n]
                        slope = SLOPES[2 * h + (branch == "ds")]
                        dve.wait_ge(z_ready, n + 1)
                        if n == 0:
                            dve.wait_ge(consts, 10)
                        then(dve.scalar_tensor_tensor(bufa[n % 2][:, :], z, SCALE / slope, reach(n)[:, :], ALU.mult, ALU.add))
                        for t, (c0, c1) in enumerate(((0, P), (P, CAUSAL))):
                            ins = dve.reduce_max(smax[:, n % 2, t:t + 1], bufa[n % 2][:, c0:c1], AX_X)
                        then(ins)
                        dve.tensor_scalar(smax[:, n % 2, :], smax[:, n % 2, :], -slope, None, ALU.mult).then_inc(max_ready, 1)

            def merge_tile(f):
                if f % 2 == 0:
                    dve.wait_ge(sig_ready, f // 2 + 1)
                dve.wait_ge(units, N_UNITS + f + 1)
                if f >= 1:
                    dve.wait_ge(merged, f)
                for br in range(3):
                    dve.tensor_tensor(gp[br], bank[2 * br + f % 2][:, 0:S], gates[:, KC * br + f, :], ALU.mult).then_inc(gated, 1)

            def merge_lo(f):
                dve.wait_ge(m_hi, f + 1)
                dve.tensor_tensor(hlo[:, f, :], h32[:, f, :], hhi[:, f, :].bitcast(F32), ALU.subtract).then_inc(m_lo, 1)

            for f in range(KC):
                b = B_PROJ + f // 2
                for q in (0, 1) if f % 2 == 0 else (2, 3):
                    cut_lo(b + 1, q)
                if f == 0:
                    rows(1)
                merge_tile(f)
                merge_lo(f)
                if f == 1:
                    columns(1)
            for q in range(4):
                cut_lo(B_WO + 1, q)
            rows(2)
            columns(2)

            def add_residual(k, g, base):
                for t in range(TT):
                    for n in range(2):
                        cols = slice(BANK * n, BANK * (n + 1))
                        then(dve.scalar_tensor_tensor(xn[:, t, cols], bank[base + 2 * t + n][:, :], stat[:, 14 + t:15 + t],
                                                      gb[g][:, cols], ALU.mult, ALU.mult))
                        dve.tensor_tensor(xt[:, t, cols], xt[:, t, cols], xn[:, t, cols], ALU.add).then_inc(x_new, 1)

            def pair_sums(k, at):
                dve.wait_ge(ss_ready, 2 * (k + 1))
                pair = stat[:, at:at + 4].rearrange("p (t n) -> p t n", n=2)
                then(dve.tensor_tensor(rinv[:, 0:2], pair[:, :, 0], pair[:, :, 1], ALU.add))

            pair_sums(1, 4)
            inverse_root(1, rinv[:, 0:2])
            dve.wait_ge(gb_ready, 2)
            add_residual(1, 1, 0)

            def cut_up_lo(i, slot, q):
                dve.wait_ge(up_hi, 4 * i + q + 1)
                dve.tensor_tensor(block_view(wlo[slot], B_FFN)[:, 2 * q:2 * q + 2, :], block_view(raw[slot], B_FFN)[:, 2 * q:2 * q + 2, :],
                                  block_view(whi[slot], B_FFN)[:, 2 * q:2 * q + 2, :].bitcast(F32), ALU.subtract).then_inc(up_lo, 1)

            def cut_down_lo(i, slot):
                dve.wait_ge(d_hi, i + 1)
                dve.tensor_tensor(dlo[slot][:, :, :], draw[slot][:, :, :], dhi[slot][:, :, :].bitcast(F32), ALU.subtract).then_inc(d_lo, 1)

            cut_up_lo(0, 1, 0)
            cut_up_lo(0, 1, 1)
            dve.wait_ge(ss_ready, 6)
            inverse_root(2, stat[:, 8:10])
            normalise(1)
            cut_up_lo(0, 1, 2)
            cut_up_lo(0, 1, 3)
            modulate(1)
            cut_down_lo(0, 1)

            def f_tile(i, slot, j):
                dve.wait_ge(silu_done, 2 * i + j + 1)
                dve.tensor_tensor(fsil[slot][:, j, :], bank[2 * (1 - slot) + j][:, S:2 * S], fsil[slot][:, j, :], ALU.mult).then_inc(f_ready, 1)

            def f_rest(i, slot, j):
                dve.wait_ge(f_hi, 2 * i + j + 1)
                dve.tensor_tensor(flo[slot][:, j, :], fsil[slot][:, j, :], fhi[slot][:, j, :].bitcast(F32), ALU.subtract).then_inc(f_lo, 1)

            def step(i, slot, last):
                if not last:
                    for q in range(2):
                        cut_up_lo(i + 1, 1 - slot, q)
                f_tile(i, slot, 0)
                if not last:
                    for q in range(2, 4):
                        cut_up_lo(i + 1, 1 - slot, q)
                f_rest(i, slot, 0)
                f_tile(i, slot, 1)
                if not last:
                    cut_down_lo(i + 1, 1 - slot)
                f_rest(i, slot, 1)

            step(0, 1, False)
            with dve.Fori(1, N_FFN - 2, 2) as i:
                step(i, 0, False)
                step(i + 1, 1, False)
            step(N_FFN - 2, 0, False)
            step(N_FFN - 1, 1, True)
            pair_sums(3, 10)
            inverse_root(3, rinv[:, 0:2])
            dve.wait_ge(gb_ready, 4)
            add_residual(3, 2, 4)

        @block.tensor
        def _(pe):
            def three(dst, a, b, first, last):
                pe.matmul(dst, a[0], b[0], start=first, stop=False)
                pe.matmul(dst, a[0], b[1], start=False, stop=False)
                return pe.matmul(dst, a[1], b[0], start=False, stop=last)

            def products(g):
                if g:
                    pe.wait_ge(o_lo, N_HEADS) if g == 1 else pe.wait_ge(gb_ready, 1)
                for u in range(4):
                    if g == 0 and u >= 2:
                        pe.wait_ge(ada_in[u - 2], 16)
                        buf = ada_end[u - 2]
                    else:
                        r = RAW_OF_ADA[(g, u)]
                        pe.wait_ge(raw_in[r % 2], RAW_ARRIVED[r])
                        buf = raw[r % 2]
                    w = buf[:, :].rearrange("p (k n) -> p k n", k=2)
                    for kk in range(2):
                        k = 2 * u + kk
                        for j in range(4):
                            mm = pe.matmul(bank[6][32 * j:32 * j + 32, :], crep[:, k, :], w[:, kk, BANK * j:BANK * (j + 1)],
                                           start=k == 0, stop=k == KC - 1, tile_position=(0, 32 * j))
                    mm.then_inc(gemv, 1)

            def turn_rows(g):
                pe.wait_ge(m_ready, g + 1)
                if g == 1:
                    pe.wait_ge(o_lo, N_HEADS)
                elif g == 2:
                    pe.wait_ge(gb_ready, 2)
                for n in range(4):
                    mm = pe.transpose(bank[7][:, P * n:P * (n + 1)], mrow[:, P * n:P * (n + 1)], ident[:, :])
                mm.then_inc(m_turned, 1)

            def spread_rows(g):
                for n in range(2):
                    j = n if g == 1 else 2 + n
                    if n:
                        pe.wait_ge(col_ready, g + 1)
                    pe.matmul(bank[6 + n][:, :], select[:, j, :], mrow[:, :], start=True, stop=True).then_inc(m_spread, 1)

            def turn_x(k):
                base = 4 * k
                pe.wait_ge(xn_ready, 2 * (k + 1))
                for m in range(KC // 2):
                    for kk in range(2):
                        for t in range(TT):
                            c0 = P * (2 * m + kk)
                            mm = pe.transpose(bank[base + m][:, S * kk + P * t:S * kk + P * (t + 1)], xn[:, t, c0:c0 + P], ident[:, :])
                    mm.then_inc(x_turned, 1)

            def unit(u):
                b, what, c0, n, dest = UNITS[u]
                if u >= 2:
                    pe.wait_ge(unit_read, u - 1)
                w = [block_view(x[b % 2], b)[:, :, c0:c0 + n] for x in (whi, wlo)]
                for k in range(KC):
                    if k % 2 == 0 and (u == 0 or UNITS[u - 1][0] != b):
                        pe.wait_ge(w_hi, 4 * b + k // 2 + 1)
                        pe.wait_ge(w_lo, 4 * b + k // 2 + 1)
                    if u == 0 and k % 2 == 0:
                        pe.wait_ge(h_hi, k // 2 + 1)
                        pe.wait_ge(h_lo, k // 2 + 1)
                    if what in ("features", "gate"):
                        mm = three(bank[B_UNIT + u % 2][0:n, 0:S], [x[:, k, :] for x in w], [hhi[:, k, :], hlo[:, k, :]],
                                   k == 0, k == KC - 1)
                    else:
                        t = dest[0]
                        mm = three(bank[B_UNIT + u % 2][:, 0:n], [x[:, k, P * t:P * (t + 1)] for x in (hhi, hlo)],
                                   [x[:, k, :] for x in w], k == 0, k == KC - 1)
                mm.then_inc(units, 1)

            def query_major(dst, q, k, p0):
                pe.matmul(dst[:, 0:P], q[p0:p0 + HD, 0:P], k[p0:p0 + HD, 0:P], start=True, stop=True)
                return pe.matmul(dst[:, P:CAUSAL], q[p0:p0 + HD, P:S], k[p0:p0 + HD, :], start=True, stop=True)

            def key_major(dst, q, k, p0):
                pe.matmul(dst[:, 0:S], k[p0:p0 + HD, 0:P], q[p0:p0 + HD, :], start=True, stop=False, skip_group_check=True)
                return pe.matmul(dst[:, S:CAUSAL], k[p0:p0 + HD, P:S], q[p0:p0 + HD, P:S], start=False, stop=True,
                                 skip_group_check=True)

            def scores(n):
                branch, h, tq, tk, _ = HEADS[n]
                q, k, p0 = qk[:, tq + h // 2, :], qk[:, tk + h // 2, :], HD * (h % 2)
                if n < 2:
                    pe.wait_ge(relu_ready, H_IX)
                elif n - 2 in SB_NO:
                    pe.wait_ge(a_ready, SB_NO[n - 2] + 1)
                else:
                    pe.wait_ge(max_ready, SOFT_NO[n - 2] + 1)
                (key_major if n in SB_NO else query_major)(bank[B_Z + n % 2], q, k, p0).then_inc(z_ready, 1)

            def second(n):
                if n in SB_NO:
                    i = SB_NO[n]
                    pe.wait_ge(sp_masked, 2 * (i + 1))
                    z, s = bank[B_Z + n % 2], bufp[n % 2]
                    pe.matmul(z[:, 0:CAUSAL], tri[:, :], s[:, :], start=False, stop=False, skip_group_check=True)
                    pe.matmul(z[:, P:S], neg1[:, :], s[:, S:CAUSAL], start=False, stop=True, skip_group_check=True).then_inc(sums, 1)
                else:
                    i = SOFT_NO[n]
                    pe.wait_ge(p_ready, i + 1)
                    if i >= 1:
                        pe.wait_ge(pt_ready, i)
                    for c in range(3):
                        mm = pe.transpose(bank[B_T + n % 2][:, P * c:P * (c + 1)], bufp[n % 2][:, P * TURNED[c]:P * (TURNED[c] + 1)], ident[:, :])
                    mm.then_inc(p_turned, 1)

            def output(n):
                branch, h, _, _, v0 = HEADS[n]
                if n in SB_NO:
                    pe.wait_ge(a_masked, 2 * (SB_NO[n] + 1))
                else:
                    pe.wait_ge(pt_ready, SOFT_NO[n] + 1)
                if n >= 2:
                    pe.wait_ge(o_lo, n - 1)
                p0, a = HD * (h % 2), buft[n % 2]
                dst, cols = bank[B_O + n % 2][p0:p0 + HD, :], slice(v0 + HD * h, v0 + HD * (h + 1))
                pe.matmul(dst[:, 0:S], v[:, 0, cols], a[:, 0:S], start=True, stop=False, skip_group_check=True)
                pe.matmul(dst[:, P:S], v[:, 1, cols], a[:, S:CAUSAL], start=False, stop=True, skip_group_check=True).then_inc(o_ready, 1)

            pe.wait_ge(consts, 7)
            turn_x(0)
            pe.wait_ge(bg_in, 16)
            pe.transpose(bank[5][:, 0:3 * KC], bgr[:, :], ident[0:3 * KC, 0:3 * KC]).then_inc(bg_turned, 1)
            pe.wait_ge(c_ready, 2)
            products(0)
            turn_rows(0)
            for u in range(N_UNITS):
                if u == 0:
                    pe.wait_ge(h_even, 4)
                    pe.wait_ge(h_odd, 4)
                unit(u)
                if u in LOGITS_AT:
                    h = LOGITS_AT[u]
                    pe.wait_ge(unit_read, 5)
                    if h == 0:
                        pe.wait_ge(bg_ready, 1)
                    if h >= 4:
                        pe.wait_ge(relu_ready, h - 3)
                    query_major(bank[B_Z + h % 4], qk[:, T_QIX + h // 2, :], qk[:, T_KIX, :], HD * (h % 2)).then_inc(logits, 1)
                if u in OUTPUT_AT:
                    output(OUTPUT_AT[u])
                if u in SECOND_AT:
                    second(SECOND_AT[u])
                if u in SCORES_AT:
                    scores(SCORES_AT[u])

            products(1)
            for f in range(KC):
                b = B_PROJ + f // 2
                if f % 2 == 0:
                    pe.wait_ge(w_hi, 4 * (b + 1))
                    pe.wait_ge(w_lo, 4 * (b + 1))
                if f == 0:
                    pe.wait_ge(o_hi, N_HEADS)
                    pe.wait_ge(o_lo, N_HEADS)
                if f < 2:
                    pe.wait_ge(unit_read, N_UNITS)
                else:
                    pe.wait_ge(gated, 3 * (f - 1))
                w = [block_view(x[b % 2], b)[:, :, P * (f % 2):P * (f % 2 + 1)] for x in (whi, wlo)]
                for i, branch in enumerate(("sb", "mb", "ds")):
                    for c, ch in enumerate(BRANCH_CHUNKS[branch]):
                        rows_ = P if ch < FULL_OCH else HD
                        mm = three(bank[2 * i + f % 2][:, 0:S], [x[0:rows_, ch, :] for x in w],
                                   [ohi[0:rows_, ch, :], olo[0:rows_, ch, :]], c == 0, c == 2)
                mm.then_inc(units, 1)
                if f == 1:
                    turn_rows(1)
                    spread_rows(1)
            products(2)

            for t in range(TT):
                for half in range(2):
                    b = B_WO + half
                    if t == 0:
                        pe.wait_ge(w_hi, 4 * (b + 1))
                        pe.wait_ge(w_lo, 4 * (b + 1))
                        pe.wait_ge(m_lo, 4 * (half + 1))
                        if half == 0:
                            pe.wait_ge(gated, 3 * KC)
                    for n in range(2):
                        for kk in range(4):
                            k = 4 * half + kk
                            mm = three(bank[2 * t + n][:, :], [x[:, k, P * t:P * (t + 1)] for x in (hhi, hlo)],
                                       [block_view(x[b % 2], b)[:, kk, BANK * n:BANK * (n + 1)] for x in (whi, wlo)],
                                       k == 0, k == KC - 1)
                    mm.then_inc(units, 1)
                if t == 0:
                    turn_rows(2)
                    spread_rows(2)

            pe.wait_ge(gb_ready, 4)
            turn_x(1)

            def up_tile(i, slot, j):
                dst = bank[2 * (1 - slot) + j]
                for a in range(2):
                    for k in range(KC):
                        w = [block_view(x[slot], B_FFN)[:, k, FSTEP * a + P * j:FSTEP * a + P * (j + 1)] for x in (whi, wlo)]
                        mm = three(dst[:, S * a:S * (a + 1)], w, [hhi[:, k, :], hlo[:, k, :]], k == 0, k == KC - 1)
                mm.then_inc(up_done, 1)

            def up(i, slot, first):
                pe.wait_ge(up_hi, 4 * (i + 1))
                pe.wait_ge(up_lo, 4 * (i + 1))
                for j in range(2):
                    if first:
                        pe.wait_ge(h_lo, KC)
                        pe.wait_ge(x_new, 2 * TT)
                    else:
                        pe.wait_ge(f_ready, 2 * (i - 2) + j + 1)
                    up_tile(i, slot, j)

            def down(i, slot, first, last):
                pe.wait_ge(d_hi, i + 1)
                pe.wait_ge(d_lo, i + 1)
                pe.wait_ge(f_lo, 2 * (i + 1))
                for t in range(TT):
                    for n in range(2):
                        for j in range(2):
                            mm = three(bank[4 + 2 * t + n][:, :], [x[:, j, P * t:P * (t + 1)] for x in (fhi[slot], flo[slot])],
                                       [x[slot][:, j, BANK * n:BANK * (n + 1)] for x in (dhi, dlo)],
                                       first and j == 0, last and j == 1)
                    if last:
                        mm.then_inc(down_done, 1)
                if not last:
                    mm.then_inc(down_done, 1)

            up(0, 1, True)
            up(1, 0, True)
            down(0, 1, True, False)
            with pe.Fori(2, N_FFN - 1, 2) as i:
                up(i, 1, False)
                down(i - 1, 0, False, False)
                up(i + 1, 0, False)
                down(i, 1, False, False)
            up(N_FFN - 1, 1, False)
            down(N_FFN - 2, 0, False, False)
            down(N_FFN - 1, 1, False, True)


LOGITS_LAST = max(LOGITS_AT)
TURNED = (0, 1, 2)


_INS = ["x", "c", "w_ada", "b_ada", "g_pre_mix", "g_post_mix", "w_in", "b_gate", "w_proj_sb", "w_proj_moba",
        "w_proj_dsa", "w_o", "g_pre_ffn", "g_post_ffn", "w_up", "w_down"]
_OUTS = [((1, S, D), "float32")]


def kernel(**inputs):
    import numpy as _np
    import concourse.bacc as _bacc
    from concourse import mybir as _mybir
    from concourse.bass_utils import run_bass_kernel_spmd as _run

    nc = _bacc.Bacc("TRN2", target_bir_lowering=False, num_devices=1)
    arrays, args = {}, []
    for name in _INS:
        a = _np.ascontiguousarray(inputs[name])
        arrays[f"in_{name}_dram"] = a
        args.append(nc.dram_tensor(f"in_{name}_dram", a.shape, _mybir.dt.from_np(a.dtype), kind="ExternalInput").ap())
    for i, (shape, dtype) in enumerate(_OUTS):
        dt = _mybir.dt.from_np(_np.dtype(dtype))
        args.append(nc.dram_tensor(f"out_{i}_dram", shape, dt, kind="ExternalOutput").ap())
    decoder_layer(nc, *args)
    r = _run(nc, [arrays], core_ids=[0])
    return r.results[0]["out_0_dram"]
```

```python
from contextlib import ExitStack

import concourse.bass as bass
from concourse import mybir

F32 = mybir.dt.float32
F32R = mybir.dt.float32r
ALU = mybir.AluOpType
ACT = mybir.ActivationFunctionType
AX_X = mybir.AxisListType.X

P = 128
D = 1024
KC = D // P
S = 256
TT = S // P
HD = 64
H_SB, H_MB, H_DS, H_IX = 6, 5, 5, 8
W_SB, W_MB, W_DS, W_IX = H_SB * HD, H_MB * HD, H_DS * HD, H_IX * HD
FF = 2816
TOPK = min(256, S // 4)
EPS = 1e-6
SCALE = HD ** -0.5
MASKED = -1e30
TAKEN = -3e38
SLOPES = [2.0 ** (-8.0 * (i + 1) / (H_MB + H_DS)) for i in range(H_MB + H_DS)]
CAUSAL = 3 * P
BANK = 512

sizes = [W_SB] * 3 + [W_MB] * 3 + [W_DS] * 3 + [W_IX, HD, H_IX, 3 * D]
offs = [sum(sizes[:i]) for i in range(len(sizes))]
(O_QSB, O_KSB, O_VSB, O_QMB, O_KMB, O_VMB, O_QDS, O_KDS, O_VDS, O_QIX, O_KIX, O_WIX, O_GATE) = offs

T_QIX, T_KIX, T_QMB, T_KMB, T_QSB, T_KSB, T_QDS, T_KDS, T_END = 0, 4, 5, 8, 11, 14, 17, 20, 23
V_MB, V_SB, V_DS = 0, W_MB, W_MB + W_SB

GATE_BLOCKS = 3 * D // BANK
MIX_BLOCKS = [(O_KIX, HD + H_IX), (O_QIX, W_IX), (O_QMB, W_MB), (O_KMB, W_MB), (O_VMB, W_MB),
              (O_QSB, W_SB), (O_KSB, W_SB), (O_VSB, W_SB), (O_QDS, W_DS), (O_KDS, W_DS), (O_VDS, W_DS)]
MIX_BLOCKS += [(O_GATE + BANK * i, BANK) for i in range(GATE_BLOCKS)]
N_MIX = len(MIX_BLOCKS)
PROJ_COLS = 256
N_PROJ = D // PROJ_COLS
B_PROJ = N_MIX
B_WO = B_PROJ + N_PROJ
B_FFN = B_WO + 2
FSTEP = 2 * P
N_FFN = FF // FSTEP


def mix_units():
    units = []
    def features(b, tile, cols, base=0):
        for n, c in enumerate(range(0, cols, P)):
            units.append((b, "features", base + c, min(P, cols - c), tile + n))
    def tokens(b, what, base, cols, dest):
        for t in range(TT):
            units.append((b, what, base, cols, (t, dest)))
    units.append((0, "index keys and weights", 0, HD + H_IX, T_KIX))
    features(1, T_QIX, W_IX)
    features(2, T_QMB, W_MB)
    features(3, T_KMB, W_MB)
    tokens(4, "values", 0, W_MB, V_MB)
    features(5, T_QSB, W_SB)
    features(6, T_KSB, W_SB)
    tokens(7, "values", 0, W_SB, V_SB)
    features(8, T_QDS, W_DS)
    features(9, T_KDS, W_DS)
    tokens(10, "values", 0, W_DS, V_DS)
    for g in range(3 * D // P):
        units.append((11 + g // 4, "gate", g % 4 * P, P, g))
    return units


UNITS = mix_units()
N_UNITS = len(UNITS)
FIRST_GATE = N_UNITS - 3 * D // P
UNITS_DONE = [max(n for n, u in enumerate(UNITS) if u[0] == b) + 1 for b in range(N_MIX)]
PROJ_DONE = [N_UNITS + 2 * (i + 1) for i in range(N_PROJ)]
WO_DONE = [PROJ_DONE[-1] + 4, PROJ_DONE[-1] + 6]
BLOCK_DONE = UNITS_DONE + PROJ_DONE + WO_DONE


def y_done(t, n):
    return PROJ_DONE[-1] + 3 * t + 2 + n

O_CHUNK = {"mb": [3, 3, 4, 4, 7], "sb": [0, 0, 1, 1, 2, 2], "ds": [5, 5, 6, 6, 8]}
N_OCH = 9
FULL_OCH = 7
BRANCH_CHUNKS = {"sb": [0, 1, 2], "mb": [3, 4, 7], "ds": [5, 6, 8]}
HEADS = [("mb", h, T_QMB, T_KMB, V_MB) for h in range(H_MB)]
HEADS += [("sb", h, T_QSB, T_KSB, V_SB) for h in range(H_SB)]
HEADS += [("ds", h, T_QDS, T_KDS, V_DS) for h in range(H_DS)]
N_HEADS = len(HEADS)
HEAD_START = 14
HEAD_EVERY = 2
SCORES_AT = {HEAD_START + HEAD_EVERY * n: n for n in range(N_HEADS)}
EXP_AT = {u + 1: n for u, n in SCORES_AT.items()}
NORM_AT = {u + 2: n for u, n in SCORES_AT.items()}
SECOND_AT = {u + 3: n for u, n in SCORES_AT.items()}
OUTPUT_AT = {u + 5: n for u, n in SCORES_AT.items()}
LOGITS_AT = {5 + h: h for h in range(H_IX)}
TOPK_ROUNDS = TOPK // 8
ROUND_AT = {15 + 2 * r: r for r in range(TOPK_ROUNDS)}
N_SOFT = H_MB + H_DS
SOFT_NO = {n: i for i, n in enumerate(n for n in range(N_HEADS) if HEADS[n][0] != "sb")}
SB_NO = {n: i for i, n in enumerate(n for n in range(N_HEADS) if HEADS[n][0] == "sb")}


def softs_before(n):
    return sum(1 for m in SOFT_NO if m < n)


def sbs_before(n):
    return sum(1 for m in SB_NO if m < n)


def pieces_at():
    plan = {}
    for b in range(N_MIX):
        us = [n for n, u in enumerate(UNITS) if u[0] == b]
        for q in range(4):
            plan.setdefault(us[q * len(us) // 4], []).append((b + 1, q))
    return plan


PIECES_AT = pieces_at()

ADA_PARTS = 2 * KC
ADA_USE = [5 + 3 * n for n in range(KC)]
ADA_USE += [31 + (N_UNITS - 4 - 31) * n // (KC - 1) for n in range(KC)]
ADA_AT = {u: n for n, u in enumerate(ADA_USE)}
ADA_LOAD_AT = {0: 0}
ADA_LOAD_AT.update({u: n + 1 for n, u in enumerate(ADA_USE[:-1])})
GEMV_DONE = [4, 4 + KC, 4 + 2 * KC]
ROWS_AT = {ADA_USE[g * KC - 1] + 1: g for g in (1, 2)}
MERGE_PIECES = [[(1, q) for q in range(4)]]
MERGE_PIECES += [[(f // 2 + 2, 0), (f // 2 + 2, 1)] if f % 2 else [(f // 2 + 1, 2), (f // 2 + 1, 3)] for f in range(1, KC - 1)]
MERGE_PIECES += [[(KC // 2 + 1, 0), (KC // 2 + 1, 1)]]
SPREAD_AT = {1: 1, 3: 2}
ROWS_LOAD_AFTER = {2: 1, 13: 2}
TURN_AT = {u + 1: g for u, g in ROWS_AT.items()}
COLUMNS_AT = {u + 1: g for u, g in TURN_AT.items()}
SIGMOID_FROM = max(EXP_AT) + 4
EARLY_GATES = SIGMOID_FROM - FIRST_GATE
SIGMOID_BATCHES = 3


def raw_uses():
    uses = [("ada", 0, u) for u in range(2)]
    uses += [("block", b, 0) for b in range(B_FFN)]
    return uses


RAW = raw_uses()
N_RAW = len(RAW)
LOADS = {b: 1 for b in range(B_FFN)}
LOADS.update({b: 5 for b in range(B_PROJ, B_WO)})


def raw_arrivals():
    count, out = [0, 0], []
    for r, (kind, b, _) in enumerate(RAW):
        count[r % 2] += 16 * (1 if kind == "ada" else LOADS[b])
        out.append(count[r % 2])
    return out, count


RAW_ARRIVED, RAW_COUNT = raw_arrivals()
RAW_OF_BLOCK = {b: r for r, (kind, b, _) in enumerate(RAW) if kind == "block"}


def decoder_layer(nc, x, c, w_ada, b_ada, g_pre_mix, g_post_mix, w_in, b_gate, w_proj_sb,
                  w_proj_moba, w_proj_dsa, w_o, g_pre_ffn, g_post_ffn, w_up, w_down, out):
    ctx = ExitStack()
    with ctx:
        def sb(name, shape, dt=F32, scope=ctx):
            return scope.enter_context(nc.sbuf_tensor(name, shape, dt))

        def sem(name):
            return ctx.enter_context(nc.semaphore(name))

        raw = [sb(f"raw{i}", [P, KC * BANK]) for i in range(2)]
        whi = [sb(f"whi{i}", [P, KC * BANK], F32R) for i in range(2)]
        wlo = [sb(f"wlo{i}", [P, KC * BANK], F32R) for i in range(2)]
        xt = sb("xt", [P, TT, D])
        hhi = sb("hhi", [P, KC, S], F32R)
        hlo = sb("hlo", [P, KC, S], F32R)
        xn = sb("xn", [P, TT, D])
        hx = xn[:, :, :].rearrange("p t (k n) -> p t k n", n=P)
        ada_part = xn[:, :, :].rearrange("p t n -> p (t n)")
        diag = [xn[:, t, D - P:D] for t in range(TT)]
        h32 = xn[:, :, :].rearrange("p t (k n) -> p (t k) n", n=S)
        ident = sb("ident", [P, P])
        crep = sb("crep", [P, KC, 32])
        ccol = sb("ccol", [P, KC])
        csil = sb("csil", [P, KC])
        col = [sb(f"col{g}", [P, 16]) for g in range(3)]
        ssq = sb("ssq", [P, 8, 2])
        var, root_, rinv = (sb(name, [P, 8]) for name in ("var", "root", "rinv"))
        warm = sb("warm", [P, 1])
        mrow = sb("mrow", [P, 2, BANK])
        select = sb("select", [P, 4, P])

        mix = ExitStack()
        v = sb("v", [P, TT, D], scope=mix)
        qk = sb("qk", [P, 3 * KC, S], scope=mix)
        gates = qk
        ohi = sb("ohi", [P, N_OCH, S], F32R, scope=mix)
        olo = sb("olo", [P, N_OCH, S], F32R, scope=mix)
        brow = sb("brow", [P, BANK], scope=mix)
        grow = sb("grow", [P, BANK], scope=mix)
        wix = sb("wix", [P, TT, H_IX], scope=mix)
        wixt = sb("wixt", [HD + H_IX, S], scope=mix)
        dist = sb("dist", [P, CAUSAL], scope=mix)
        dsel = sb("dsel", [P, CAUSAL], scope=mix)
        tri = sb("tri", [P, P], scope=mix)
        neg1 = sb("neg1", [P, P], scope=mix)
        bgr = sb("bgr", [3 * KC, P], scope=mix)
        bgc = sb("bgc", [P, 3 * KC], scope=mix)
        score = sb("score", [P, CAUSAL], scope=mix)
        work = sb("work", [P, CAUSAL], scope=mix)
        top8 = sb("top8", [P, TT, 8], scope=mix)
        bufa = [sb(f"bufa{i}", [P, CAUSAL], scope=mix) for i in range(2)]
        bufp = [sb(f"bufp{i}", [P, CAUSAL], scope=mix) for i in range(2)]
        buft = [sb(f"buft{i}", [P, CAUSAL], scope=mix) for i in range(2)]
        smax = sb("smax", [P, 2, TT], scope=mix)
        ssum = sb("ssum", [P, 2, TT], scope=mix)
        gp = [[b[:, 0:S] for b in bufs] for bufs in ((bufa[0], bufa[1], bufp[0]), (bufp[1], buft[0], buft[1]))]
        mix.close()

        start = ExitStack()
        ada_end = [sb(f"ada_end{i}", [P, KC * BANK], scope=start) for i in range(2)]
        start.close()

        ffn = ExitStack()
        gb = [None] + [sb(f"gb{g}", [P, D], scope=ffn) for g in (1, 2)]
        draw = [sb(f"draw{i}", [P, 2, D], scope=ffn) for i in range(2)]
        dhi = [sb(f"dhi{i}", [P, 2, D], F32R, scope=ffn) for i in range(2)]
        dlo = [sb(f"dlo{i}", [P, 2, D], F32R, scope=ffn) for i in range(2)]
        fsil = [sb(f"fsil{i}", [P, 2, S], scope=ffn) for i in range(2)]
        fhi = [sb(f"fhi{i}", [P, 2, S], F32R, scope=ffn) for i in range(2)]
        flo = [sb(f"flo{i}", [P, 2, S], F32R, scope=ffn) for i in range(2)]
        ffn.close()

        psum = ctx.enter_context(nc.psum_tensor("psum", [P, 8, BANK], F32))
        bank = [psum[:, i, :] for i in range(8)]
        B_UNIT, B_Z, B_T, B_ADA, B_O = 0, 2, 4, 5, 6
        B_ROWS = (7, B_ADA, B_T)
        B_Y = ((6, 0), (4, 6))
        B_TURNED = (2, 4)

        ada_in = [sem(f"ada_in{k}") for k in range(KC // 2, KC)]
        part_in = sem("part_in")
        raw_in = [sem(f"raw_in{i}") for i in range(2)]
        down_in = [sem(f"down_in{i}") for i in range(2)]
        pool_step = sem("pool_step")
        x_in, c_in, rows_in, stored = sem("x_in"), sem("c_in"), sem("rows_in"), sem("stored")
        rows_set, consts = sem("rows_set"), sem("consts")
        w_hi, w_lo = sem("w_hi"), sem("w_lo")
        units = sem("units")
        unit_read = sem("unit_read")
        gemv = sem("gemv")
        c_ready = sem("c_ready")
        act_step, dve_step = sem("act_step"), sem("dve_step")
        ss_ready, var_ready, sqrt_ready, xn_ready = sem("ss_ready"), sem("var_ready"), sem("sqrt_ready"), sem("xn_ready")
        x_turned, h_act, h_dve, h_hi, h_lo = sem("x_turned"), sem("h_act"), sem("h_dve"), sem("h_hi"), sem("h_lo")
        wix_turned, wix_ready, dve_scaled = sem("wix_turned"), sem("wix_ready"), sem("dve_scaled")
        m_ready, m_turned, col_ready, m_spread, gb_ready = (sem("m_ready"), sem("m_turned"), sem("col_ready"),
                                                           sem("m_spread"), sem("gb_ready"))
        bg_in, bg_turned, bg_ready = sem("bg_in"), sem("bg_turned"), sem("bg_ready")
        logits, relu_ready, score_added, score_masked, sel_ready = (sem("logits"), sem("relu_ready"),
                                                                   sem("score_added"), sem("score_masked"), sem("sel_ready"))
        z_ready, y_ready, max_ready, exp_ready, p_ready = sem("z_ready"), sem("y_ready"), sem("max_ready"), sem("exp_ready"), sem("p_ready")
        p_turned, pt_ready = sem("p_turned"), sem("pt_ready")
        ln_ready, sp_ready, sp_masked, sums, a_ready, a_masked = (sem("ln_ready"), sem("sp_ready"), sem("sp_masked"),
                                                                 sem("sums"), sem("a_ready"), sem("a_masked"))
        o_ready, o_hi, o_lo = sem("o_ready"), sem("o_hi"), sem("o_lo")
        sig_ready, gated, merged, m_hi, m_lo = sem("sig_ready"), sem("gated"), sem("merged"), sem("m_hi"), sem("m_lo")
        x_new = sem("x_new")
        up_done, down_done, silu_done, f_ready, f_hi, f_lo = (sem("up_done"), sem("down_done"), sem("silu_done"),
                                                             sem("f_ready"), sem("f_hi"), sem("f_lo"))
        d_hi, d_lo, up_hi, up_lo = sem("d_hi"), sem("d_lo"), sem("up_hi"), sem("up_lo")

        block = ctx.enter_context(nc.Block())

        x_dram = x.rearrange("b (t p) d -> p (b t) d", p=P)
        out_dram = out.rearrange("b (t p) d -> p (b t) d", p=P)
        ada_dram = w_ada.rearrange("l (p k) n -> p (l k) n", k=KC)
        in_dram = w_in.rearrange("l (k p) n -> p (l k) n", p=P)
        up_dram = w_up.rearrange("l (k p) n -> p (l k) n", p=P)
        down_dram = w_down.rearrange("l (k p) n -> p (l k) n", p=P)
        wo_dram = w_o.rearrange("l (k p) n -> p (l k) n", p=P)

        def turned(c):
            return bank[c // 2][:, S * (c % 2):S * (c % 2 + 1)]

        def block_view(buf, b):
            if b < N_MIX:
                n = MIX_BLOCKS[b][1]
                return buf[:, 0:KC * n].rearrange("p (k n) -> p k n", n=n)
            if b < B_WO:
                return buf[:, 0:N_OCH * PROJ_COLS].rearrange("p (k n) -> p k n", n=PROJ_COLS)
            if b < B_FFN:
                return buf[:, :].rearrange("p (k n) -> p k n", n=D)
            return buf[:, :].rearrange("p (k n) -> p k n", n=BANK)

        def block_parts(b):
            if b < N_MIX or b >= B_FFN:
                return [(P, 2 * q, 2 * q + 2) for q in range(4)]
            if b < B_WO:
                return [(P, 0, 3), (P, 3, 5), (P, 5, FULL_OCH), (HD, FULL_OCH, N_OCH)]
            return [(P, q, q + 1) for q in range(4)]

        def hold(b):
            return BLOCK_DONE[b - 2] if b >= 2 else 0

        @block.sync
        def _(sp):
            sp.dma_start(ccol[:, :], c.rearrange("b (p k) -> p (b k)", k=KC)).then_inc(c_in, 16)
            for t in range(TT):
                sp.dma_start(xt[:, t, :], x_dram[:, t, :]).then_inc(x_in, 16)

            def load(r):
                kind, b, u = RAW[r]
                dst, arrived = raw[r % 2], raw_in[r % 2]
                if r >= 2:
                    before, b0, u0 = RAW[r - 2]
                    if before == "ada":
                        sp.wait_ge(gemv, u0 + 1)
                    else:
                        sp.wait_ge(w_hi, 4 * (b0 + 1))
                        sp.wait_ge(w_lo, 4 * (b0 + 1))
                if kind == "ada":
                    sp.dma_start(dst[:, :].rearrange("p (k n) -> p k n", k=2),
                                 ada_dram[:, 2 * u:2 * u + 2, 4 * BANK * b:4 * BANK * (b + 1)]).then_inc(arrived, 16)
                elif b < N_MIX:
                    c0, n = MIX_BLOCKS[b]
                    sp.dma_start(block_view(dst, b), in_dram[:, :, c0:c0 + n]).then_inc(arrived, 16)
                elif b < B_WO:
                    c0 = PROJ_COLS * (b - B_PROJ)
                    view = block_view(dst, b)
                    cols = slice(c0, c0 + PROJ_COLS)
                    for w, k0, n, last in ((w_proj_sb, 0, 3, None), (w_proj_moba, 3, 2, 7), (w_proj_dsa, 5, 2, 8)):
                        sp.dma_start(view[:, k0:k0 + n, :],
                                     w[0, 0:n * P, cols].rearrange("(k p) n -> p k n", p=P)).then_inc(arrived, 16)
                        if last is not None:
                            sp.dma_start(view[0:HD, last, :], w[0, n * P:n * P + HD, cols]).then_inc(arrived, 16)
                else:
                    k0 = 4 * (b - B_WO)
                    sp.dma_start(block_view(dst, b), wo_dram[:, k0:k0 + 4, :]).then_inc(arrived, 16)

            def load_rows(g):
                if g == 0:
                    sp.wait_ge(rows_set, 2)
                else:
                    sp.wait_ge(m_ready, g)
                sp.dma_start(brow[0:P:32, :], b_ada[0, 4 * BANK * g:4 * BANK * (g + 1)].rearrange("(j n) -> j n", n=BANK)).then_inc(rows_in, 16)
                for w, j in GAIN_ROWS[g]:
                    sp.dma_start(grow[32 * j:32 * j + 33:32, :], w.rearrange("l (j n) -> (l j) n", j=2)).then_inc(rows_in, 16)

            GAIN_ROWS = [[(g_pre_mix, 2)], [(g_post_mix, 0)], [(g_pre_ffn, 0), (g_post_ffn, 2)]]
            sp.dma_start(bgr[:, :], b_gate.rearrange("l (k p) -> (l k) p", p=P)).then_inc(bg_in, 16)
            load(0)
            load(1)
            for i in range(2):
                for kk in range(2):
                    k = 4 + 2 * i + kk
                    sp.dma_start(ada_end[i][:, 4 * BANK * kk:4 * BANK * (kk + 1)], ada_dram[:, k, 0:4 * BANK]).then_inc(ada_in[2 * i + kk], 16)
            load_rows(0)
            for r in range(2, N_RAW):
                load(r)
                if RAW[r][1] in ROWS_LOAD_AFTER:
                    load_rows(ROWS_LOAD_AFTER[RAW[r][1]])

            def load_step(i, slot, first, third=False):
                view = block_view(raw[slot], B_FFN).rearrange("p k (a n) -> p k a n", a=2)
                if first:
                    sp.wait_ge(w_hi, 4 * (B_WO + 1 + i))
                    sp.wait_ge(w_lo, 4 * (B_WO + 1 + i))
                elif third:
                    sp.wait_ge(up_done, 2)
                else:
                    sp.wait_ge(up_hi, 4 * (i - 2))
                    sp.wait_ge(up_lo, 4 * (i - 2))
                for a in range(2):
                    sp.dma_start(view[:, :, a, :], up_dram[:, :, bass.ds(i * FSTEP + FF * a, FSTEP)]).then_inc(raw_in[slot], 16)
                if first:
                    sp.wait_ge(units, BLOCK_DONE[B_WO - 1])
                    sp.wait_ge(merged, KC)
                else:
                    sp.wait_ge(d_hi, i - 1)
                    sp.wait_ge(d_lo, i - 1)
                sp.dma_start(draw[slot][:, :, :], down_dram[:, bass.ds(2 * i, 2), :]).then_inc(down_in[slot], 16)

            load_step(0, 1, True)
            load_step(1, 0, True)
            load_step(2, 1, False, True)
            with sp.Fori(3, N_FFN - 1, 2) as i:
                load_step(i, 0, False)
                load_step(i + 1, 1, False)

            for t in range(TT):
                for n in range(2):
                    cols = slice(BANK * n, BANK * (n + 1))
                    sp.wait_ge(x_new, 4 + 2 * t + n + 1)
                    sp.dma_start(out_dram[:, t, cols], xt[:, t, cols]).then_inc(stored, 16)
            sp.wait_ge(stored, 16 * 2 * TT)

        @block.gpsimd
        def _(pool):
            pool.memset(brow[:, :], 0.0).then_inc(rows_set, 1)
            pool.memset(grow[:, :], 1.0).then_inc(rows_set, 1)
            pool.memset(ident[:, :], 0.0).then_inc(consts, 1)
            pool.memset(tri[:, :], -1.0).then_inc(consts, 1)
            pool.memset(neg1[:, :], -1.0).then_inc(consts, 1)
            pool.iota(bufa[0][:, 0:P].bitcast(mybir.dt.int32), pattern=[[1, P]], base=0, channel_multiplier=-1).then_inc(consts, 1)
            pool.iota(bufa[0][:, P:CAUSAL].bitcast(mybir.dt.int32), pattern=[[1, 2 * P]], base=-P, channel_multiplier=-1).then_inc(consts, 1)
            pool.wait_ge(consts, 5)
            pool.affine_select(out=ident[:, :], in_=ident[:, :], compare_op=ALU.not_equal, fill=1.0,
                               base=0, pattern=[[-1, P]], channel_multiplier=1).then_inc(consts, 1)
            pool.affine_select(out=tri[:, :], in_=tri[:, :], compare_op=ALU.is_ge, fill=0.0,
                               base=0, pattern=[[-1, P]], channel_multiplier=1).then_inc(consts, 1)
            pool.tensor_copy(dist[:, :], bufa[0][:, :].bitcast(mybir.dt.int32)).then_inc(consts, 1)
            pool.wait_ge(consts, 8)
            for c0 in (0, 2 * P):
                pool.affine_select(out=dist[:, c0:c0 + P], in_=dist[:, c0:c0 + P], compare_op=ALU.is_ge, fill=MASKED,
                                   base=0, pattern=[[-1, P]], channel_multiplier=1).then_inc(consts, 1)

            for u in range(N_UNITS):
                if u in ADA_LOAD_AT:
                    n = ADA_LOAD_AT[u]
                    if n == 0:
                        pool.wait_ge(h_lo, 4)
                    else:
                        pool.wait_ge(gemv, 4 + n)
                    pool.dma_start(ada_part, ada_dram[:, n % KC, 4 * BANK * (1 + n // KC):4 * BANK * (2 + n // KC)]).then_inc(part_in, 16)
                if u == LOGITS_LAST:
                    pool.wait_ge(score_added, TT * H_IX)
                    for c0 in (0, 2 * P):
                        pool.affine_select(out=score[:, c0:c0 + P], in_=score[:, c0:c0 + P], compare_op=ALU.is_ge, fill=MASKED,
                                           base=0, pattern=[[-1, P]], channel_multiplier=1).then_inc(score_masked, 1)
                if u in SECOND_AT and SECOND_AT[u] in SB_NO:
                    i = SB_NO[SECOND_AT[u]]
                    n = SECOND_AT[u]
                    pool.wait_ge(a_ready, i + 1)
                    for c0 in (0, 2 * P):
                        pool.affine_select(out=buft[n % 2][:, c0:c0 + P], in_=buft[n % 2][:, c0:c0 + P], compare_op=ALU.is_gt, fill=0.0,
                                           base=0, pattern=[[1, P]], channel_multiplier=-1).then_inc(a_masked, 1)
                if u in EXP_AT and EXP_AT[u] in SB_NO:
                    n = EXP_AT[u]
                    i = SB_NO[n]
                    pool.wait_ge(sp_ready, i + 1)
                    for c0 in (0, 2 * P):
                        pool.affine_select(out=bufp[n % 2][:, c0:c0 + P], in_=bufp[n % 2][:, c0:c0 + P], compare_op=ALU.is_gt, fill=0.0,
                                           base=0, pattern=[[1, P]], channel_multiplier=-1).then_inc(sp_masked, 1)

            for f in range(KC):
                g = gp[f % 2]
                pool.wait_ge(gated, 3 * f + 2)
                pool.tensor_tensor(g[0], g[0], g[1], ALU.add).then_inc(pool_step, 1)
                pool.wait_ge(gated, 3 * (f + 1))
                pool.wait_ge(pool_step, f + 1)
                pool.tensor_tensor(h32[:, f, :], g[0], g[2], ALU.add).then_inc(merged, 1)

        @block.scalar
        def _(act):
            steps = [0]

            def then(ins):
                steps[0] += 1
                ins.then_inc(act_step, 1)
                act.wait_ge(act_step, steps[0])

            def cut_hi(b, q):
                if q == 0:
                    r = RAW_OF_BLOCK[b]
                    act.wait_ge(raw_in[r % 2], RAW_ARRIVED[r])
                    if b >= 2:
                        act.wait_ge(units, hold(b))
                r = RAW_OF_BLOCK[b]
                p, k0, k1 = block_parts(b)[q]
                act.activation(block_view(whi[b % 2], b)[0:p, k0:k1, :], block_view(raw[r % 2], b)[0:p, k0:k1, :],
                               ACT.Copy).then_inc(w_hi, 1)

            def square_sum(j, n, src, squares):
                act.activation(squares, src, ACT.Square, accum_out=ssq[:, j, n:n + 1]).then_inc(ss_ready, 1)

            def root(j):
                act.wait_ge(var_ready, j + 1)
                act.activation(root_[:, j:j + 1], var[:, j:j + 1], ACT.Sqrt).then_inc(sqrt_ready, 1)

            def load_roots():
                act.activation(warm[:, :], crep[:, 0, 0:1], ACT.Sqrt, scale=0.0, bias=1.0)

            def modulate(t):
                j = TT + t
                act.wait_ge(x_turned, 2 * j + 1)
                act.wait_ge(col_ready, 3)
                for c in range(4):
                    ins = act.activation(hx[:, t, c, :], bank[B_TURNED[t]][:, P * c:P * (c + 1)], ACT.Identity,
                                         bias=col[1][:, 8 + c:9 + c], scale=col[2][:, c:c + 1])
                ins.then_inc(h_act, 1)

            def cut_h(t):
                j, tokens = TT + t, slice(P * t, P * (t + 1))
                for half, ready in enumerate((h_act, h_dve)):
                    act.wait_ge(ready, j + 1)
                    act.activation(hhi[:, 4 * half:4 * half + 4, tokens], hx[:, t, 4 * half:4 * half + 4, :],
                                   ACT.Copy).then_inc(h_hi, 1)

            def take_unit(u):
                b, what, c0, n, dest = UNITS[u]
                src = bank[B_UNIT + u % 2]
                act.wait_ge(units, u + 1)
                if what == "index keys and weights":
                    act.activation(qk[0:HD, dest, :], src[0:HD, 0:S], ACT.Copy)
                    act.activation(qk[HD:2 * HD, dest, :], src[0:HD, 0:S], ACT.Copy)
                    ins = act.activation(wixt[HD:n, :], src[HD:n, 0:S], ACT.Copy)
                elif what == "features":
                    scale = SCALE if T_QSB <= dest < T_KSB else 1.0
                    ins = act.activation(qk[0:n, dest, :], src[0:n, 0:S], ACT.Copy, scale=scale)
                elif what == "values":
                    ins = act.activation(v[:, dest[0], dest[1]:dest[1] + n], src[:, 0:n], ACT.Copy)
                else:
                    if u == FIRST_GATE:
                        act.wait_ge(bg_ready, 1)
                    ins = act.activation(gates[:, dest, :], src[:, 0:S], ACT.Sigmoid if u >= SIGMOID_FROM else ACT.Identity,
                                         bias=bgc[:, dest:dest + 1])
                ins.then_inc(unit_read, 1)

            act.wait_ge(c_in, 16)
            act.activation(csil[:, :], ccol[:, :], ACT.Silu).then_inc(c_ready, 1)
            act.wait_ge(c_ready, 2)
            load_roots()
            act.wait_ge(x_in, 16 * TT)
            for t in range(TT):
                for n in range(2):
                    cols = slice(BANK * n, BANK * (n + 1))
                    square_sum(t, n, xt[:, t, cols], xn[:, t, cols])
            for t in range(TT):
                root(t)
            act.preload_act_table_set("natural_log_exp_and_others")
            for q in range(4):
                cut_hi(0, q)

            act.wait_ge(x_turned, 2 * TT)
            act.wait_ge(col_ready, 1)
            for pair in range(4):
                if pair % 2 == 0:
                    for c in (2 * pair, 2 * pair + 1):
                        ins = act.activation(h32[:, c, :], turned(c), ACT.Identity, bias=col[0][:, c:c + 1],
                                             scale=col[0][:, 8 + c:9 + c])
                    ins.then_inc(h_act, 1)
                act.wait_ge(h_dve if pair % 2 else h_act, pair // 2 + 1)
                act.activation(hhi[:, 2 * pair:2 * pair + 2, :], h32[:, 2 * pair:2 * pair + 2, :], ACT.Copy).then_inc(h_hi, 1)

            for u in range(N_UNITS):
                for b, q in PIECES_AT.get(u, []):
                    cut_hi(b, q)
                take_unit(u)
                if u in LOGITS_AT:
                    h = LOGITS_AT[u]
                    act.wait_ge(logits, h + 1)
                    if h >= 2:
                        act.wait_ge(score_added, TT * (h - 1))
                    act.activation(bufp[h % 2][:, :], bank[B_Z + h % 3][:, 0:CAUSAL], ACT.Relu).then_inc(relu_ready, 1)
                if u in EXP_AT and EXP_AT[u] in SOFT_NO:
                    n = EXP_AT[u]
                    branch, h = HEADS[n][0:2]
                    act.wait_ge(max_ready, SOFT_NO[n] + 1)
                    if n >= 2:
                        if n - 2 in SB_NO:
                            act.wait_ge(sums, SB_NO[n - 2] + 1)
                        else:
                            act.wait_ge(p_turned, SOFT_NO[n - 2] + 1)
                    for t, (c0, c1) in enumerate(((0, P), (P, CAUSAL))):
                        ins = act.activation(bufp[n % 2][:, c0:c1], bufa[n % 2][:, c0:c1], ACT.Exp,
                                             scale=SLOPES[2 * h + (branch == "ds")],
                                             bias=smax[:, n % 2, t:t + 1], accum_out=ssum[:, n % 2, t:t + 1])
                    ins.then_inc(exp_ready, 1)
                if u in OUTPUT_AT:
                    n = OUTPUT_AT[u]
                    p0, ch = HD * (HEADS[n][1] % 2), O_CHUNK[HEADS[n][0]][HEADS[n][1]]
                    act.wait_ge(o_ready, n + 1)
                    act.activation(ohi[p0:p0 + HD, ch, :], bank[B_O + n % 2][p0:p0 + HD, 0:S], ACT.Copy).then_inc(o_hi, 1)
                if u in SECOND_AT:
                    n = SECOND_AT[u]
                    if n >= 2:
                        act.wait_ge(o_ready, n - 1)
                    if n in SB_NO:
                        act.wait_ge(sums, SB_NO[n] + 1)
                        act.activation(buft[n % 2][:, :], bank[B_Z + n % 2][:, 0:CAUSAL], ACT.Exp).then_inc(a_ready, 1)
                    else:
                        act.wait_ge(p_turned, SOFT_NO[n] + 1)
                        act.activation(buft[n % 2][:, :], bank[B_T][:, 0:CAUSAL], ACT.Copy).then_inc(pt_ready, 1)
                if u in SCORES_AT and SCORES_AT[u] in SB_NO:
                    n = SCORES_AT[u]
                    act.wait_ge(z_ready, n + 1)
                    if SB_NO[n] == 0:
                        act.wait_ge(p_turned, softs_before(n))
                    z = bank[B_Z + n % 2][:, 0:CAUSAL]
                    e = bufa[n % 2][:, :]
                    if n >= 2:
                        act.wait_ge(sp_ready if n - 2 in SB_NO else p_ready, (SB_NO[n - 2] + 1) if n - 2 in SB_NO else SOFT_NO[n - 2] + 1)
                    then(act.activation(e, z, ACT.Abs))
                    then(act.activation(e, e, ACT.Exp, scale=-1.0))
                    act.activation(e, e, ACT.Ln, bias=1.0).then_inc(ln_ready, 1)
                if SIGMOID_FROM <= u < SIGMOID_FROM + SIGMOID_BATCHES:
                    i = u - SIGMOID_FROM
                    if i == 0:
                        act.wait_ge(unit_read, SIGMOID_FROM)
                    tiles = slice(EARLY_GATES * i // SIGMOID_BATCHES, EARLY_GATES * (i + 1) // SIGMOID_BATCHES)
                    act.activation(gates[:, tiles, :], gates[:, tiles, :], ACT.Sigmoid).then_inc(sig_ready, 1)

            def spread_rows(g):
                for n in range(2):
                    act.wait_ge(m_spread, 2 * (g - 1) + n + 1)
                    act.activation(gb[g][:, BANK * n:BANK * (n + 1)], bank[6 + n][:, :], ACT.Copy).then_inc(gb_ready, 1)

            for f in range(KC):
                for b, q in MERGE_PIECES[f]:
                    cut_hi(B_PROJ + b, q)
                act.wait_ge(merged, f + 1)
                act.wait_ge(units, N_UNITS)
                act.activation(hhi[:, f, :], h32[:, f, :], ACT.Copy).then_inc(m_hi, 1)
                if f in SPREAD_AT:
                    spread_rows(SPREAD_AT[f])
            for q in range(2, 4):
                cut_hi(B_WO + 1, q)
            load_roots()

            def cut_up_hi(i, slot, q, first=False):
                if q == 0:
                    act.wait_ge(raw_in[slot], RAW_COUNT[slot] + 16 * (i + 1 + slot))
                    if first:
                        act.wait_ge(units, BLOCK_DONE[B_WO + 1])
                    else:
                        act.wait_ge(up_done, 2 * (i - 1))
                act.activation(block_view(whi[slot], B_FFN)[:, 2 * q:2 * q + 2, :],
                               block_view(raw[slot], B_FFN)[:, 2 * q:2 * q + 2, :], ACT.Copy).then_inc(up_hi, 1)

            def cut_down_hi(i, slot, first=False):
                act.wait_ge(down_in[slot], 8 * (i + 1 + slot))
                if not first:
                    act.wait_ge(down_done, i - 1)
                act.activation(dhi[slot][:, :, :], draw[slot][:, :, :], ACT.Copy).then_inc(d_hi, 1)

            def norm_y(k, t):
                j = 2 + 2 * t if k == 0 else 6 + t
                for n in range(2):
                    if k == 0:
                        act.wait_ge(units, y_done(t, n))
                    else:
                        act.wait_ge(down_done, N_FFN - 2 + 2 * t + n + 1)
                    square_sum(j, n, bank[B_Y[k][t] + n][:, :], squares[n])
                    if k == 0 and t == 1 and n == 0:
                        modulate(0)
                root(j)

            def norm_new_x(t):
                for n in range(2):
                    act.wait_ge(x_new, 2 * t + n + 1)
                    square_sum(3 + 2 * t, n, xt[:, t, BANK * n:BANK * (n + 1)], squares[n])
                root(3 + 2 * t)

            squares = [f[:, :, :].rearrange("p j n -> p (j n)") for f in fsil]
            norm_y(0, 0)
            norm_new_x(0)
            norm_y(0, 1)
            norm_new_x(1)
            modulate(1)
            for t in range(TT):
                cut_h(t)

            def silu_tile(i, slot, j):
                act.wait_ge(up_done, 2 * i + j + 1)
                act.activation(fsil[slot][:, j, :], bank[2 * (1 - slot) + j][:, 0:S], ACT.Silu).then_inc(silu_done, 1)

            def f_part(i, slot, j):
                act.wait_ge(f_ready, 2 * i + j + 1)
                act.activation(fhi[slot][:, j, :], fsil[slot][:, j, :], ACT.Copy).then_inc(f_hi, 1)

            def step(i, slot, first, last):
                if not last:
                    for q in range(2):
                        cut_up_hi(i + 1, 1 - slot, q, first)
                silu_tile(i, slot, 0)
                if not last:
                    for q in range(2, 4):
                        cut_up_hi(i + 1, 1 - slot, q, first)
                f_part(i, slot, 0)
                silu_tile(i, slot, 1)
                if first:
                    cut_down_hi(0, 1, True)
                if not last:
                    cut_down_hi(i + 1, 1 - slot, first)
                f_part(i, slot, 1)

            step(0, 1, True, False)
            with act.Fori(1, N_FFN - 2, 2) as i:
                step(i, 0, False, False)
                step(i + 1, 1, False, False)
            step(N_FFN - 2, 0, False, False)
            step(N_FFN - 1, 1, False, True)
            load_roots()
            for t in range(TT):
                norm_y(1, t)

        @block.vector
        def _(dve):
            steps = [0]

            def then(ins):
                steps[0] += 1
                ins.then_inc(dve_step, 1)
                dve.wait_ge(dve_step, steps[0])

            def cut_lo(b, q):
                dve.wait_ge(w_hi, 4 * b + q + 1)
                r = RAW_OF_BLOCK[b]
                p, k0, k1 = block_parts(b)[q]
                dve.tensor_tensor(block_view(wlo[b % 2], b)[0:p, k0:k1, :], block_view(raw[r % 2], b)[0:p, k0:k1, :],
                                  block_view(whi[b % 2], b)[0:p, k0:k1, :].bitcast(F32), ALU.subtract).then_inc(w_lo, 1)

            def inverse_root(j, meanwhile=lambda: None):
                v, r, t = var[:, j:j + 1], rinv[:, j:j + 1], root_[:, j:j + 1]
                dve.wait_ge(ss_ready, 2 * j + 1)
                then(dve.tensor_scalar(v, ssq[:, j, 0:1], 1.0 / D, EPS, ALU.mult, ALU.add))
                dve.wait_ge(ss_ready, 2 * j + 2)
                dve.scalar_tensor_tensor(v, ssq[:, j, 1:2], 1.0 / D, v, ALU.mult, ALU.add).then_inc(var_ready, 1)
                meanwhile()
                dve.wait_ge(sqrt_ready, j + 1)
                then(dve.reciprocal(r, t))
                then(dve.tensor_scalar(t, v, r, r, ALU.mult, ALU.mult))
                then(dve.tensor_scalar(t, t, -0.5, 1.5, ALU.mult, ALU.add))
                then(dve.tensor_scalar(r, r, t, None, ALU.mult))

            def spread_root(j, t):
                dve.tensor_scalar(diag[t], ident[:, :], rinv[:, j:j + 1], None, ALU.mult).then_inc(xn_ready, 1)

            def modulate(t):
                j = TT + t
                dve.wait_ge(x_turned, 2 * j + 2)
                for c in range(4, 8):
                    ins = dve.tensor_scalar(hx[:, t, c, :], bank[B_TURNED[t] + 1][:, P * (c - 4):P * (c - 3)], col[2][:, c:c + 1],
                                            col[1][:, 8 + c:9 + c], ALU.mult, ALU.add)
                ins.then_inc(h_dve, 1)

            def cut_h(t):
                j, tokens = TT + t, slice(P * t, P * (t + 1))
                for half in range(2):
                    dve.wait_ge(h_hi, 2 * j + half + 1)
                    dve.tensor_tensor(hlo[:, 4 * half:4 * half + 4, tokens], hx[:, t, 4 * half:4 * half + 4, :],
                                      hhi[:, 4 * half:4 * half + 4, tokens].bitcast(F32), ALU.subtract).then_inc(h_lo, 1)

            def rows(g):
                dve.wait_ge(gemv, GEMV_DONE[g])
                dve.wait_ge(rows_in, (32, 64, 112)[g])
                m = mrow[:, g % 2, :]
                then(dve.tensor_tensor(m, bank[B_ADA][:, :], brow[:, :], ALU.add))
                lo, hi = mrow[0:HD, g % 2, :], mrow[HD:P, g % 2, :]
                if g == 0:
                    ins = dve.scalar_tensor_tensor(hi, hi, 1.0, grow[HD:P, :], ALU.add, ALU.mult)
                elif g == 1:
                    ins = dve.tensor_tensor(lo, lo, grow[0:HD, :], ALU.mult)
                else:
                    dve.scalar_tensor_tensor(lo, lo, 1.0, grow[0:HD, :], ALU.add, ALU.mult)
                    ins = dve.tensor_tensor(hi, hi, grow[HD:P, :], ALU.mult)
                then(ins)
                dve.sem_inc(m_ready, 1)

            def columns(g):
                dve.wait_ge(m_turned, g + 1)
                then(dve.tensor_copy(col[g][:, :].rearrange("p (j c) -> p j c", j=4),
                                     bank[B_ROWS[g]][:, :].rearrange("p (c j r) -> p j c r", c=4, j=4)[:, :, :, 0]))
                dve.sem_inc(col_ready, 1)

            then(dve.memset(select[:, :, :], 0.0))
            for j in range(4):
                ins = dve.memset(select[32 * j:32 * j + 1, j, :], 1.0)
            then(ins)
            dve.wait_ge(c_ready, 1)
            dve.tensor_copy(crep[:, :, :], csil[:, :, None].to_broadcast([P, KC, 32])).then_inc(c_ready, 1)
            for t in range(TT):
                inverse_root(t)
            dve.wait_ge(consts, 7)
            for t in range(TT):
                spread_root(t, t)
            dve.wait_ge(bg_turned, 1)
            dve.tensor_copy(bgc[:, :], bank[4][:, 0:3 * KC]).then_inc(bg_ready, 1)
            rows(0)
            for q in range(4):
                cut_lo(0, q)
            columns(0)

            dve.wait_ge(x_turned, 2 * TT)
            for pair in range(4):
                if pair % 2 == 0:
                    for c in (2 * pair + 2, 2 * pair + 3):
                        ins = dve.tensor_scalar(h32[:, c, :], turned(c), col[0][:, 8 + c:9 + c], col[0][:, c:c + 1],
                                                ALU.mult, ALU.add)
                    ins.then_inc(h_dve, 1)
                dve.wait_ge(h_hi, pair + 1)
                dve.tensor_tensor(hlo[:, 2 * pair:2 * pair + 2, :], h32[:, 2 * pair:2 * pair + 2, :],
                                  hhi[:, 2 * pair:2 * pair + 2, :].bitcast(F32), ALU.subtract).then_inc(h_lo, 1)

            def reach(n):
                return dsel if HEADS[n][0] == "ds" else dist

            for u in range(N_UNITS):
                for b, q in PIECES_AT.get(u, []):
                    cut_lo(b, q)
                if u == 3:
                    dve.wait_ge(wix_turned, 1)
                    then(dve.tensor_copy(wix[:, :, :], bank[B_ADA][:, 0:TT * H_IX].rearrange("p (t h) -> p t h", t=TT)))
                    dve.sem_inc(wix_ready, 1)
                if u in LOGITS_AT:
                    h = LOGITS_AT[u]
                    dve.wait_ge(relu_ready, h + 1)
                    if h:
                        dve.wait_ge(score_added, TT * h)
                    for t, (c0, c1) in enumerate(((0, P), (P, CAUSAL))):
                        w = wix[:, t, h:h + 1]
                        if h == 0:
                            ins = dve.tensor_scalar(score[:, c0:c1], bufp[0][:, c0:c1], w, 0.0, ALU.mult, ALU.add)
                        else:
                            ins = dve.scalar_tensor_tensor(score[:, c0:c1], bufp[h % 2][:, c0:c1], w, score[:, c0:c1],
                                                           ALU.mult, ALU.add)
                        ins.then_inc(score_added, 1)
                if u in OUTPUT_AT:
                    n = OUTPUT_AT[u]
                    p0, ch = HD * (HEADS[n][1] % 2), O_CHUNK[HEADS[n][0]][HEADS[n][1]]
                    dve.wait_ge(o_hi, n + 1)
                    dve.tensor_tensor(olo[p0:p0 + HD, ch, :], bank[B_O + n % 2][p0:p0 + HD, 0:S],
                                      ohi[p0:p0 + HD, ch, :].bitcast(F32), ALU.subtract).then_inc(o_lo, 1)
                if u in NORM_AT and NORM_AT[u] in SOFT_NO:
                    n = NORM_AT[u]
                    i = SOFT_NO[n]
                    dve.wait_ge(exp_ready, i + 1)
                    then(dve.reciprocal(ssum[:, n % 2, :], ssum[:, n % 2, :]))
                    for t, (c0, c1) in enumerate(((0, P), (P, CAUSAL))):
                        ins = dve.tensor_scalar(bufp[n % 2][:, c0:c1], bufp[n % 2][:, c0:c1], ssum[:, n % 2, t:t + 1], None, ALU.mult)
                    ins.then_inc(p_ready, 1)
                if u in EXP_AT and EXP_AT[u] in SB_NO:
                    n = EXP_AT[u]
                    z = bank[B_Z + n % 2][:, 0:CAUSAL]
                    i = SB_NO[n]
                    dve.wait_ge(ln_ready, i + 1)
                    if n >= 2:
                        if n - 2 in SB_NO:
                            dve.wait_ge(sums, SB_NO[n - 2] + 1)
                        else:
                            dve.wait_ge(p_turned, SOFT_NO[n - 2] + 1)
                    dve.scalar_tensor_tensor(bufp[n % 2][:, :], z, 0.0, bufa[n % 2][:, :], ALU.max, ALU.add).then_inc(sp_ready, 1)
                if u in SCORES_AT and SCORES_AT[u] in SOFT_NO:
                    n = SCORES_AT[u]
                    branch, h = HEADS[n][0:2]
                    z = bank[B_Z + n % 2][:, 0:CAUSAL]
                    i = SOFT_NO[n]
                    slope = SLOPES[2 * h + (branch == "ds")]
                    dve.wait_ge(z_ready, n + 1)
                    if n == 0:
                        dve.wait_ge(consts, 10)
                    then(dve.scalar_tensor_tensor(bufa[n % 2][:, :], z, SCALE / slope, reach(n)[:, :], ALU.mult, ALU.add))
                    for t, (c0, c1) in enumerate(((0, P), (P, CAUSAL))):
                        ins = dve.reduce_max(smax[:, n % 2, t:t + 1], bufa[n % 2][:, c0:c1], AX_X)
                    then(ins)
                    dve.tensor_scalar(smax[:, n % 2, :], smax[:, n % 2, :], -slope, None, ALU.mult).then_inc(max_ready, 1)

                if u in ROUND_AT:
                    r = ROUND_AT[u]
                    src = score if r == 0 else work
                    if r == 0:
                        dve.wait_ge(score_masked, 2)
                    halves = ((0, 0, P), (1, P, CAUSAL))
                    for t, c0, c1 in halves:
                        ins = dve.max(top8[:, t, :], src[:, c0:c1])
                    then(ins)
                    for t, c0, c1 in halves:
                        ins = dve.match_replace(work[:, c0:c1], top8[:, t, :], src[:, c0:c1], TAKEN)
                    then(ins)
                    if r == TOPK_ROUNDS - 1:
                        then(dve.tensor_tensor(work[:, :], work[:, :], score[:, :], ALU.not_equal))
                        then(dve.tensor_scalar(work[:, :], work[:, :], -MASKED, MASKED, ALU.mult, ALU.add))
                        dve.wait_ge(consts, 10)
                        then(dve.tensor_tensor(dsel[:, :], work[:, :], dist[:, :], ALU.add))
                if u in ROWS_AT:
                    rows(ROWS_AT[u])
                if u in COLUMNS_AT:
                    columns(COLUMNS_AT[u])

            def merge_tile(f):
                if f == 0:
                    dve.wait_ge(sig_ready, SIGMOID_BATCHES)
                    dve.wait_ge(unit_read, N_UNITS)
                dve.wait_ge(units, N_UNITS + f + 1)
                if f >= 2:
                    dve.wait_ge(merged, f - 1)
                for br in range(3):
                    dve.tensor_tensor(gp[f % 2][br], bank[2 * br + 1 - f % 2][:, 0:S], gates[:, KC * br + f, :], ALU.mult).then_inc(gated, 1)

            def merge_lo(f):
                dve.wait_ge(m_hi, f + 1)
                dve.tensor_tensor(hlo[:, f, :], h32[:, f, :], hhi[:, f, :].bitcast(F32), ALU.subtract).then_inc(m_lo, 1)

            for f in range(KC):
                if f:
                    merge_tile(f)
                    merge_lo(f - 1)
                for b, q in MERGE_PIECES[f]:
                    cut_lo(B_PROJ + b, q)
                if f == 0:
                    merge_tile(0)
            merge_lo(KC - 1)
            for q in range(2, 4):
                cut_lo(B_WO + 1, q)

            def add_residual(k, t):
                j = 2 + 2 * t if k == 0 else 6 + t
                halves = [slice(BANK * n, BANK * (n + 1)) for n in range(2)]

                def gain(n):
                    dve.wait_ge(ss_ready, 2 * j + n + 1)
                    ins = dve.tensor_tensor(xn[:, t, halves[n]], bank[B_Y[k][t] + n][:, :], gb[k + 1][:, halves[n]], ALU.mult)
                    ins.then_inc(dve_scaled, 1)

                if t == 0:
                    dve.wait_ge(gb_ready, 2 * (k + 1))
                gain(0)
                if k == 0 and t == 1:
                    modulate(0)
                inverse_root(j, lambda: gain(1))
                for n in range(2):
                    dve.wait_ge(dve_scaled, 2 * (2 * k + t) + n + 1)
                    dve.scalar_tensor_tensor(xt[:, t, halves[n]], xn[:, t, halves[n]], rinv[:, j:j + 1], xt[:, t, halves[n]],
                                             ALU.mult, ALU.add).then_inc(x_new, 1)

            def cut_up_lo(i, slot, q):
                dve.wait_ge(up_hi, 4 * (i - 1) + q + 1)
                dve.tensor_tensor(block_view(wlo[slot], B_FFN)[:, 2 * q:2 * q + 2, :], block_view(raw[slot], B_FFN)[:, 2 * q:2 * q + 2, :],
                                  block_view(whi[slot], B_FFN)[:, 2 * q:2 * q + 2, :].bitcast(F32), ALU.subtract).then_inc(up_lo, 1)

            def cut_down_lo(i, slot):
                dve.wait_ge(d_hi, i + 1)
                dve.tensor_tensor(dlo[slot][:, :, :], draw[slot][:, :, :], dhi[slot][:, :, :].bitcast(F32), ALU.subtract).then_inc(d_lo, 1)

            for t in range(TT):
                add_residual(0, t)
                inverse_root(3 + 2 * t)
                spread_root(3 + 2 * t, t)
            modulate(TT - 1)
            for t in range(TT):
                cut_h(t)

            def f_tile(i, slot, j):
                dve.wait_ge(silu_done, 2 * i + j + 1)
                dve.tensor_tensor(fsil[slot][:, j, :], bank[2 * (1 - slot) + j][:, S:2 * S], fsil[slot][:, j, :], ALU.mult).then_inc(f_ready, 1)

            def f_rest(i, slot, j):
                dve.wait_ge(f_hi, 2 * i + j + 1)
                dve.tensor_tensor(flo[slot][:, j, :], fsil[slot][:, j, :], fhi[slot][:, j, :].bitcast(F32), ALU.subtract).then_inc(f_lo, 1)

            def step(i, slot, last, first=False):
                if not last:
                    for q in range(2):
                        cut_up_lo(i + 1, 1 - slot, q)
                f_tile(i, slot, 0)
                if not last:
                    for q in range(2, 4):
                        cut_up_lo(i + 1, 1 - slot, q)
                f_rest(i, slot, 0)
                f_tile(i, slot, 1)
                if first:
                    cut_down_lo(0, 1)
                if not last:
                    cut_down_lo(i + 1, 1 - slot)
                f_rest(i, slot, 1)

            step(0, 1, False, True)
            with dve.Fori(1, N_FFN - 2, 2) as i:
                step(i, 0, False)
                step(i + 1, 1, False)
            step(N_FFN - 2, 0, False)
            step(N_FFN - 1, 1, True)
            for t in range(TT):
                add_residual(1, t)

        @block.tensor
        def _(pe):
            def three(dst, a, b, first, last):
                pe.matmul(dst, a[0], b[0], start=first, stop=False)
                pe.matmul(dst, a[0], b[1], start=False, stop=False)
                return pe.matmul(dst, a[1], b[0], start=False, stop=last)

            def product(k, w):
                for j in range(4):
                    mm = pe.matmul(bank[B_ADA][32 * j:32 * j + 32, :], crep[:, k, :], w[:, BANK * j:BANK * (j + 1)],
                                   start=k == 0, stop=k == KC - 1, tile_position=(0, 32 * j))
                return mm

            def first_products():
                for u in range(4):
                    if u < 2:
                        pe.wait_ge(raw_in[u], RAW_ARRIVED[u])
                    for kk in range(2):
                        if u >= 2:
                            pe.wait_ge(ada_in[2 * (u - 2) + kk], 16)
                        buf = raw[u] if u < 2 else ada_end[u - 2]
                        mm = product(2 * u + kk, buf[:, 4 * BANK * kk:4 * BANK * (kk + 1)])
                    mm.then_inc(gemv, 1)

            def later_product(n):
                if n == 0:
                    pe.wait_ge(wix_ready, 1)
                elif n == KC:
                    pe.wait_ge(col_ready, 2)
                pe.wait_ge(part_in, 16 * (n + 1))
                product(n % KC, ada_part).then_inc(gemv, 1)

            def turn_rows(g):
                pe.wait_ge(m_ready, g + 1)
                if g == 2:
                    pe.wait_ge(pt_ready, N_SOFT)
                for n in range(4):
                    mm = pe.transpose(bank[B_ROWS[g]][:, P * n:P * (n + 1)], mrow[:, g % 2, P * n:P * (n + 1)], ident[:, :])
                mm.then_inc(m_turned, 1)

            def spread_rows(g):
                if g == 1:
                    pe.wait_ge(o_lo, N_HEADS)
                else:
                    pe.wait_ge(gb_ready, 2)
                for n in range(2):
                    j = n if g == 1 else 2 + n
                    pe.matmul(bank[6 + n][:, :], select[:, j, :], mrow[:, g % 2, :], start=True, stop=True).then_inc(m_spread, 1)

            def turn_x(k, t):
                pe.wait_ge(xn_ready, 2 * k + t + 1)
                for half in range(2):
                    for c in range(4 * half, 4 * half + 4):
                        if k == 0:
                            dst = turned(c)[:, P * t:P * (t + 1)]
                        else:
                            dst = bank[B_TURNED[t] + half][:, P * (c % 4):P * (c % 4 + 1)]
                        mm = pe.matmul(dst, xt[:, t, P * c:P * (c + 1)], diag[t], start=True, stop=True)
                    mm.then_inc(x_turned, 1)

            def unit(u):
                b, what, c0, n, dest = UNITS[u]
                if u >= 2:
                    pe.wait_ge(unit_read, u - 1)
                w = [block_view(x[b % 2], b)[:, :, c0:c0 + n] for x in (whi, wlo)]
                for k in range(KC):
                    if k % 2 == 0 and (u == 0 or UNITS[u - 1][0] != b):
                        pe.wait_ge(w_hi, 4 * b + k // 2 + 1)
                        pe.wait_ge(w_lo, 4 * b + k // 2 + 1)
                    if u == 0 and k % 2 == 0:
                        pe.wait_ge(h_hi, k // 2 + 1)
                        pe.wait_ge(h_lo, k // 2 + 1)
                    if what != "values":
                        mm = three(bank[B_UNIT + u % 2][0:n, 0:S], [x[:, k, :] for x in w], [hhi[:, k, :], hlo[:, k, :]],
                                   k == 0, k == KC - 1)
                    else:
                        t = dest[0]
                        mm = three(bank[B_UNIT + u % 2][:, 0:n], [x[:, k, P * t:P * (t + 1)] for x in (hhi, hlo)],
                                   [x[:, k, :] for x in w], k == 0, k == KC - 1)
                mm.then_inc(units, 1)

            def query_major(dst, q, k, p0):
                pe.matmul(dst[:, 0:P], q[p0:p0 + HD, 0:P], k[p0:p0 + HD, 0:P], start=True, stop=True)
                return pe.matmul(dst[:, P:CAUSAL], q[p0:p0 + HD, P:S], k[p0:p0 + HD, :], start=True, stop=True)

            def key_major(dst, q, k, p0):
                pe.matmul(dst[:, 0:S], k[p0:p0 + HD, 0:P], q[p0:p0 + HD, :], start=True, stop=False, skip_group_check=True)
                return pe.matmul(dst[:, S:CAUSAL], k[p0:p0 + HD, P:S], q[p0:p0 + HD, P:S], start=False, stop=True,
                                 skip_group_check=True)

            def scores(n):
                branch, h, tq, tk, _ = HEADS[n]
                q, k, p0 = qk[:, tq + h // 2, :], qk[:, tk + h // 2, :], HD * (h % 2)
                if n < 2:
                    pe.wait_ge(relu_ready, H_IX)
                elif n - 2 in SB_NO:
                    pe.wait_ge(a_ready, SB_NO[n - 2] + 1)
                else:
                    pe.wait_ge(max_ready, SOFT_NO[n - 2] + 1)
                (key_major if n in SB_NO else query_major)(bank[B_Z + n % 2], q, k, p0).then_inc(z_ready, 1)

            def second(n):
                if n in SB_NO:
                    i = SB_NO[n]
                    pe.wait_ge(sp_masked, 2 * (i + 1))
                    z, s = bank[B_Z + n % 2], bufp[n % 2]
                    pe.matmul(z[:, 0:CAUSAL], tri[:, :], s[:, :], start=False, stop=False, skip_group_check=True)
                    pe.matmul(z[:, P:S], neg1[:, :], s[:, S:CAUSAL], start=False, stop=True, skip_group_check=True).then_inc(sums, 1)
                else:
                    i = SOFT_NO[n]
                    pe.wait_ge(p_ready, i + 1)
                    if i >= 1:
                        pe.wait_ge(pt_ready, i)
                    for c in range(3):
                        mm = pe.transpose(bank[B_T][:, P * c:P * (c + 1)], bufp[n % 2][:, P * TURNED[c]:P * (TURNED[c] + 1)], ident[:, :])
                    mm.then_inc(p_turned, 1)

            def output(n):
                branch, h, _, _, v0 = HEADS[n]
                if n in SB_NO:
                    pe.wait_ge(a_masked, 2 * (SB_NO[n] + 1))
                else:
                    pe.wait_ge(pt_ready, SOFT_NO[n] + 1)
                if n >= 2:
                    pe.wait_ge(o_lo, n - 1)
                p0, a = HD * (h % 2), buft[n % 2]
                dst, cols = bank[B_O + n % 2][p0:p0 + HD, :], slice(v0 + HD * h, v0 + HD * (h + 1))
                pe.matmul(dst[:, 0:S], v[:, 0, cols], a[:, 0:S], start=True, stop=False, skip_group_check=True)
                pe.matmul(dst[:, P:S], v[:, 1, cols], a[:, S:CAUSAL], start=False, stop=True, skip_group_check=True).then_inc(o_ready, 1)

            pe.wait_ge(consts, 7)
            for t in range(TT):
                turn_x(0, t)
            pe.wait_ge(bg_in, 16)
            pe.transpose(bank[4][:, 0:3 * KC], bgr[:, :], ident[0:3 * KC, 0:3 * KC]).then_inc(bg_turned, 1)
            pe.wait_ge(c_ready, 2)
            first_products()
            turn_rows(0)
            for u in range(N_UNITS):
                unit(u)
                if u == 2:
                    pe.wait_ge(unit_read, 1)
                    pe.wait_ge(m_ready, 1)
                    for t in range(TT):
                        mm = pe.transpose(bank[B_ADA][:, H_IX * t:H_IX * (t + 1)], wixt[HD:HD + H_IX, P * t:P * (t + 1)],
                                          ident[HD:HD + H_IX, HD:HD + H_IX])
                    mm.then_inc(wix_turned, 1)
                if u in ADA_AT:
                    later_product(ADA_AT[u])
                if u in TURN_AT:
                    turn_rows(TURN_AT[u])
                if u in LOGITS_AT:
                    h = LOGITS_AT[u]
                    if h == 0:
                        pe.wait_ge(unit_read, 5)
                        pe.wait_ge(bg_ready, 1)
                    if h >= 3:
                        pe.wait_ge(relu_ready, h - 2)
                    query_major(bank[B_Z + h % 3], qk[:, T_QIX + h // 2, :], qk[:, T_KIX, :], HD * (h % 2)).then_inc(logits, 1)
                if u in OUTPUT_AT:
                    output(OUTPUT_AT[u])
                if u in SECOND_AT:
                    second(SECOND_AT[u])
                if u in SCORES_AT:
                    scores(SCORES_AT[u])

            for f in range(KC):
                b = B_PROJ + f // 2
                if f % 2 == 0:
                    pe.wait_ge(w_hi, 4 * (b + 1))
                    pe.wait_ge(w_lo, 4 * (b + 1))
                if f == 0:
                    pe.wait_ge(o_hi, N_HEADS)
                    pe.wait_ge(o_lo, N_HEADS)
                if f == 0:
                    pe.wait_ge(unit_read, N_UNITS - 1)
                elif f == 1:
                    pe.wait_ge(unit_read, N_UNITS)
                    pe.wait_ge(col_ready, 3)
                else:
                    pe.wait_ge(gated, 3 * (f - 1))
                w = [block_view(x[b % 2], b)[:, :, P * (f % 2):P * (f % 2 + 1)] for x in (whi, wlo)]
                for i, branch in enumerate(("sb", "mb", "ds")):
                    for c, ch in enumerate(BRANCH_CHUNKS[branch]):
                        rows_ = P if ch < FULL_OCH else HD
                        mm = three(bank[2 * i + 1 - f % 2][:, 0:S], [x[0:rows_, ch, :] for x in w],
                                   [ohi[0:rows_, ch, :], olo[0:rows_, ch, :]], c == 0, c == 2)
                mm.then_inc(units, 1)
                if f in SPREAD_AT:
                    spread_rows(SPREAD_AT[f])

            def out_part(t, half, n, kk):
                b, k = B_WO + half, 4 * half + kk
                return three(bank[B_Y[0][t] + n][:, :], [x[:, k, P * t:P * (t + 1)] for x in (hhi, hlo)],
                             [block_view(x[b % 2], b)[:, kk, BANK * n:BANK * (n + 1)] for x in (whi, wlo)],
                             k == 0, k == KC - 1)

            pe.wait_ge(gb_ready, 4)
            for t in range(TT):
                if t == 1:
                    pe.wait_ge(gated, 3 * KC)
                for kk in range(4):
                    if t == 0:
                        pe.wait_ge(w_hi, 4 * B_WO + kk + 1)
                        pe.wait_ge(w_lo, 4 * B_WO + kk + 1)
                        pe.wait_ge(m_lo, kk + 1)
                    for n in range(2):
                        mm = out_part(t, 0, n, kk)
                mm.then_inc(units, 1)
                for n in range(2):
                    for kk in range(4):
                        if t == 0 and n == 0:
                            pe.wait_ge(w_hi, 4 * (B_WO + 1) + kk + 1)
                            pe.wait_ge(w_lo, 4 * (B_WO + 1) + kk + 1)
                            pe.wait_ge(m_lo, 4 + kk + 1)
                        mm = out_part(t, 1, n, kk)
                    mm.then_inc(units, 1)
                    if t == 1 and n == 0:
                        turn_x(1, 0)

            def first_up(t, j):
                w = block_view(raw[1], B_FFN)
                for a in range(2):
                    for k in range(KC):
                        if j == 0 and a == 0 and k == 0:
                            pe.wait_ge(h_act, TT + t + 1)
                        if j == 0 and a == 0 and k == KC // 2:
                            pe.wait_ge(h_dve, TT + t + 1)
                        mm = pe.matmul(bank[j][:, S * a + P * t:S * a + P * (t + 1)],
                                       w[:, k, FSTEP * a + P * j:FSTEP * a + P * (j + 1)], hx[:, t, k, :],
                                       start=k == 0, stop=k == KC - 1)
                return mm

            pe.wait_ge(raw_in[1], RAW_COUNT[1] + 32)
            for j in range(2):
                pe.wait_ge(dve_scaled, 3 + j)
                first_up(0, j)
            turn_x(1, 1)
            for j in range(2):
                first_up(1, j).then_inc(up_done, 1)

            def up(i, slot, first):
                pe.wait_ge(up_hi, 4 * i)
                pe.wait_ge(up_lo, 4 * i)
                for j in range(2):
                    if first:
                        pe.wait_ge(h_lo, 8)
                    else:
                        pe.wait_ge(f_ready, 2 * (i - 2) + j + 1)
                    dst = bank[2 * (1 - slot) + j]
                    for a in range(2):
                        for k in range(KC):
                            w = [block_view(x[slot], B_FFN)[:, k, FSTEP * a + P * j:FSTEP * a + P * (j + 1)] for x in (whi, wlo)]
                            mm = three(dst[:, S * a:S * (a + 1)], w, [hhi[:, k, :], hlo[:, k, :]], k == 0, k == KC - 1)
                    mm.then_inc(up_done, 1)

            def down_part(i, slot, t, n, first, last):
                for j in range(2):
                    mm = three(bank[B_Y[1][t] + n][:, :], [x[:, j, P * t:P * (t + 1)] for x in (fhi[slot], flo[slot])],
                               [x[slot][:, j, BANK * n:BANK * (n + 1)] for x in (dhi, dlo)],
                               first and j == 0, last and j == 1)
                return mm

            def down_ready(i):
                pe.wait_ge(d_hi, i + 1)
                pe.wait_ge(d_lo, i + 1)
                pe.wait_ge(f_lo, 2 * (i + 1))

            def down(i, slot, first):
                down_ready(i)
                for t in range(TT):
                    for n in range(2):
                        mm = down_part(i, slot, t, n, first, False)
                mm.then_inc(down_done, 1)

            up(1, 0, True)
            down(0, 1, True)
            with pe.Fori(2, N_FFN - 1, 2) as i:
                up(i, 1, False)
                down(i - 1, 0, False)
                up(i + 1, 0, False)
                down(i, 1, False)
            up(N_FFN - 1, 1, False)
            down_ready(N_FFN - 2)
            for t in range(TT):
                for n in range(2):
                    down_part(N_FFN - 2, 0, t, n, False, False)
                    if t == 0 and n == 0:
                        down_ready(N_FFN - 1)
                    down_part(N_FFN - 1, 1, t, n, False, True).then_inc(down_done, 1)


LOGITS_LAST = max(LOGITS_AT)
TURNED = (0, 1, 2)


_INS = ["x", "c", "w_ada", "b_ada", "g_pre_mix", "g_post_mix", "w_in", "b_gate", "w_proj_sb", "w_proj_moba",
        "w_proj_dsa", "w_o", "g_pre_ffn", "g_post_ffn", "w_up", "w_down"]
_OUTS = [((1, S, D), "float32")]


def kernel(**inputs):
    import numpy as _np
    import concourse.bacc as _bacc
    from concourse import mybir as _mybir
    from concourse.bass_utils import run_bass_kernel_spmd as _run

    nc = _bacc.Bacc("TRN2", target_bir_lowering=False, num_devices=1)
    arrays, args = {}, []
    for name in _INS:
        a = _np.ascontiguousarray(inputs[name])
        arrays[f"in_{name}_dram"] = a
        args.append(nc.dram_tensor(f"in_{name}_dram", a.shape, _mybir.dt.from_np(a.dtype), kind="ExternalInput").ap())
    for i, (shape, dtype) in enumerate(_OUTS):
        dt = _mybir.dt.from_np(_np.dtype(dtype))
        args.append(nc.dram_tensor(f"out_{i}_dram", shape, dt, kind="ExternalOutput").ap())
    decoder_layer(nc, *args)
    r = _run(nc, [arrays], core_ids=[0])
    return r.results[0]["out_0_dram"]
```

```python
from contextlib import ExitStack

import concourse.bass as bass
from concourse import mybir

F32 = mybir.dt.float32
F32R = mybir.dt.float32r
ALU = mybir.AluOpType
ACT = mybir.ActivationFunctionType
AX_X = mybir.AxisListType.X

P = 128
D = 1024
KC = D // P
S = 256
TT = S // P
HD = 64
H_SB, H_MB, H_DS, H_IX = 6, 5, 5, 8
W_SB, W_MB, W_DS, W_IX = H_SB * HD, H_MB * HD, H_DS * HD, H_IX * HD
FF = 2816
TOPK = min(256, S // 4)
EPS = 1e-6
SCALE = HD ** -0.5
MASKED = -1e30
TAKEN = -3e38
SLOPES = [2.0 ** (-8.0 * (i + 1) / (H_MB + H_DS)) for i in range(H_MB + H_DS)]
CAUSAL = 3 * P
BANK = 512

sizes = [W_SB] * 3 + [W_MB] * 3 + [W_DS] * 3 + [W_IX, HD, H_IX, 3 * D]
offs = [sum(sizes[:i]) for i in range(len(sizes))]
(O_QSB, O_KSB, O_VSB, O_QMB, O_KMB, O_VMB, O_QDS, O_KDS, O_VDS, O_QIX, O_KIX, O_WIX, O_GATE) = offs

T_QIX, T_KIX, T_QMB, T_KMB, T_QSB, T_KSB, T_QDS, T_KDS = 0, 4, 5, 8, 11, 14, 17, 20
V_MB, V_SB, V_DS = 0, W_MB, W_MB + W_SB

GATE_BLOCKS = 3 * D // BANK
MIX_BLOCKS = [(O_KIX, HD + H_IX), (O_QIX, W_IX), (O_QMB, W_MB - HD), (O_KMB - HD, HD + W_MB), (O_VMB, W_MB),
              (O_QSB, W_SB), (O_KSB, W_SB), (O_VSB, W_SB), (O_QDS, W_DS - HD), (O_KDS - HD, HD + W_DS), (O_VDS, W_DS)]
MIX_BLOCKS += [(O_GATE + BANK * i, BANK) for i in range(GATE_BLOCKS)]
KEY_BLOCKS = (3, 9)
N_MIX = len(MIX_BLOCKS)
PROJ_COLS = 256
N_PROJ = D // PROJ_COLS
B_PROJ = N_MIX
B_WO = B_PROJ + N_PROJ
B_FFN = B_WO + 2
FSTEP = 2 * P
N_FFN = FF // FSTEP


def mix_units():
    units = []
    def features(b, tile, cols, base=0):
        for n, c in enumerate(range(0, cols, P)):
            units.append((b, "features", base + c, min(P, cols - c), tile + n))
    def tokens(b, what, base, cols, dest):
        for t in range(TT):
            units.append((b, what, base, cols, (t, dest)))
    def keys(b, tq, tk, cols):
        features(b, tk, cols - HD)
        units.append((b, "last head", cols - HD, P, (tk + cols // P, tq + cols // P)))
    units.append((0, "index keys and weights", 0, HD + H_IX, T_KIX))
    features(1, T_QIX, W_IX)
    features(2, T_QMB, W_MB - HD)
    keys(3, T_QMB, T_KMB, W_MB)
    tokens(4, "values", 0, W_MB, V_MB)
    features(5, T_QSB, W_SB)
    features(6, T_KSB, W_SB)
    tokens(7, "values", 0, W_SB, V_SB)
    features(8, T_QDS, W_DS - HD)
    keys(9, T_QDS, T_KDS, W_DS)
    tokens(10, "values", 0, W_DS, V_DS)
    for g in range(3 * D // P):
        units.append((11 + g // 4, "gate", g % 4 * P, P, g))
    return units


UNITS = mix_units()
N_UNITS = len(UNITS)
FIRST_GATE = N_UNITS - 3 * D // P
UNITS_DONE = [max(n for n, u in enumerate(UNITS) if u[0] == b) + 1 for b in range(N_MIX)]
PROJ_DONE = [N_UNITS + 2 * (i + 1) for i in range(N_PROJ)]
WO_DONE = [PROJ_DONE[-1] + 4, PROJ_DONE[-1] + 6]
BLOCK_DONE = UNITS_DONE + PROJ_DONE + WO_DONE


def y_done(t, n):
    return PROJ_DONE[-1] + 3 * t + 2 + n


O_CHUNK = {"mb": [3, 3, 4, 4, 7], "sb": [0, 0, 1, 1, 2, 2], "ds": [5, 5, 6, 6, 8]}
N_OCH = 9
FULL_OCH = 7
BRANCH_CHUNKS = {"sb": [0, 1, 2], "mb": [3, 4, 7], "ds": [5, 6, 8]}
HEADS = [("mb", h, T_QMB, T_KMB, V_MB) for h in range(H_MB)]
HEADS += [("sb", h, T_QSB, T_KSB, V_SB) for h in range(H_SB)]
HEADS += [("ds", h, T_QDS, T_KDS, V_DS) for h in range(H_DS)]
N_HEADS = len(HEADS)
HEAD_START = 13
HEAD_EVERY = 2
SCORES_AT = {HEAD_START + HEAD_EVERY * n: n for n in range(N_HEADS)}
EXP_AT = {u + 1: n for u, n in SCORES_AT.items()}
NORM_AT = {u + 2: n for u, n in SCORES_AT.items()}
SECOND_AT = {u + 3: n for u, n in SCORES_AT.items()}
PAIRS = [(n, n + 1) for n in range(N_HEADS - 1) if HEADS[n][0] == HEADS[n + 1][0] and HEADS[n][1] % 2 == 0]
OUTPUT_AT = {}
for _n in range(N_HEADS):
    if (_n, _n + 1) in PAIRS:
        OUTPUT_AT[HEAD_START + HEAD_EVERY * (_n + 1) + 4] = (_n, _n + 1)
    elif (_n - 1, _n) not in PAIRS:
        OUTPUT_AT[HEAD_START + HEAD_EVERY * _n + 5] = (_n,)
LOGITS_AT = {5 + h: h for h in range(H_IX)}
TOPK_ROUNDS = TOPK // 8
ROUND_AT = {25 + r: r for r in range(TOPK_ROUNDS)}
N_SOFT = H_MB + H_DS
SOFT_NO = {n: i for i, n in enumerate(n for n in range(N_HEADS) if HEADS[n][0] != "sb")}
SB_NO = {n: i for i, n in enumerate(n for n in range(N_HEADS) if HEADS[n][0] == "sb")}


def softs_before(n):
    return sum(1 for m in SOFT_NO if m < n)


def pieces_at():
    plan = {}
    for b in range(N_MIX):
        us = [n for n, u in enumerate(UNITS) if u[0] == b]
        for q in range(4):
            plan.setdefault(us[q * len(us) // 4], []).append((b + 1, q))
    return plan


PIECES_AT = pieces_at()

ADA_COLS = 4 * BANK
ADA_UNIT = [2, 4, 6, 9, 12, 15, 18, 22, 25, 28, 31, 34, 37, 40, 43, 46]
ADA_AT = {u: n for n, u in enumerate(ADA_UNIT)}
SUM_AT = {ADA_UNIT[g * KC - 1] + 2: g for g in (1, 2)}
TURN_AT = {u + 1: g for u, g in SUM_AT.items()}
COLUMNS_AT = {u + 1: g for u, g in TURN_AT.items()}
MERGE_PIECES = [[(1, q) for q in range(4)]]
MERGE_PIECES += [[(f // 2 + 2, 0), (f // 2 + 2, 1)] if f % 2 else [(f // 2 + 1, 2), (f // 2 + 1, 3)] for f in range(1, KC - 1)]
MERGE_PIECES += [[(KC // 2 + 1, q) for q in range(4)]]
SPREADS = [(1, 0, 0), (1, 0, 1), (2, 1, 0), (2, 1, 1)]
VEC_GATE, VEC_ADA, VEC_PRE_MIX, VEC_POST_MIX, VEC_PRE_FFN, VEC_POST_FFN, VEC_END = (
    0, 3 * KC, 9 * KC, 10 * KC, 11 * KC, 12 * KC, 13 * KC)
SIGMOID_FROM = max(EXP_AT) + 4
EARLY_GATES = SIGMOID_FROM - FIRST_GATE
SIGMOID_BATCHES = 3


def raw_uses():
    uses = [("ada", u) for u in range(2)]
    uses += [("block", b) for b in range(B_FFN)]
    return uses


RAW = raw_uses()
N_RAW = len(RAW)
LOADS = {b: 1 for b in range(B_FFN)}
LOADS.update({b: 7 for b in range(B_PROJ, B_WO)})
LOADS.update({b: 2 for b in KEY_BLOCKS})


def raw_arrivals():
    count, out = [0, 0], []
    for r, (kind, b) in enumerate(RAW):
        count[r % 2] += 16 * (1 if kind == "ada" else LOADS[b])
        out.append(count[r % 2])
    return out, count


RAW_ARRIVED, RAW_COUNT = raw_arrivals()
RAW_OF_BLOCK = {b: r for r, (kind, b) in enumerate(RAW) if kind == "block"}


def decoder_layer(nc, x, c, w_ada, b_ada, g_pre_mix, g_post_mix, w_in, b_gate, w_proj_sb,
                  w_proj_moba, w_proj_dsa, w_o, g_pre_ffn, g_post_ffn, w_up, w_down, out):
    ctx = ExitStack()
    with ctx:
        def sb(name, shape, dt=F32, scope=ctx):
            return scope.enter_context(nc.sbuf_tensor(name, shape, dt))

        def sem(name):
            return ctx.enter_context(nc.semaphore(name))

        raw = [sb(f"raw{i}", [P, KC * BANK]) for i in range(2)]
        whi = [sb(f"whi{i}", [P, KC * BANK], F32R) for i in range(2)]
        wlo = [sb(f"wlo{i}", [P, KC * BANK], F32R) for i in range(2)]
        xt = sb("xt", [P, TT, D])
        hhi = sb("hhi", [P, KC, S], F32R)
        hlo = sb("hlo", [P, KC, S], F32R)
        xn = sb("xn", [P, TT, D])
        hx = xn[:, :, :].rearrange("p t (k n) -> p t k n", n=P)
        ada_part = xn[:, :, :].rearrange("p t n -> p (t n)")
        diag = [xn[:, t, D - P:D] for t in range(TT)]
        h32 = xn[:, :, :].rearrange("p t (k n) -> p (t k) n", n=S)
        ident = sb("ident", [P, P])
        ccol = sb("ccol", [P, KC])
        csil = sb("csil", [P, KC])
        crep = sb("crep", [P, KC, 32])
        col = [sb(f"col{g}", [P, 16]) for g in range(3)]
        ssq = sb("ssq", [P, 8, 2])
        var, root_, rinv = (sb(name, [P, 8]) for name in ("var", "root", "rinv"))
        warm = sb("warm", [P, 1])

        mix = ExitStack()
        v = sb("v", [P, TT, D], scope=mix)
        qk = sb("qk", [P, 3 * KC, S], scope=mix)
        gates = qk
        ohi = sb("ohi", [P, N_OCH, S], F32R, scope=mix)
        olo = sb("olo", [P, FULL_OCH, S], F32R, scope=mix)
        acc = sb("acc", [P, ADA_COLS], scope=mix)
        spread = [acc[:, BANK * i:BANK * (i + 1)] for i in range(len(SPREADS))]
        mrow = sb("mrow", [P, BANK], scope=mix)
        wix = sb("wix", [P, TT, H_IX], scope=mix)
        dist = sb("dist", [P, CAUSAL], scope=mix)
        dsel = sb("dsel", [P, CAUSAL], scope=mix)
        tri = sb("tri", [P, P], scope=mix)
        neg1 = sb("neg1", [P, P], scope=mix)
        vec_rows = sb("vec_rows", [VEC_END, P], scope=mix)
        vecs = sb("vecs", [P, VEC_END], scope=mix)
        score = sb("score", [P, CAUSAL], scope=mix)
        work = sb("work", [P, CAUSAL], scope=mix)
        wixt = work[0:HD + H_IX, 0:S]
        top8 = sb("top8", [P, TT, 8], scope=mix)
        bufa = [sb(f"bufa{i}", [P, CAUSAL], scope=mix) for i in range(2)]
        bufp = [sb(f"bufp{i}", [P, CAUSAL], scope=mix) for i in range(2)]
        buft = [sb(f"buft{i}", [P, CAUSAL], scope=mix) for i in range(2)]
        smax = sb("smax", [P, 2, TT], scope=mix)
        ssum = sb("ssum", [P, 2, TT], scope=mix)
        gp = [[b[:, 0:S] for b in bufs] for bufs in ((bufa[0], bufa[1], bufp[0]), (bufp[1], buft[0], buft[1]))]
        mix.close()

        start = ExitStack()
        ada_end = [sb(f"ada_end{i}", [P, KC * BANK], scope=start) for i in range(2)]
        start.close()

        ffn = ExitStack()
        gb = [None] + [sb(f"gb{g}", [P, D], scope=ffn) for g in (1, 2)]
        draw = [sb(f"draw{i}", [P, 2, D], scope=ffn) for i in range(2)]
        dhi = [sb(f"dhi{i}", [P, 2, D], F32R, scope=ffn) for i in range(2)]
        dlo = [sb(f"dlo{i}", [P, 2, D], F32R, scope=ffn) for i in range(2)]
        fsil = [sb(f"fsil{i}", [P, 2, S], scope=ffn) for i in range(2)]
        fhi = [sb(f"fhi{i}", [P, 2, S], F32R, scope=ffn) for i in range(2)]
        flo = [sb(f"flo{i}", [P, 2, S], F32R, scope=ffn) for i in range(2)]
        ffn.close()

        psum = ctx.enter_context(nc.psum_tensor("psum", [P, 8, BANK], F32))
        bank = [psum[:, i, :] for i in range(8)]
        B_UNIT, B_Z, B_T, B_ADA, B_O = 0, 2, 4, 5, 6
        B_ROWS = (7, B_ADA, B_T)
        B_Y = ((6, 0), (4, 6))
        B_TURNED = (2, 4)

        ada_in = [sem(f"ada_in{k}") for k in range(KC // 2, KC)]
        part_in = sem("part_in")
        raw_in = [sem(f"raw_in{i}") for i in range(2)]
        down_in = [sem(f"down_in{i}") for i in range(2)]
        pool_step = sem("pool_step")
        x_in, c_in, stored = sem("x_in"), sem("c_in"), sem("stored")
        consts = sem("consts")
        w_hi, w_lo = sem("w_hi"), sem("w_lo")
        units = sem("units")
        unit_read = sem("unit_read")
        gemv = sem("gemv")
        acc_done = sem("acc_done")
        summed = sem("summed")
        m_ready, m_turned = sem("m_ready"), sem("m_turned")
        c_ready = sem("c_ready")
        act_step, dve_step = sem("act_step"), sem("dve_step")
        ss_ready, var_ready, sqrt_ready, xn_ready = sem("ss_ready"), sem("var_ready"), sem("sqrt_ready"), sem("xn_ready")
        x_turned, h_act, h_dve, h_hi, h_lo = sem("x_turned"), sem("h_act"), sem("h_dve"), sem("h_hi"), sem("h_lo")
        wix_turned, wix_ready, dve_scaled = sem("wix_turned"), sem("wix_ready"), sem("dve_scaled")
        col_ready, diag_ready, m_spread, gb_ready = sem("col_ready"), sem("diag_ready"), sem("m_spread"), sem("gb_ready")
        vec_in, vec_turned, vec_ready = sem("vec_in"), sem("vec_turned"), sem("vec_ready")
        logits, relu_ready, score_added, score_masked = (sem("logits"), sem("relu_ready"), sem("score_added"),
                                                        sem("score_masked"))
        z_ready, max_ready, exp_ready, p_ready = sem("z_ready"), sem("max_ready"), sem("exp_ready"), sem("p_ready")
        p_turned, pt_ready = sem("p_turned"), sem("pt_ready")
        ln_ready, sp_ready, sp_masked, sums, a_ready, a_masked = (sem("ln_ready"), sem("sp_ready"), sem("sp_masked"),
                                                                 sem("sums"), sem("a_ready"), sem("a_masked"))
        o_ready, o_hi, o_lo = sem("o_ready"), sem("o_hi"), sem("o_lo")
        sig_ready, gated, merged, m_hi, m_lo = sem("sig_ready"), sem("gated"), sem("merged"), sem("m_hi"), sem("m_lo")
        x_new = sem("x_new")
        up_done, down_done, silu_done, f_ready, f_hi, f_lo = (sem("up_done"), sem("down_done"), sem("silu_done"),
                                                             sem("f_ready"), sem("f_hi"), sem("f_lo"))
        d_hi, d_lo, up_hi, up_lo = sem("d_hi"), sem("d_lo"), sem("up_hi"), sem("up_lo")

        block = ctx.enter_context(nc.Block())

        x_dram = x.rearrange("b (t p) d -> p (b t) d", p=P)
        out_dram = out.rearrange("b (t p) d -> p (b t) d", p=P)
        ada_dram = w_ada.rearrange("l (p k) n -> p (l k) n", k=KC)
        in_dram = w_in.rearrange("l (k p) n -> p (l k) n", p=P)
        up_dram = w_up.rearrange("l (k p) n -> p (l k) n", p=P)
        down_dram = w_down.rearrange("l (k p) n -> p (l k) n", p=P)
        wo_dram = w_o.rearrange("l (k p) n -> p (l k) n", p=P)

        def turned(c):
            return bank[(2, 3, 4, 6)[c % 4]][:, S * (c // 4):S * (c // 4 + 1)]

        def block_view(buf, b):
            if b < N_MIX:
                n = MIX_BLOCKS[b][1]
                return buf[:, 0:KC * n].rearrange("p (k n) -> p k n", n=n)
            if b < B_WO:
                return buf[:, 0:N_OCH * PROJ_COLS].rearrange("p (k n) -> p k n", n=PROJ_COLS)
            if b < B_FFN:
                return buf[:, :].rearrange("p (k n) -> p k n", n=D)
            return buf[:, :].rearrange("p (k n) -> p k n", n=BANK)

        def block_parts(b):
            every = slice(None)
            if b == 1:
                return [(P, every, slice(P * q, P * (q + 1))) for q in range(4)]
            if b < N_MIX or b >= B_FFN:
                return [(P, slice(2 * q, 2 * q + 2), every) for q in range(4)]
            if b < B_WO:
                return [(P, slice(0, 3), every), (P, slice(3, 5), every), (P, slice(5, FULL_OCH), every),
                        (P, slice(FULL_OCH, N_OCH), every)]
            return [(P, slice(q, q + 1), every) for q in range(4)]

        def hold(b):
            return BLOCK_DONE[b - 2] if b >= 2 else 0

        @block.sync
        def _(sp):
            sp.dma_start(ccol[:, :], c.rearrange("b (p k) -> p (b k)", k=KC)).then_inc(c_in, 16)
            for t in range(TT):
                sp.dma_start(xt[:, t, :], x_dram[:, t, :]).then_inc(x_in, 16)

            def load(r):
                kind, b = RAW[r]
                dst, arrived = raw[r % 2], raw_in[r % 2]
                if r >= 2:
                    before, b0 = RAW[r - 2]
                    if before == "ada":
                        sp.wait_ge(gemv, b0 + 1)
                    else:
                        sp.wait_ge(w_hi, 4 * (b0 + 1))
                        sp.wait_ge(w_lo, 4 * (b0 + 1))
                if kind == "ada":
                    sp.dma_start(dst[:, :].rearrange("p (k n) -> p k n", k=2),
                                 ada_dram[:, 2 * b:2 * b + 2, 0:ADA_COLS]).then_inc(arrived, 16)
                elif b < N_MIX:
                    c0, n = MIX_BLOCKS[b]
                    if b in KEY_BLOCKS:
                        view = block_view(dst, b)
                        sp.dma_start(view[:, :, 0:n - HD], in_dram[:, :, c0 + HD:c0 + n]).then_inc(arrived, 16)
                        sp.dma_start(view[:, :, n - HD:n], in_dram[:, :, c0:c0 + HD]).then_inc(arrived, 16)
                    else:
                        sp.dma_start(block_view(dst, b), in_dram[:, :, c0:c0 + n]).then_inc(arrived, 16)
                elif b < B_WO:
                    c0 = PROJ_COLS * (b - B_PROJ)
                    view = block_view(dst, b)
                    cols = slice(c0, c0 + PROJ_COLS)
                    for w, k0, n, last in ((w_proj_sb, 0, 3, None), (w_proj_moba, 3, 2, 7), (w_proj_dsa, 5, 2, 8)):
                        sp.dma_start(view[:, k0:k0 + n, :],
                                     w[0, 0:n * P, cols].rearrange("(k p) n -> p k n", p=P)).then_inc(arrived, 16)
                        if last is not None:
                            for p0 in (0, HD):
                                sp.dma_start(view[p0:p0 + HD, last, :], w[0, n * P:n * P + HD, cols]).then_inc(arrived, 16)
                else:
                    k0 = 4 * (b - B_WO)
                    sp.dma_start(block_view(dst, b), wo_dram[:, k0:k0 + 4, :]).then_inc(arrived, 16)

            for i, (w, k0) in enumerate(((b_gate, VEC_GATE), (b_ada, VEC_ADA), (g_pre_mix, VEC_PRE_MIX),
                                         (g_post_mix, VEC_POST_MIX), (g_pre_ffn, VEC_PRE_FFN), (g_post_ffn, VEC_POST_FFN))):
                n = w.shape[0] * w.shape[1] // P
                sp.dma_start(vec_rows[k0:k0 + n, :], w.rearrange("l (k p) -> (l k) p", p=P)).then_inc(vec_in, 16)
            load(0)
            load(1)
            for i in range(2):
                for kk in range(2):
                    k = 4 + 2 * i + kk
                    sp.dma_start(ada_end[i][:, ADA_COLS * kk:ADA_COLS * (kk + 1)], ada_dram[:, k, 0:ADA_COLS]).then_inc(ada_in[2 * i + kk], 16)
            for r in range(2, N_RAW):
                load(r)

            def load_step(i, slot, first, third=False):
                view = block_view(raw[slot], B_FFN).rearrange("p k (a n) -> p k a n", a=2)
                if first:
                    sp.wait_ge(w_hi, 4 * (B_WO + 1 + i))
                    sp.wait_ge(w_lo, 4 * (B_WO + 1 + i))
                elif third:
                    sp.wait_ge(up_done, 2)
                else:
                    sp.wait_ge(up_hi, 4 * (i - 2))
                    sp.wait_ge(up_lo, 4 * (i - 2))
                for a in range(2):
                    sp.dma_start(view[:, :, a, :], up_dram[:, :, bass.ds(i * FSTEP + FF * a, FSTEP)]).then_inc(raw_in[slot], 16)
                if first:
                    sp.wait_ge(units, BLOCK_DONE[B_WO - 1])
                    sp.wait_ge(merged, KC)
                else:
                    sp.wait_ge(d_hi, i - 1)
                    sp.wait_ge(d_lo, i - 1)
                sp.dma_start(draw[slot][:, :, :], down_dram[:, bass.ds(2 * i, 2), :]).then_inc(down_in[slot], 16)

            load_step(0, 1, True)
            load_step(1, 0, True)
            load_step(2, 1, False, True)
            with sp.Fori(3, N_FFN - 1, 2) as i:
                load_step(i, 0, False)
                load_step(i + 1, 1, False)

            for t in range(TT):
                for n in range(2):
                    cols = slice(BANK * n, BANK * (n + 1))
                    sp.wait_ge(x_new, 4 + 2 * t + n + 1)
                    sp.dma_start(out_dram[:, t, cols], xt[:, t, cols]).then_inc(stored, 16)
            sp.wait_ge(stored, 16 * 2 * TT)

        @block.gpsimd
        def _(pool):
            pool.memset(ident[:, :], 0.0).then_inc(consts, 1)
            pool.memset(tri[:, :], -1.0).then_inc(consts, 1)
            pool.memset(neg1[:, :], -1.0).then_inc(consts, 1)
            pool.iota(bufa[0][:, 0:P].bitcast(mybir.dt.int32), pattern=[[1, P]], base=0, channel_multiplier=-1).then_inc(consts, 1)
            pool.iota(bufa[0][:, P:CAUSAL].bitcast(mybir.dt.int32), pattern=[[1, 2 * P]], base=-P, channel_multiplier=-1).then_inc(consts, 1)
            pool.wait_ge(consts, 5)
            pool.affine_select(out=ident[:, :], in_=ident[:, :], compare_op=ALU.not_equal, fill=1.0,
                               base=0, pattern=[[-1, P]], channel_multiplier=1).then_inc(consts, 1)
            pool.affine_select(out=tri[:, :], in_=tri[:, :], compare_op=ALU.is_ge, fill=0.0,
                               base=0, pattern=[[-1, P]], channel_multiplier=1).then_inc(consts, 1)
            pool.tensor_copy(dist[:, :], bufa[0][:, :].bitcast(mybir.dt.int32)).then_inc(consts, 1)
            pool.wait_ge(consts, 8)
            for c0 in (0, 2 * P):
                pool.affine_select(out=dist[:, c0:c0 + P], in_=dist[:, c0:c0 + P], compare_op=ALU.is_ge, fill=MASKED,
                                   base=0, pattern=[[-1, P]], channel_multiplier=1).then_inc(consts, 1)

            def load_part(n):
                if n == 0:
                    pool.wait_ge(h_lo, 4)
                else:
                    pool.wait_ge(acc_done, n)
                pool.dma_start(ada_part, ada_dram[:, n % KC, ADA_COLS * (1 + n // KC):ADA_COLS * (2 + n // KC)]).then_inc(part_in, 16)

            load_part(0)
            for u in range(N_UNITS):
                if u == max(LOGITS_AT):
                    pool.wait_ge(score_added, TT * H_IX)
                    for c0 in (0, 2 * P):
                        pool.affine_select(out=score[:, c0:c0 + P], in_=score[:, c0:c0 + P], compare_op=ALU.is_ge, fill=MASKED,
                                           base=0, pattern=[[-1, P]], channel_multiplier=1).then_inc(score_masked, 1)
                if u in SECOND_AT and SECOND_AT[u] in SB_NO:
                    i = SB_NO[SECOND_AT[u]]
                    n = SECOND_AT[u]
                    pool.wait_ge(a_ready, i + 1)
                    for c0 in (0, 2 * P):
                        pool.affine_select(out=buft[n % 2][:, c0:c0 + P], in_=buft[n % 2][:, c0:c0 + P], compare_op=ALU.is_gt, fill=0.0,
                                           base=0, pattern=[[1, P]], channel_multiplier=-1).then_inc(a_masked, 1)
                if u in EXP_AT and EXP_AT[u] in SB_NO:
                    n = EXP_AT[u]
                    i = SB_NO[n]
                    pool.wait_ge(sp_ready, i + 1)
                    for c0 in (0, 2 * P):
                        pool.affine_select(out=bufp[n % 2][:, c0:c0 + P], in_=bufp[n % 2][:, c0:c0 + P], compare_op=ALU.is_gt, fill=0.0,
                                           base=0, pattern=[[1, P]], channel_multiplier=-1).then_inc(sp_masked, 1)

                if u in ADA_AT:
                    n = ADA_AT[u]
                    if n + 1 < 2 * KC:
                        load_part(n + 1)

            def spread_diag(i):
                g, vector, half = SPREADS[i]
                pool.wait_ge(summed, 3)
                pool.wait_ge(col_ready, g + 1)
                for c in range(4):
                    k = KC * vector + 4 * half + c
                    ins = pool.tensor_scalar(spread[i][:, P * c:P * (c + 1)], ident[:, :], col[g][:, k:k + 1], -1.0, ALU.mult, ALU.mult)
                ins.then_inc(diag_ready, 1)

            for i in range(3):
                spread_diag(i)

            def merge_lo(f):
                pool.wait_ge(m_hi, f + 1)
                pool.tensor_tensor(hlo[:, f, :], h32[:, f, :], hhi[:, f, :].bitcast(F32), ALU.subtract).then_inc(m_lo, 1)

            for f in range(KC):
                g = gp[f % 2]
                pool.wait_ge(gated, 3 * f + 2)
                pool.tensor_tensor(g[0], g[0], g[1], ALU.add).then_inc(pool_step, 1)
                pool.wait_ge(gated, 3 * (f + 1))
                pool.wait_ge(pool_step, f + 1)
                pool.tensor_tensor(h32[:, f, :], g[0], g[2], ALU.add).then_inc(merged, 1)
                if f == 0:
                    spread_diag(3)
                else:
                    merge_lo(f - 1)
            merge_lo(KC - 1)

        @block.scalar
        def _(act):
            steps = [0]

            def then(ins):
                steps[0] += 1
                ins.then_inc(act_step, 1)
                act.wait_ge(act_step, steps[0])

            def cut_hi(b, q):
                if q == 0:
                    r = RAW_OF_BLOCK[b]
                    act.wait_ge(raw_in[r % 2], RAW_ARRIVED[r])
                    if b >= 2:
                        act.wait_ge(units, hold(b))
                r = RAW_OF_BLOCK[b]
                p, chunks, cols = block_parts(b)[q]
                act.activation(block_view(whi[b % 2], b)[0:p, chunks, cols], block_view(raw[r % 2], b)[0:p, chunks, cols],
                               ACT.Copy).then_inc(w_hi, 1)

            def square_sum(j, n, src, squares):
                act.activation(squares, src, ACT.Square, accum_out=ssq[:, j, n:n + 1]).then_inc(ss_ready, 1)

            def root(j):
                act.wait_ge(var_ready, j + 1)
                act.activation(root_[:, j:j + 1], var[:, j:j + 1], ACT.Sqrt).then_inc(sqrt_ready, 1)

            def load_roots():
                act.activation(warm[:, :], csil[:, 0:1], ACT.Sqrt, scale=0.0, bias=1.0)

            def modulate(t):
                j = TT + t
                act.wait_ge(x_turned, 2 * j + 1)
                act.wait_ge(col_ready, 3)
                for c in range(4):
                    ins = act.activation(hx[:, t, c, :], bank[B_TURNED[t]][:, P * c:P * (c + 1)], ACT.Identity,
                                         bias=col[1][:, 8 + c:9 + c], scale=col[2][:, c:c + 1])
                ins.then_inc(h_act, 1)

            def cut_h(t):
                j, tokens = TT + t, slice(P * t, P * (t + 1))
                for half, ready in enumerate((h_act, h_dve)):
                    act.wait_ge(ready, 4 + t + 1)
                    act.activation(hhi[:, 4 * half:4 * half + 4, tokens], hx[:, t, 4 * half:4 * half + 4, :],
                                   ACT.Copy).then_inc(h_hi, 1)

            def take_unit(u):
                b, what, c0, n, dest = UNITS[u]
                src = bank[B_UNIT + u % 2]
                act.wait_ge(units, u + 1)
                if what == "index keys and weights":
                    act.activation(qk[0:HD, dest, :], src[0:HD, 0:S], ACT.Copy)
                    act.activation(qk[HD:2 * HD, dest, :], src[0:HD, 0:S], ACT.Copy)
                    ins = act.activation(wixt[HD:n, :], src[HD:n, 0:S], ACT.Copy)
                elif what == "features":
                    scale = SCALE if T_QSB <= dest < T_KSB else 1.0
                    ins = act.activation(qk[0:n, dest, :], src[0:n, 0:S], ACT.Copy, scale=scale)
                elif what == "last head":
                    for part in range(2):
                        ins = act.activation(qk[0:HD, dest[part], :], src[HD * part:HD * (part + 1), 0:S], ACT.Copy)
                elif what == "values":
                    ins = act.activation(v[:, dest[0], dest[1]:dest[1] + n], src[:, 0:n], ACT.Copy)
                else:
                    if u == FIRST_GATE:
                        act.wait_ge(vec_ready, 1)
                    ins = act.activation(gates[:, dest, :], src[:, 0:S], ACT.Sigmoid if u >= SIGMOID_FROM else ACT.Identity,
                                         bias=vecs[:, VEC_GATE + dest:VEC_GATE + dest + 1])
                ins.then_inc(unit_read, 1)

            act.wait_ge(c_in, 16)
            act.activation(csil[:, :], ccol[:, :], ACT.Silu).then_inc(c_ready, 1)
            act.wait_ge(c_ready, 1)
            load_roots()
            act.wait_ge(x_in, 16 * TT)
            for t in range(TT):
                for n in range(2):
                    cols = slice(BANK * n, BANK * (n + 1))
                    square_sum(t, n, xt[:, t, cols], xn[:, t, cols])
            for t in range(TT):
                root(t)
            act.preload_act_table_set("natural_log_exp_and_others")
            for q in range(4):
                cut_hi(0, q)

            act.wait_ge(x_turned, 2 * TT)
            act.wait_ge(col_ready, 1)
            for pair in range(4):
                c = 2 * pair
                act.activation(h32[:, c, :], turned(c), ACT.Identity, bias=col[0][:, c:c + 1],
                               scale=col[0][:, 8 + c:9 + c]).then_inc(h_act, 1)
                act.wait_ge(h_act, pair + 1)
                act.wait_ge(h_dve, pair + 1)
                act.activation(hhi[:, 2 * pair:2 * pair + 2, :], h32[:, 2 * pair:2 * pair + 2, :], ACT.Copy).then_inc(h_hi, 1)

            for u in range(N_UNITS):
                for b, q in PIECES_AT.get(u, []):
                    cut_hi(b, q)
                if u in EXP_AT and EXP_AT[u] in SB_NO:
                    n = EXP_AT[u]
                    act.wait_ge(z_ready, n + 1)
                    if SB_NO[n] == 0:
                        act.wait_ge(p_turned, softs_before(n))
                    z = bank[B_Z + n % 2][:, 0:CAUSAL]
                    e = bufa[n % 2][:, :]
                    if n >= 2:
                        act.wait_ge(sp_ready if n - 2 in SB_NO else p_ready, (SB_NO[n - 2] + 1) if n - 2 in SB_NO else SOFT_NO[n - 2] + 1)
                    then(act.activation(e, z, ACT.Abs))
                    then(act.activation(e, e, ACT.Exp, scale=-1.0))
                    act.activation(e, e, ACT.Ln, bias=1.0).then_inc(ln_ready, 1)
                take_unit(u)
                if u in LOGITS_AT:
                    h = LOGITS_AT[u]
                    act.wait_ge(logits, h + 1)
                    if h >= 2:
                        act.wait_ge(score_added, TT * (h - 1))
                    act.activation(bufp[h % 2][:, :], bank[B_Z + h % 3][:, 0:CAUSAL], ACT.Relu).then_inc(relu_ready, 1)
                if u in EXP_AT and EXP_AT[u] in SOFT_NO:
                    n = EXP_AT[u]
                    branch, h = HEADS[n][0:2]
                    act.wait_ge(max_ready, SOFT_NO[n] + 1)
                    if n >= 2:
                        if n - 2 in SB_NO:
                            act.wait_ge(sums, SB_NO[n - 2] + 1)
                        else:
                            act.wait_ge(p_turned, SOFT_NO[n - 2] + 1)
                    for t, (c0, c1) in enumerate(((0, P), (P, CAUSAL))):
                        ins = act.activation(bufp[n % 2][:, c0:c1], bufa[n % 2][:, c0:c1], ACT.Exp,
                                             scale=SLOPES[2 * h + (branch == "ds")],
                                             bias=smax[:, n % 2, t:t + 1], accum_out=ssum[:, n % 2, t:t + 1])
                    ins.then_inc(exp_ready, 1)
                for n in OUTPUT_AT.get(u, ()):
                    p0, ch = HD * (HEADS[n][1] % 2), O_CHUNK[HEADS[n][0]][HEADS[n][1]]
                    act.wait_ge(o_ready, n + 1)
                    act.activation(ohi[p0:p0 + HD, ch, :], bank[B_O + n % 2][p0:p0 + HD, 0:S], ACT.Copy).then_inc(o_hi, 1)
                if u in SECOND_AT:
                    n = SECOND_AT[u]
                    if n >= 2:
                        act.wait_ge(o_ready, n - 1)
                    if n in SB_NO:
                        act.wait_ge(sums, SB_NO[n] + 1)
                        act.activation(buft[n % 2][:, :], bank[B_Z + n % 2][:, 0:CAUSAL], ACT.Exp).then_inc(a_ready, 1)
                    else:
                        act.wait_ge(p_turned, SOFT_NO[n] + 1)
                        act.activation(buft[n % 2][:, :], bank[B_T][:, 0:CAUSAL], ACT.Copy).then_inc(pt_ready, 1)
                if SIGMOID_FROM <= u < SIGMOID_FROM + SIGMOID_BATCHES:
                    i = u - SIGMOID_FROM
                    if i == 0:
                        act.wait_ge(unit_read, SIGMOID_FROM)
                    tiles = slice(EARLY_GATES * i // SIGMOID_BATCHES, EARLY_GATES * (i + 1) // SIGMOID_BATCHES)
                    act.activation(gates[:, tiles, :], gates[:, tiles, :], ACT.Sigmoid).then_inc(sig_ready, 1)

            for f in range(KC):
                for b, q in MERGE_PIECES[f]:
                    cut_hi(B_PROJ + b, q)
                act.wait_ge(merged, f + 1)
                act.wait_ge(units, N_UNITS)
                act.activation(hhi[:, f, :], h32[:, f, :], ACT.Copy).then_inc(m_hi, 1)
                if 1 <= f <= len(SPREADS):
                    g, _, half = SPREADS[f - 1]
                    act.wait_ge(m_spread, f)
                    act.activation(gb[g][:, BANK * half:BANK * (half + 1)], bank[6 + half][:, :], ACT.Copy).then_inc(gb_ready, 1)
            load_roots()

            def cut_up_hi(i, slot, q, first=False):
                if q == 0:
                    act.wait_ge(raw_in[slot], RAW_COUNT[slot] + 16 * (i + 1 + slot))
                    if first:
                        act.wait_ge(units, BLOCK_DONE[B_WO + 1])
                    else:
                        act.wait_ge(up_done, 2 * (i - 1))
                act.activation(block_view(whi[slot], B_FFN)[:, 2 * q:2 * q + 2, :],
                               block_view(raw[slot], B_FFN)[:, 2 * q:2 * q + 2, :], ACT.Copy).then_inc(up_hi, 1)

            def cut_down_hi(i, slot, first=False):
                act.wait_ge(down_in[slot], 8 * (i + 1 + slot))
                if not first:
                    act.wait_ge(down_done, i - 1)
                act.activation(dhi[slot][:, :, :], draw[slot][:, :, :], ACT.Copy).then_inc(d_hi, 1)

            def norm_y(k, t):
                j = 2 + 2 * t if k == 0 else 6 + t
                for n in range(2):
                    if k == 0:
                        act.wait_ge(units, y_done(t, n))
                    else:
                        act.wait_ge(down_done, N_FFN - 2 + 2 * t + n + 1)
                    square_sum(j, n, bank[B_Y[k][t] + n][:, :], squares[n])
                    if k == 0 and t == 1 and n == 0:
                        modulate(0)
                root(j)

            def norm_new_x(t):
                for n in range(2):
                    act.wait_ge(x_new, 2 * t + n + 1)
                    square_sum(3 + 2 * t, n, xt[:, t, BANK * n:BANK * (n + 1)], squares[n])
                root(3 + 2 * t)

            squares = [f[:, :, :].rearrange("p j n -> p (j n)") for f in fsil]
            norm_y(0, 0)
            norm_new_x(0)
            norm_y(0, 1)
            norm_new_x(1)
            modulate(1)
            for t in range(TT):
                cut_h(t)

            def silu_tile(i, slot, j):
                act.wait_ge(up_done, 2 * i + j + 1)
                act.activation(fsil[slot][:, j, :], bank[2 * (1 - slot) + j][:, 0:S], ACT.Silu).then_inc(silu_done, 1)

            def f_part(i, slot, j):
                act.wait_ge(f_ready, 2 * i + j + 1)
                act.activation(fhi[slot][:, j, :], fsil[slot][:, j, :], ACT.Copy).then_inc(f_hi, 1)

            def step(i, slot, first, last):
                if not last:
                    for q in range(4 if first else 2):
                        cut_up_hi(i + 1, 1 - slot, q, first)
                silu_tile(i, slot, 0)
                if not last and not first:
                    for q in range(2, 4):
                        cut_up_hi(i + 1, 1 - slot, q, first)
                f_part(i, slot, 0)
                silu_tile(i, slot, 1)
                if first:
                    cut_down_hi(0, 1, True)
                if not last:
                    cut_down_hi(i + 1, 1 - slot, first)
                f_part(i, slot, 1)

            step(0, 1, True, False)
            with act.Fori(1, N_FFN - 2, 2) as i:
                step(i, 0, False, False)
                step(i + 1, 1, False, False)
            step(N_FFN - 2, 0, False, False)
            step(N_FFN - 1, 1, False, True)
            load_roots()
            for t in range(TT):
                norm_y(1, t)

        @block.vector
        def _(dve):
            steps = [0]

            def then(ins):
                steps[0] += 1
                ins.then_inc(dve_step, 1)
                dve.wait_ge(dve_step, steps[0])

            def cut_lo(b, q):
                dve.wait_ge(w_hi, 4 * b + q + 1)
                r = RAW_OF_BLOCK[b]
                p, chunks, cols = block_parts(b)[q]
                dve.tensor_tensor(block_view(wlo[b % 2], b)[0:p, chunks, cols], block_view(raw[r % 2], b)[0:p, chunks, cols],
                                  block_view(whi[b % 2], b)[0:p, chunks, cols].bitcast(F32), ALU.subtract).then_inc(w_lo, 1)

            def inverse_root(j, meanwhile=lambda: None):
                v, r, t = var[:, j:j + 1], rinv[:, j:j + 1], root_[:, j:j + 1]
                dve.wait_ge(ss_ready, 2 * j + 1)
                then(dve.tensor_scalar(v, ssq[:, j, 0:1], 1.0 / D, EPS, ALU.mult, ALU.add))
                dve.wait_ge(ss_ready, 2 * j + 2)
                dve.scalar_tensor_tensor(v, ssq[:, j, 1:2], 1.0 / D, v, ALU.mult, ALU.add).then_inc(var_ready, 1)
                meanwhile()
                dve.wait_ge(sqrt_ready, j + 1)
                then(dve.reciprocal(r, t))
                then(dve.tensor_scalar(t, v, r, r, ALU.mult, ALU.mult))
                then(dve.tensor_scalar(t, t, -0.5, 1.5, ALU.mult, ALU.add))
                then(dve.tensor_scalar(r, r, t, None, ALU.mult))

            def spread_root(j, t):
                dve.tensor_scalar(diag[t], ident[:, :], rinv[:, j:j + 1], None, ALU.mult).then_inc(xn_ready, 1)

            def modulate(t):
                j = TT + t
                dve.wait_ge(x_turned, 2 * j + 2)
                for c in range(4, 8):
                    ins = dve.tensor_scalar(hx[:, t, c, :], bank[B_TURNED[t] + 1][:, P * (c - 4):P * (c - 3)], col[2][:, c:c + 1],
                                            col[1][:, 8 + c:9 + c], ALU.mult, ALU.add)
                ins.then_inc(h_dve, 1)

            def cut_h(t):
                j, tokens = TT + t, slice(P * t, P * (t + 1))
                for half in range(2):
                    dve.wait_ge(h_hi, 2 * j + half + 1)
                    dve.tensor_tensor(hlo[:, 4 * half:4 * half + 4, tokens], hx[:, t, 4 * half:4 * half + 4, :],
                                      hhi[:, 4 * half:4 * half + 4, tokens].bitcast(F32), ALU.subtract).then_inc(h_lo, 1)

            def columns(g):
                dve.wait_ge(m_turned, g + 1)
                m, first, second = col[g][:, :], col[g][:, 0:KC], col[g][:, KC:2 * KC]
                bias = VEC_ADA + 2 * KC * g
                turned_sums = bank[B_ROWS[g]][:, :].rearrange("p (c j r) -> p j c r", c=4, j=4)[:, :, :, 0]
                then(dve.tensor_tensor(m.rearrange("p (j c) -> p j c", j=4), vecs[:, bias:bias + 2 * KC].rearrange("p (j c) -> p j c", j=4),
                                       turned_sums, ALU.add if g == 0 else ALU.subtract))
                if g == 0:
                    ins = dve.scalar_tensor_tensor(second, second, 1.0, vecs[:, VEC_PRE_MIX:VEC_PRE_MIX + KC], ALU.add, ALU.mult)
                elif g == 1:
                    ins = dve.tensor_tensor(first, first, vecs[:, VEC_POST_MIX:VEC_POST_MIX + KC], ALU.mult)
                else:
                    then(dve.scalar_tensor_tensor(first, first, 1.0, vecs[:, VEC_PRE_FFN:VEC_PRE_FFN + KC], ALU.add, ALU.mult))
                    ins = dve.tensor_tensor(second, second, vecs[:, VEC_POST_FFN:VEC_POST_FFN + KC], ALU.mult)
                then(ins)
                dve.sem_inc(col_ready, 1)

            def accumulate(n):
                k = n % KC
                dve.wait_ge(part_in, 16 * (n + 1))
                if n == 0:
                    ins = dve.tensor_scalar(acc[:, :], ada_part, csil[:, 0:1], None, ALU.mult)
                elif k == 0:
                    dve.wait_ge(summed, n // KC + 1)
                    ins = dve.tensor_scalar(acc[:, :], ada_part, csil[:, 0:1], None, ALU.mult)
                else:
                    dve.wait_ge(acc_done, n)
                    ins = dve.scalar_tensor_tensor(acc[:, :], ada_part, csil[:, k:k + 1], acc[:, :], ALU.mult, ALU.add)
                ins.then_inc(acc_done, 1)

            def rows(g):
                dve.wait_ge(summed, g + 1)
                dve.tensor_copy(mrow[:, :], bank[B_ADA][:, :]).then_inc(m_ready, 1)

            dve.wait_ge(c_ready, 1)
            dve.tensor_copy(crep[:, :, :], csil[:, :, None].to_broadcast([P, KC, 32])).then_inc(c_ready, 1)
            for t in range(TT):
                inverse_root(t)
            dve.wait_ge(consts, 7)
            for t in range(TT):
                spread_root(t, t)
            dve.wait_ge(vec_turned, 1)
            then(dve.tensor_copy(vecs[:, :], bank[0][:, 0:VEC_END]))
            dve.sem_inc(vec_ready, 1)
            rows(0)
            for q in range(4):
                cut_lo(0, q)
            columns(0)

            dve.wait_ge(x_turned, 2 * TT)
            def odd_chunk(pair):
                c = 2 * pair + 1
                dve.tensor_scalar(h32[:, c, :], turned(c), col[0][:, 8 + c:9 + c], col[0][:, c:c + 1],
                                  ALU.mult, ALU.add).then_inc(h_dve, 1)

            odd_chunk(0)
            for pair in range(4):
                if pair < 3:
                    odd_chunk(pair + 1)
                dve.wait_ge(h_hi, pair + 1)
                dve.tensor_tensor(hlo[:, 2 * pair:2 * pair + 2, :], h32[:, 2 * pair:2 * pair + 2, :],
                                  hhi[:, 2 * pair:2 * pair + 2, :].bitcast(F32), ALU.subtract).then_inc(h_lo, 1)

            def reach(n):
                return dsel if HEADS[n][0] == "ds" else dist

            for u in range(N_UNITS):
                for b, q in PIECES_AT.get(u, []):
                    cut_lo(b, q)
                if u == 3:
                    dve.wait_ge(wix_turned, 1)
                    then(dve.tensor_copy(wix[:, :, :], bank[B_ADA][:, 0:TT * H_IX].rearrange("p (t h) -> p t h", t=TT)))
                    dve.sem_inc(wix_ready, 1)
                if u in LOGITS_AT:
                    h = LOGITS_AT[u]
                    dve.wait_ge(relu_ready, h + 1)
                    if h:
                        dve.wait_ge(score_added, TT * h)
                    for t, (c0, c1) in enumerate(((0, P), (P, CAUSAL))):
                        w = wix[:, t, h:h + 1]
                        if h == 0:
                            ins = dve.tensor_scalar(score[:, c0:c1], bufp[0][:, c0:c1], w, 0.0, ALU.mult, ALU.add)
                        else:
                            ins = dve.scalar_tensor_tensor(score[:, c0:c1], bufp[h % 2][:, c0:c1], w, score[:, c0:c1],
                                                           ALU.mult, ALU.add)
                        ins.then_inc(score_added, 1)
                for n in OUTPUT_AT.get(u, ()):
                    p0, ch = HD * (HEADS[n][1] % 2), O_CHUNK[HEADS[n][0]][HEADS[n][1]]
                    dve.wait_ge(o_hi, n + 1)
                    lo = olo[p0:p0 + HD, ch, :] if ch < FULL_OCH else ohi[HD:P, ch, :]
                    dve.tensor_tensor(lo, bank[B_O + n % 2][p0:p0 + HD, 0:S],
                                      ohi[p0:p0 + HD, ch, :].bitcast(F32), ALU.subtract).then_inc(o_lo, 1)
                if u in NORM_AT and NORM_AT[u] in SOFT_NO:
                    n = NORM_AT[u]
                    i = SOFT_NO[n]
                    dve.wait_ge(exp_ready, i + 1)
                    then(dve.reciprocal(ssum[:, n % 2, :], ssum[:, n % 2, :]))
                    for t, (c0, c1) in enumerate(((0, P), (P, CAUSAL))):
                        ins = dve.tensor_scalar(bufp[n % 2][:, c0:c1], bufp[n % 2][:, c0:c1], ssum[:, n % 2, t:t + 1], None, ALU.mult)
                    ins.then_inc(p_ready, 1)
                if u in EXP_AT and EXP_AT[u] in SB_NO:
                    n = EXP_AT[u]
                    z = bank[B_Z + n % 2][:, 0:CAUSAL]
                    i = SB_NO[n]
                    dve.wait_ge(ln_ready, i + 1)
                    if n >= 2:
                        if n - 2 in SB_NO:
                            dve.wait_ge(sums, SB_NO[n - 2] + 1)
                        else:
                            dve.wait_ge(p_turned, SOFT_NO[n - 2] + 1)
                    dve.scalar_tensor_tensor(bufp[n % 2][:, :], z, 0.0, bufa[n % 2][:, :], ALU.max, ALU.add).then_inc(sp_ready, 1)
                if u in SCORES_AT and SCORES_AT[u] in SOFT_NO:
                    n = SCORES_AT[u]
                    branch, h = HEADS[n][0:2]
                    z = bank[B_Z + n % 2][:, 0:CAUSAL]
                    i = SOFT_NO[n]
                    slope = SLOPES[2 * h + (branch == "ds")]
                    dve.wait_ge(z_ready, n + 1)
                    if n == 0:
                        dve.wait_ge(consts, 10)
                    then(dve.scalar_tensor_tensor(bufa[n % 2][:, :], z, SCALE / slope, reach(n)[:, :], ALU.mult, ALU.add))
                    for t, (c0, c1) in enumerate(((0, P), (P, CAUSAL))):
                        ins = dve.reduce_max(smax[:, n % 2, t:t + 1], bufa[n % 2][:, c0:c1], AX_X)
                    then(ins)
                    dve.tensor_scalar(smax[:, n % 2, :], smax[:, n % 2, :], -slope, None, ALU.mult).then_inc(max_ready, 1)

                if u in ROUND_AT:
                    r = ROUND_AT[u]
                    src = score if r == 0 else work
                    if r == 0:
                        dve.wait_ge(score_masked, 2)
                    halves = ((0, 0, P), (1, P, CAUSAL))
                    for t, c0, c1 in halves:
                        ins = dve.max(top8[:, t, :], src[:, c0:c1])
                    then(ins)
                    for t, c0, c1 in halves:
                        ins = dve.match_replace(work[:, c0:c1], top8[:, t, :], src[:, c0:c1], TAKEN)
                    then(ins)
                    if r == TOPK_ROUNDS - 1:
                        then(dve.tensor_tensor(work[:, :], work[:, :], score[:, :], ALU.not_equal))
                        then(dve.tensor_scalar(work[:, :], work[:, :], -MASKED, MASKED, ALU.mult, ALU.add))
                        dve.wait_ge(consts, 10)
                        then(dve.tensor_tensor(dsel[:, :], work[:, :], dist[:, :], ALU.add))
                if u in ADA_AT:
                    accumulate(ADA_AT[u])
                if u in SUM_AT:
                    rows(SUM_AT[u])
                if u in COLUMNS_AT:
                    columns(COLUMNS_AT[u])

            def merge_tile(f):
                if f == 0:
                    dve.wait_ge(sig_ready, SIGMOID_BATCHES)
                    dve.wait_ge(unit_read, N_UNITS)
                dve.wait_ge(units, N_UNITS + f + 1)
                if f >= 2:
                    dve.wait_ge(merged, f - 1)
                for br in range(3):
                    dve.tensor_tensor(gp[f % 2][br], bank[2 * br + 1 - f % 2][:, 0:S], gates[:, KC * br + f, :], ALU.mult).then_inc(gated, 1)

            for f in range(KC):
                if f:
                    merge_tile(f)
                for b, q in MERGE_PIECES[f]:
                    cut_lo(B_PROJ + b, q)
                if f == 0:
                    merge_tile(0)

            def add_residual(k, t):
                j = 2 + 2 * t if k == 0 else 6 + t
                halves = [slice(BANK * n, BANK * (n + 1)) for n in range(2)]

                def gain(n):
                    dve.wait_ge(ss_ready, 2 * j + n + 1)
                    ins = dve.tensor_tensor(xn[:, t, halves[n]], bank[B_Y[k][t] + n][:, :], gb[k + 1][:, halves[n]], ALU.mult)
                    ins.then_inc(dve_scaled, 1)

                if t == 0:
                    dve.wait_ge(gb_ready, 2 * (k + 1))
                gain(0)
                if k == 0 and t == 1:
                    modulate(0)
                inverse_root(j, lambda: gain(1))
                for n in range(2):
                    dve.wait_ge(dve_scaled, 2 * (2 * k + t) + n + 1)
                    dve.scalar_tensor_tensor(xt[:, t, halves[n]], xn[:, t, halves[n]], rinv[:, j:j + 1], xt[:, t, halves[n]],
                                             ALU.mult, ALU.add).then_inc(x_new, 1)

            def cut_up_lo(i, slot, q):
                dve.wait_ge(up_hi, 4 * (i - 1) + q + 1)
                dve.tensor_tensor(block_view(wlo[slot], B_FFN)[:, 2 * q:2 * q + 2, :], block_view(raw[slot], B_FFN)[:, 2 * q:2 * q + 2, :],
                                  block_view(whi[slot], B_FFN)[:, 2 * q:2 * q + 2, :].bitcast(F32), ALU.subtract).then_inc(up_lo, 1)

            def cut_down_lo(i, slot):
                dve.wait_ge(d_hi, i + 1)
                dve.tensor_tensor(dlo[slot][:, :, :], draw[slot][:, :, :], dhi[slot][:, :, :].bitcast(F32), ALU.subtract).then_inc(d_lo, 1)

            for t in range(TT):
                add_residual(0, t)
                inverse_root(3 + 2 * t)
                spread_root(3 + 2 * t, t)
            modulate(TT - 1)
            for t in range(TT):
                cut_h(t)

            def f_tile(i, slot, j):
                dve.wait_ge(silu_done, 2 * i + j + 1)
                dve.tensor_tensor(fsil[slot][:, j, :], bank[2 * (1 - slot) + j][:, S:2 * S], fsil[slot][:, j, :], ALU.mult).then_inc(f_ready, 1)

            def f_rest(i, slot, j):
                dve.wait_ge(f_hi, 2 * i + j + 1)
                dve.tensor_tensor(flo[slot][:, j, :], fsil[slot][:, j, :], fhi[slot][:, j, :].bitcast(F32), ALU.subtract).then_inc(f_lo, 1)

            def step(i, slot, last, first=False):
                if not last:
                    for q in range(4 if first else 2):
                        cut_up_lo(i + 1, 1 - slot, q)
                f_tile(i, slot, 0)
                if not last and not first:
                    for q in range(2, 4):
                        cut_up_lo(i + 1, 1 - slot, q)
                f_rest(i, slot, 0)
                f_tile(i, slot, 1)
                if first:
                    cut_down_lo(0, 1)
                if not last:
                    cut_down_lo(i + 1, 1 - slot)
                f_rest(i, slot, 1)

            step(0, 1, False, True)
            with dve.Fori(1, N_FFN - 2, 2) as i:
                step(i, 0, False)
                step(i + 1, 1, False)
            step(N_FFN - 2, 0, False)
            step(N_FFN - 1, 1, True)
            for t in range(TT):
                add_residual(1, t)

        @block.tensor
        def _(pe):
            def three(dst, a, b, first, last):
                pe.matmul(dst, a[0], b[0], start=first, stop=False)
                pe.matmul(dst, a[0], b[1], start=False, stop=False)
                return pe.matmul(dst, a[1], b[0], start=False, stop=last)

            def product(k, w):
                for j in range(4):
                    mm = pe.matmul(bank[B_ADA][32 * j:32 * j + 32, :], crep[:, k, :], w[:, BANK * j:BANK * (j + 1)],
                                   start=k == 0, stop=k == KC - 1, tile_position=(0, 32 * j))
                return mm

            def first_products():
                for k in range(KC):
                    if k < 4:
                        pe.wait_ge(raw_in[k // 2], 16)
                        buf = raw[k // 2]
                    else:
                        pe.wait_ge(ada_in[k - 4], 16)
                        buf = ada_end[k // 2 - 2]
                    mm = product(k, buf[:, ADA_COLS * (k % 2):ADA_COLS * (k % 2 + 1)])
                    if k % 2:
                        mm.then_inc(gemv, 1)
                pe.wait_ge(gemv, KC // 2)
                pe.sem_inc(summed, 1)

            def sum_acc(g):
                pe.wait_ge(acc_done, g * KC)
                if g == 1:
                    pe.wait_ge(wix_ready, 1)
                else:
                    pe.wait_ge(col_ready, 2)
                for j in range(4):
                    mm = pe.matmul(bank[B_ADA][32 * j:32 * j + 32, :], neg1[:, 0:32], acc[:, BANK * j:BANK * (j + 1)],
                                   start=True, stop=True, tile_position=(0, 32 * j))
                mm.then_inc(summed, 1)

            def turn_rows(g):
                pe.wait_ge(m_ready, g + 1)
                if g == 2:
                    pe.wait_ge(pt_ready, N_SOFT)
                for n in range(4):
                    mm = pe.transpose(bank[B_ROWS[g]][:, P * n:P * (n + 1)], mrow[:, P * n:P * (n + 1)], ident[:, :])
                mm.then_inc(m_turned, 1)

            def spread_gain(i):
                pe.wait_ge(diag_ready, i + 1)
                if i == 0:
                    pe.wait_ge(o_lo, N_HEADS)
                elif i >= 2:
                    pe.wait_ge(gb_ready, i - 1)
                pe.matmul(bank[6 + SPREADS[i][2]][:, :], neg1[:, :], spread[i], start=True, stop=True).then_inc(m_spread, 1)

            def turn_x(k, t):
                pe.wait_ge(xn_ready, 2 * k + t + 1)
                for half in range(2):
                    for c in range(4 * half, 4 * half + 4):
                        if k == 0:
                            dst = turned(c)[:, P * t:P * (t + 1)]
                        else:
                            dst = bank[B_TURNED[t] + half][:, P * (c % 4):P * (c % 4 + 1)]
                        mm = pe.matmul(dst, xt[:, t, P * c:P * (c + 1)], diag[t], start=True, stop=True)
                    mm.then_inc(x_turned, 1)

            def unit(u):
                b, what, c0, n, dest = UNITS[u]
                if u >= 2:
                    pe.wait_ge(unit_read, u - 1)
                w = [block_view(x[b % 2], b)[:, :, c0:c0 + n] for x in (whi, wlo)]
                if b == 1:
                    pe.wait_ge(w_hi, 4 + c0 // P + 1)
                    pe.wait_ge(w_lo, 4 + c0 // P + 1)
                for k in range(KC):
                    if b != 1 and k % 2 == 0 and (u == 0 or UNITS[u - 1][0] != b):
                        pe.wait_ge(w_hi, 4 * b + k // 2 + 1)
                        pe.wait_ge(w_lo, 4 * b + k // 2 + 1)
                    if u == 0 and k % 2 == 0:
                        pe.wait_ge(h_hi, k // 2 + 1)
                        pe.wait_ge(h_lo, k // 2 + 1)
                    if what != "values":
                        mm = three(bank[B_UNIT + u % 2][0:n, 0:S], [x[:, k, :] for x in w], [hhi[:, k, :], hlo[:, k, :]],
                                   k == 0, k == KC - 1)
                    else:
                        t = dest[0]
                        mm = three(bank[B_UNIT + u % 2][:, 0:n], [x[:, k, P * t:P * (t + 1)] for x in (hhi, hlo)],
                                   [x[:, k, :] for x in w], k == 0, k == KC - 1)
                mm.then_inc(units, 1)

            def query_major(dst, q, k, p0):
                pe.matmul(dst[:, 0:P], q[p0:p0 + HD, 0:P], k[p0:p0 + HD, 0:P], start=True, stop=True)
                return pe.matmul(dst[:, P:CAUSAL], q[p0:p0 + HD, P:S], k[p0:p0 + HD, :], start=True, stop=True)

            def key_major(dst, q, k, p0):
                pe.matmul(dst[:, 0:S], k[p0:p0 + HD, 0:P], q[p0:p0 + HD, :], start=True, stop=False, skip_group_check=True)
                return pe.matmul(dst[:, S:CAUSAL], k[p0:p0 + HD, P:S], q[p0:p0 + HD, P:S], start=False, stop=True,
                                 skip_group_check=True)

            def scores(n):
                branch, h, tq, tk, _ = HEADS[n]
                q, k, p0 = qk[:, tq + h // 2, :], qk[:, tk + h // 2, :], HD * (h % 2)
                if n < 2:
                    pe.wait_ge(relu_ready, H_IX)
                elif n - 2 in SB_NO:
                    pe.wait_ge(a_ready, SB_NO[n - 2] + 1)
                else:
                    pe.wait_ge(max_ready, SOFT_NO[n - 2] + 1)
                (key_major if n in SB_NO else query_major)(bank[B_Z + n % 2], q, k, p0).then_inc(z_ready, 1)

            def second(n):
                if n in SB_NO:
                    i = SB_NO[n]
                    pe.wait_ge(sp_masked, 2 * (i + 1))
                    z, s = bank[B_Z + n % 2], bufp[n % 2]
                    pe.matmul(z[:, 0:CAUSAL], tri[:, :], s[:, :], start=False, stop=False, skip_group_check=True)
                    pe.matmul(z[:, P:S], neg1[:, :], s[:, S:CAUSAL], start=False, stop=True, skip_group_check=True).then_inc(sums, 1)
                else:
                    i = SOFT_NO[n]
                    pe.wait_ge(p_ready, i + 1)
                    if i >= 1:
                        pe.wait_ge(pt_ready, i)
                    for c in range(3):
                        mm = pe.transpose(bank[B_T][:, P * c:P * (c + 1)], bufp[n % 2][:, P * c:P * (c + 1)], ident[:, :])
                    mm.then_inc(p_turned, 1)

            def output(heads):
                for n in heads:
                    if n in SB_NO:
                        pe.wait_ge(a_masked, 2 * (SB_NO[n] + 1))
                    else:
                        pe.wait_ge(pt_ready, SOFT_NO[n] + 1)
                    if n >= 2:
                        pe.wait_ge(o_lo, n - 1)
                for keys in range(2):
                    for n in heads:
                        h, v0 = HEADS[n][1], HEADS[n][4]
                        p0, a = HD * (h % 2), buft[n % 2]
                        dst, cols = bank[B_O + n % 2][p0:p0 + HD, :], slice(v0 + HD * h, v0 + HD * (h + 1))
                        if keys == 0:
                            pe.matmul(dst[:, 0:S], v[:, 0, cols], a[:, 0:S], start=True, stop=False, skip_group_check=True)
                        else:
                            pe.matmul(dst[:, P:S], v[:, 1, cols], a[:, S:CAUSAL], start=False, stop=True,
                                      skip_group_check=True).then_inc(o_ready, 1)

            pe.wait_ge(consts, 10)
            pe.wait_ge(c_ready, 2)
            pe.wait_ge(vec_in, 16 * 6)
            pe.transpose(bank[0][:, 0:VEC_END], vec_rows[:, :], ident[0:VEC_END, 0:VEC_END]).then_inc(vec_turned, 1)
            for t in range(TT):
                turn_x(0, t)
            first_products()
            turn_rows(0)
            for u in range(N_UNITS):
                unit(u)
                if u == 2:
                    pe.wait_ge(unit_read, 1)
                    pe.wait_ge(col_ready, 1)
                    for t in range(TT):
                        mm = pe.transpose(bank[B_ADA][:, H_IX * t:H_IX * (t + 1)], wixt[HD:HD + H_IX, P * t:P * (t + 1)],
                                          ident[HD:HD + H_IX, HD:HD + H_IX])
                    mm.then_inc(wix_turned, 1)
                if u in SUM_AT:
                    sum_acc(SUM_AT[u])
                if u in TURN_AT:
                    turn_rows(TURN_AT[u])
                if u in LOGITS_AT:
                    h = LOGITS_AT[u]
                    if h == 0:
                        pe.wait_ge(unit_read, 5)
                        pe.wait_ge(vec_ready, 1)
                    if h >= 3:
                        pe.wait_ge(relu_ready, h - 2)
                    query_major(bank[B_Z + h % 3], qk[:, T_QIX + h // 2, :], qk[:, T_KIX, :], HD * (h % 2)).then_inc(logits, 1)
                if u in OUTPUT_AT:
                    output(OUTPUT_AT[u])
                if u in SECOND_AT:
                    second(SECOND_AT[u])
                if u in SCORES_AT:
                    scores(SCORES_AT[u])

            for f in range(KC):
                b = B_PROJ + f // 2
                if f % 2 == 0:
                    pe.wait_ge(w_hi, 4 * (b + 1))
                    pe.wait_ge(w_lo, 4 * (b + 1))
                if f == 0:
                    pe.wait_ge(o_hi, N_HEADS)
                    pe.wait_ge(o_lo, N_HEADS)
                if f == 0:
                    pe.wait_ge(unit_read, N_UNITS - 1)
                elif f == 1:
                    pe.wait_ge(unit_read, N_UNITS)
                    pe.wait_ge(col_ready, 3)
                else:
                    pe.wait_ge(gated, 3 * (f - 1))
                w = [block_view(x[b % 2], b)[:, :, P * (f % 2):P * (f % 2 + 1)] for x in (whi, wlo)]
                for i, branch in enumerate(("sb", "mb", "ds")):
                    dst = bank[2 * i + 1 - f % 2][:, 0:S]
                    for c, ch in enumerate(BRANCH_CHUNKS[branch]):
                        if ch < FULL_OCH:
                            mm = three(dst, [x[:, ch, :] for x in w], [ohi[:, ch, :], olo[:, ch, :]], c == 0, c == 2)
                        else:
                            pe.matmul(dst, w[0][:, ch, :], ohi[:, ch, :], start=False, stop=False)
                            mm = pe.matmul(dst, w[1][0:HD, ch, :], ohi[0:HD, ch, :], start=False, stop=True)
                mm.then_inc(units, 1)
                if 1 <= f <= len(SPREADS):
                    spread_gain(f - 1)

            def out_part(t, half, n, kk):
                b, k = B_WO + half, 4 * half + kk
                return three(bank[B_Y[0][t] + n][:, :], [x[:, k, P * t:P * (t + 1)] for x in (hhi, hlo)],
                             [block_view(x[b % 2], b)[:, kk, BANK * n:BANK * (n + 1)] for x in (whi, wlo)],
                             k == 0, k == KC - 1)

            pe.wait_ge(gb_ready, 4)
            for t in range(TT):
                if t == 1:
                    pe.wait_ge(gated, 3 * KC)
                for kk in range(4):
                    if t == 0:
                        pe.wait_ge(w_hi, 4 * B_WO + kk + 1)
                        pe.wait_ge(w_lo, 4 * B_WO + kk + 1)
                        pe.wait_ge(m_lo, kk + 1)
                    for n in range(2):
                        mm = out_part(t, 0, n, kk)
                mm.then_inc(units, 1)
                for n in range(2):
                    for kk in range(4):
                        if t == 0 and n == 0:
                            pe.wait_ge(w_hi, 4 * (B_WO + 1) + kk + 1)
                            pe.wait_ge(w_lo, 4 * (B_WO + 1) + kk + 1)
                            pe.wait_ge(m_lo, 4 + kk + 1)
                        mm = out_part(t, 1, n, kk)
                    mm.then_inc(units, 1)
                    if t == 1 and n == 0:
                        turn_x(1, 0)

            def first_up(t, j):
                w = block_view(raw[1], B_FFN)
                for a in range(2):
                    for k in range(KC):
                        if j == 0 and a == 0 and k == 0:
                            pe.wait_ge(h_act, 4 + t + 1)
                        if j == 0 and a == 0 and k == KC // 2:
                            pe.wait_ge(h_dve, 4 + t + 1)
                        mm = pe.matmul(bank[j][:, S * a + P * t:S * a + P * (t + 1)],
                                       w[:, k, FSTEP * a + P * j:FSTEP * a + P * (j + 1)], hx[:, t, k, :],
                                       start=k == 0, stop=k == KC - 1)
                return mm

            pe.wait_ge(raw_in[1], RAW_COUNT[1] + 32)
            for j in range(2):
                pe.wait_ge(dve_scaled, 3 + j)
                first_up(0, j)
            turn_x(1, 1)
            for j in range(2):
                first_up(1, j).then_inc(up_done, 1)

            def up(i, slot, first):
                if not first:
                    pe.wait_ge(up_hi, 4 * i)
                    pe.wait_ge(up_lo, 4 * i)
                for j in range(2):
                    if first:
                        pe.wait_ge(h_lo, 8)
                    else:
                        pe.wait_ge(f_ready, 2 * (i - 2) + j + 1)
                    dst = bank[2 * (1 - slot) + j]
                    for a in range(2):
                        for k in range(KC):
                            if first and j == 0 and a == 0 and k % 2 == 0:
                                pe.wait_ge(up_hi, k // 2 + 1)
                                pe.wait_ge(up_lo, k // 2 + 1)
                            w = [block_view(x[slot], B_FFN)[:, k, FSTEP * a + P * j:FSTEP * a + P * (j + 1)] for x in (whi, wlo)]
                            mm = three(dst[:, S * a:S * (a + 1)], w, [hhi[:, k, :], hlo[:, k, :]], k == 0, k == KC - 1)
                    mm.then_inc(up_done, 1)

            def down_part(i, slot, t, n, first, last):
                for j in range(2):
                    mm = three(bank[B_Y[1][t] + n][:, :], [x[:, j, P * t:P * (t + 1)] for x in (fhi[slot], flo[slot])],
                               [x[slot][:, j, BANK * n:BANK * (n + 1)] for x in (dhi, dlo)],
                               first and j == 0, last and j == 1)
                return mm

            def down_ready(i):
                pe.wait_ge(d_hi, i + 1)
                pe.wait_ge(d_lo, i + 1)
                pe.wait_ge(f_lo, 2 * (i + 1))

            def down(i, slot, first):
                down_ready(i)
                for t in range(TT):
                    for n in range(2):
                        mm = down_part(i, slot, t, n, first, False)
                mm.then_inc(down_done, 1)

            up(1, 0, True)
            down(0, 1, True)
            with pe.Fori(2, N_FFN - 1, 2) as i:
                up(i, 1, False)
                down(i - 1, 0, False)
                up(i + 1, 0, False)
                down(i, 1, False)
            up(N_FFN - 1, 1, False)
            down_ready(N_FFN - 2)
            for t in range(TT):
                for n in range(2):
                    down_part(N_FFN - 2, 0, t, n, False, False)
                if t == 0:
                    down_ready(N_FFN - 1)
                for n in range(2):
                    down_part(N_FFN - 1, 1, t, n, False, True).then_inc(down_done, 1)


_INS = ["x", "c", "w_ada", "b_ada", "g_pre_mix", "g_post_mix", "w_in", "b_gate", "w_proj_sb", "w_proj_moba",
        "w_proj_dsa", "w_o", "g_pre_ffn", "g_post_ffn", "w_up", "w_down"]
_OUTS = [((1, S, D), "float32")]


def kernel(**inputs):
    import numpy as _np
    import concourse.bacc as _bacc
    from concourse import mybir as _mybir
    from concourse.bass_utils import run_bass_kernel_spmd as _run

    nc = _bacc.Bacc("TRN2", target_bir_lowering=False, num_devices=1)
    arrays, args = {}, []
    for name in _INS:
        a = _np.ascontiguousarray(inputs[name])
        arrays[f"in_{name}_dram"] = a
        args.append(nc.dram_tensor(f"in_{name}_dram", a.shape, _mybir.dt.from_np(a.dtype), kind="ExternalInput").ap())
    for i, (shape, dtype) in enumerate(_OUTS):
        dt = _mybir.dt.from_np(_np.dtype(dtype))
        args.append(nc.dram_tensor(f"out_{i}_dram", shape, dt, kind="ExternalOutput").ap())
    decoder_layer(nc, *args)
    r = _run(nc, [arrays], core_ids=[0])
    return r.results[0]["out_0_dram"]
```
